# Optimizing a Trainium2 kernel written in Bass

```python
import math
import jax
import jax.numpy as jnp
from jax import lax
import numpy as np

'''Hybrid diffusion / flow-matching backbone: DEPTH layers over latent tokens with a context prefix.

Inputs:  x (BATCH, SEQ, D_MODEL) noisy latent tokens on a GRID_W-wide grid,
         c (BATCH, D_MODEL) conditioning vector, ctx (BATCH, CTX_LEN, D_MODEL) context tokens,
         c_ctx (D_MODEL,) learned modulation vector for context tokens, plus per-layer weights.
Output:  (BATCH, SEQ, D_MODEL) latent stream after the final RMSNorm.
Each layer: adaLN-modulated macaron SwiGLU (1/2) -> four parallel token mixers (windowed GQA with
sinks, 2-D neighbourhood attention, QK-norm dense GQA with axial rotary, bidirectional Mamba-2 SSD)
from one combined input projection, merged by per-channel sigmoid gates, one output projection ->
adaLN-modulated macaron SwiGLU (1/2). Context tokens use the same weights, modulated by c_ctx,
and read only context tokens.
'''

D_MODEL = 1024
BATCH = 1
SEQ = 256
DEPTH = 2

CTX_LEN = 256
GRID_W = 64
HEAD_DIM = 64
ROPE_THETA = 10000.0
EPS = 1e-6
NEG_INF = -1e30
D_FF = 2816
N_BRANCH = 4
BRANCH_W = 256
WA_Q_HEADS = 4
WA_KV_HEADS = 2
WA_WINDOW = 128
WA_BLOCK = 128
NA_HEADS = 4
NA_ROWS = 8
NA_COLS = 16
NA_QCOLS = 16
NA_KCOLS = 32
GA_Q_HEADS = 4
GA_KV_HEADS = 2
GA_BLOCK = 128
SSM_HEADS = 4
SSM_HEAD_DIM = 64
SSM_GROUPS = 2
SSM_STATE = 128
SSM_CONV = 5
SSM_CHUNK = 128
SSM_INNER = SSM_HEADS * SSM_HEAD_DIM
SSM_CONV_CH = SSM_INNER + 2 * SSM_GROUPS * SSM_STATE
IN_SIZES = (WA_Q_HEADS * HEAD_DIM, WA_KV_HEADS * HEAD_DIM, WA_KV_HEADS * HEAD_DIM,
            NA_HEADS * HEAD_DIM, NA_HEADS * HEAD_DIM, NA_HEADS * HEAD_DIM,
            GA_Q_HEADS * HEAD_DIM, GA_KV_HEADS * HEAD_DIM, GA_KV_HEADS * HEAD_DIM,
            SSM_INNER, SSM_CONV_CH, 2 * SSM_HEADS,
            N_BRANCH * D_MODEL)

kernel_name = 'hybrid_flow_backbone'

def rms_norm(x, g):
    xf = x.astype(jnp.float32)
    y = xf * lax.rsqrt(jnp.mean(xf * xf, axis=-1, keepdims=True) + EPS)
    return (y * g.astype(jnp.float32)).astype(x.dtype)

def swiglu(h, wg, wu, wd):
    return (jax.nn.silu(h @ wg) * (h @ wu)) @ wd

def split_heads(t):
    return t.reshape(t.shape[:-1] + (-1, HEAD_DIM))

def rope_tables(seq):
    pos = jnp.arange(seq)
    axes = jnp.stack([pos // GRID_W, pos % GRID_W], axis=-1).astype(jnp.float32)
    quarter = HEAD_DIM // 4
    inv = 1.0 / (ROPE_THETA ** (jnp.arange(quarter, dtype=jnp.float32) * 4.0 / HEAD_DIM))
    ang = axes[:, :, None] * inv
    return jnp.cos(ang), jnp.sin(ang)

def apply_rope(x, cos, sin):
    shp = x.shape
    xs = x.reshape(shp[:-1] + (2, 2, HEAD_DIM // 4))
    x1, x2 = xs[..., 0, :], xs[..., 1, :]
    cs = cos[:, None].astype(x.dtype)
    sn = sin[:, None].astype(x.dtype)
    out = jnp.stack([x1 * cs - x2 * sn, x2 * cs + x1 * sn], axis=-2)
    return out.reshape(shp)

def joint_softmax(parts):
    sizes = [p.shape[-1] for p in parts]
    p = jax.nn.softmax(jnp.concatenate(parts, axis=-1), axis=-1)
    return jnp.split(p, np.cumsum(sizes)[:-1].tolist(), axis=-1)

def context_attention(q, k, v, sink):
    bsz, lq, hq, d = q.shape
    hk = k.shape[2]
    g = hq // hk
    qg = q.reshape(bsz, lq, hk, g, d)
    s = jnp.einsum('bqhgd,bkhd->bhgqk', qg, k).astype(jnp.float32) * d ** -0.5
    if sink is not None:
        s_sink = jnp.broadcast_to(sink.astype(jnp.float32).reshape(1, hk, g, 1, 1), s.shape[:-1] + (1,))
        p, _ = joint_softmax([s, s_sink])
    else:
        p = jax.nn.softmax(s, axis=-1)
    o = jnp.einsum('bhgqk,bkhd->bqhgd', p.astype(v.dtype), v)
    return o.reshape(bsz, lq, hq * d)

def window_attention(q, k, v, kc, vc, sink):
    bsz, seq, hq, d = q.shape
    hk = k.shape[2]
    g = hq // hk
    nb = seq // WA_BLOCK
    scale = d ** -0.5
    qb = q.reshape(bsz, nb, WA_BLOCK, hk, g, d)

    def band(t):
        tp = jnp.pad(t, ((0, 0), (WA_WINDOW, WA_WINDOW), (0, 0), (0, 0))).reshape(bsz, nb + 2, WA_BLOCK, hk, d)
        return jnp.concatenate([tp[:, :-2], tp[:, 1:-1], tp[:, 2:]], axis=2)

    kb, vb = band(k), band(v)
    s_loc = jnp.einsum('bnqhgd,bnkhd->bnhgqk', qb, kb).astype(jnp.float32) * scale
    blk = jnp.arange(nb)[:, None, None] * WA_BLOCK
    qpos = blk + jnp.arange(WA_BLOCK)[None, :, None]
    kpos = blk - WA_WINDOW + jnp.arange(3 * WA_BLOCK)[None, None, :]
    valid = (jnp.abs(qpos - kpos) <= WA_WINDOW) & (kpos >= 0) & (kpos < seq)
    s_loc = jnp.where(valid[None, :, None, None], s_loc, NEG_INF)
    s_ctx = jnp.einsum('bnqhgd,bchd->bnhgqc', qb, kc).astype(jnp.float32) * scale
    s_sink = jnp.broadcast_to(sink.astype(jnp.float32).reshape(1, 1, hk, g, 1, 1), s_ctx.shape[:-1] + (1,))
    p_loc, p_ctx, _ = joint_softmax([s_loc, s_ctx, s_sink])
    o = (jnp.einsum('bnhgqk,bnkhd->bnqhgd', p_loc.astype(vb.dtype), vb)
         + jnp.einsum('bnhgqc,bchd->bnqhgd', p_ctx.astype(vc.dtype), vc))
    return o.reshape(bsz, seq, hq * d)

def neighborhood_attention(q, k, v, kc, vc, rpb):
    bsz, seq, h, d = q.shape
    rows = seq // GRID_W
    rw = min(NA_ROWS, rows)
    ncb = GRID_W // NA_QCOLS
    scale = d ** -0.5
    r = jnp.arange(rows)
    row_start = jnp.clip(r - rw // 2, 0, rows - rw)
    idx_r = row_start[:, None] + jnp.arange(rw)[None, :]
    qcol = jnp.arange(ncb)[:, None] * NA_QCOLS + jnp.arange(NA_QCOLS)[None, :]
    qcol_start = jnp.clip(qcol - NA_COLS // 2, 0, GRID_W - NA_COLS)
    kcol_start = jnp.clip(jnp.arange(ncb) * NA_QCOLS - NA_COLS // 2, 0, GRID_W - NA_KCOLS)
    idx_c = kcol_start[:, None] + jnp.arange(NA_KCOLS)[None, :]
    nk = rw * NA_KCOLS

    def gather(t):
        tg = t.reshape(bsz, rows, GRID_W, h, d)
        return tg[:, idx_r[:, None, :, None], idx_c[None, :, None, :]].reshape(bsz, rows, ncb, nk, h, d)

    kn, vn = gather(k), gather(v)
    qg = q.reshape(bsz, rows, ncb, NA_QCOLS, h, d)
    col_ok = (idx_c[:, None, :] >= qcol_start[:, :, None]) & (idx_c[:, None, :] < qcol_start[:, :, None] + NA_COLS)
    col_ok = jnp.broadcast_to(col_ok[:, :, None, :], (ncb, NA_QCOLS, rw, NA_KCOLS)).reshape(ncb, NA_QCOLS, nk)
    dr = idx_r - r[:, None] + NA_ROWS - 1
    dc = jnp.clip(idx_c[:, None, :] - qcol[:, :, None] + NA_COLS - 1, 0, 2 * NA_COLS - 2)
    bias = rpb[:, dr[:, None, None, :, None], dc[None, :, :, None, :]]
    bias = bias.reshape(h, rows, ncb, NA_QCOLS, nk).transpose(1, 2, 0, 3, 4).astype(jnp.float32)
    s_nb = jnp.einsum('brjqhd,brjkhd->brjhqk', qg, kn).astype(jnp.float32) * scale + bias
    s_nb = jnp.where(col_ok[None, None, :, None], s_nb, NEG_INF)
    s_ctx = jnp.einsum('brjqhd,bchd->brjhqc', qg, kc).astype(jnp.float32) * scale
    p_nb, p_ctx = joint_softmax([s_nb, s_ctx])
    o = (jnp.einsum('brjhqk,brjkhd->brjqhd', p_nb.astype(vn.dtype), vn)
         + jnp.einsum('brjhqc,bchd->brjqhd', p_ctx.astype(vc.dtype), vc))
    return o.reshape(bsz, seq, h * d)

def dense_block_attention(q, k, v, kc, vc):
    bsz, seq, hq, d = q.shape
    hk = k.shape[2]
    g = hq // hk
    nb = seq // GA_BLOCK
    scale = d ** -0.5
    qb = q.reshape(bsz, nb, GA_BLOCK, hk, g, d).transpose(1, 0, 2, 3, 4, 5)

    def one_block(qi):
        s_lat = jnp.einsum('bqhgd,bkhd->bhgqk', qi, k).astype(jnp.float32) * scale
        s_ctx = jnp.einsum('bqhgd,bkhd->bhgqk', qi, kc).astype(jnp.float32) * scale
        p_lat, p_ctx = joint_softmax([s_lat, s_ctx])
        return (jnp.einsum('bhgqk,bkhd->bqhgd', p_lat.astype(v.dtype), v)
                + jnp.einsum('bhgqk,bkhd->bqhgd', p_ctx.astype(vc.dtype), vc))

    o = lax.map(one_block, qb)
    return o.transpose(1, 0, 2, 3, 4, 5).reshape(bsz, seq, hq * d)

def segsum(a):
    t = a.shape[-1]
    a_rep = jnp.broadcast_to(a[..., :, None], a.shape + (t,))
    strict = jnp.tril(jnp.ones((t, t), dtype=bool), -1)
    cs = jnp.cumsum(jnp.where(strict, a_rep, 0.0), axis=-2)
    return jnp.where(jnp.tril(jnp.ones((t, t), dtype=bool)), cs, -jnp.inf)

def ssd(x, dt, a, bm, cm, init):
    bsz, seq, h, p = x.shape
    g, n = bm.shape[2], bm.shape[3]
    nc = seq // SSM_CHUNK
    rep = h // g
    f32 = jnp.float32
    bh = jnp.repeat(bm.astype(f32), rep, axis=2).reshape(bsz, nc, SSM_CHUNK, h, n)
    ch = jnp.repeat(cm.astype(f32), rep, axis=2).reshape(bsz, nc, SSM_CHUNK, h, n)
    xdt = (x.astype(f32) * dt[..., None]).reshape(bsz, nc, SSM_CHUNK, h, p)
    da = (dt * a).reshape(bsz, nc, SSM_CHUNK, h).transpose(0, 3, 1, 2)
    da_cum = jnp.cumsum(da, axis=-1)
    decay = jnp.exp(segsum(da))
    scores = jnp.einsum('bclhn,bcshn->bhcls', ch, bh) * decay
    y_diag = jnp.einsum('bhcls,bcshp->bclhp', scores, xdt)
    decay_states = jnp.exp(da_cum[..., -1:] - da_cum)
    states = jnp.einsum('bclhn,bhcl,bclhp->bchpn', bh, decay_states, xdt)
    chunk_decay = jnp.exp(da_cum[..., -1])

    def step(s, inp):
        st, dec = inp
        return s * dec[..., None, None] + st, s

    final, s_in = lax.scan(step, init, (states.transpose(1, 0, 2, 3, 4), chunk_decay.transpose(2, 0, 1)))
    s_in = s_in.transpose(1, 0, 2, 3, 4)
    y_off = jnp.einsum('bclhn,bchpn,bhcl->bclhp', ch, s_in, jnp.exp(da_cum))
    return (y_diag + y_off).reshape(bsz, seq, h, p), final

def depthwise_conv(u, w, b):
    pad = SSM_CONV // 2
    y = lax.conv_general_dilated(u, w.astype(u.dtype)[:, None, :], (1,), [(pad, pad)],
                                 dimension_numbers=('NWC', 'WIO', 'NWC'), feature_group_count=u.shape[-1])
    return y + b.astype(u.dtype)

def ssm_mixer(z, xbc, dt_raw, zc, xbcc, dtc_raw, lp, with_ctx):
    def prep(xbc_, dt_raw_):
        u = jax.nn.silu(depthwise_conv(xbc_, lp['ssm_conv_w'], lp['ssm_conv_b']))
        xs, bm, cm = jnp.split(u, [SSM_INNER, SSM_INNER + SSM_GROUPS * SSM_STATE], axis=-1)
        xs = xs.reshape(xs.shape[:-1] + (SSM_HEADS, SSM_HEAD_DIM))
        bm = bm.reshape(bm.shape[:-1] + (SSM_GROUPS, SSM_STATE))
        cm = cm.reshape(cm.shape[:-1] + (SSM_GROUPS, SSM_STATE))
        dtr = dt_raw_.astype(jnp.float32).reshape(dt_raw_.shape[:-1] + (2, SSM_HEADS))
        dt = jax.nn.softplus(dtr + lp['ssm_dt_bias'].astype(jnp.float32))
        return xs, bm, cm, dt

    a = -jnp.exp(lp['ssm_a_log'].astype(jnp.float32))
    xl, bl, cl, dtl = prep(xbc, dt_raw)
    xc, bc, cc, dtc = prep(xbcc, dtc_raw)
    init = jnp.zeros((xl.shape[0], SSM_HEADS, SSM_HEAD_DIM, SSM_STATE), jnp.float32)
    flip = lambda t: jnp.flip(t, axis=1)
    yc_f, sc_f = ssd(xc, dtc[..., 0, :], a[0], bc, cc, init)
    yl_f, _ = ssd(xl, dtl[..., 0, :], a[0], bl, cl, sc_f)
    yc_b, sc_b = ssd(flip(xc), flip(dtc[..., 1, :]), a[1], flip(bc), flip(cc), init)
    yl_b, _ = ssd(flip(xl), flip(dtl[..., 1, :]), a[1], flip(bl), flip(cl), sc_b)
    dskip = lp['ssm_d'].astype(jnp.float32)[:, None]

    def finish(yf, yb_rev, xs, z_):
        y = yf + flip(yb_rev) + dskip * xs.astype(jnp.float32)
        y = y.reshape(y.shape[:2] + (SSM_INNER,)).astype(z_.dtype) * jax.nn.silu(z_)
        return rms_norm(y, lp['ssm_norm'])

    y_lat = finish(yl_f, yl_b, xl, z)
    y_ctx = finish(yc_f, yc_b, xc, zc) if with_ctx else None
    return y_lat, y_ctx

def merge(ys, gate_pre, lp):
    gates = jax.nn.sigmoid(gate_pre + lp['b_gate']).reshape(gate_pre.shape[:-1] + (N_BRANCH, D_MODEL))
    yb = jnp.stack(ys, axis=-2)
    branch = jnp.einsum('...kw,kwd->...kd', yb, lp['w_branch'])
    return jnp.sum(gates * branch, axis=-2) @ lp['w_out']

def token_mix(h, hc, lp, cos, sin, with_ctx):
    offs = np.cumsum(IN_SIZES)[:-1].tolist()
    aq, ak, av, bq, bk, bv, cq, ck, cv, z, xbc, dt, gl = jnp.split(h @ lp['w_in'], offs, axis=-1)
    aqc, akc, avc, bqc, bkc, bvc, cqc, ckc, cvc, zc, xbcc, dtc, gc = jnp.split(hc @ lp['w_in'], offs, axis=-1)
    hs = split_heads
    rope = lambda t: apply_rope(t, cos, sin)
    qn = lambda t: rms_norm(hs(t), lp['qk_norm_q'])
    kn = lambda t: rms_norm(hs(t), lp['qk_norm_k'])
    akc_h, avc_h = hs(akc), hs(avc)
    bkc_h, bvc_h = hs(bkc), hs(bvc)
    ckc_h, cvc_h = kn(ckc), hs(cvc)
    ya = window_attention(rope(hs(aq)), rope(hs(ak)), hs(av), akc_h, avc_h, lp['attn_sink'])
    yb = neighborhood_attention(hs(bq), hs(bk), hs(bv), bkc_h, bvc_h, lp['na_rpb'])
    yc = dense_block_attention(rope(qn(cq)), rope(kn(ck)), hs(cv), ckc_h, cvc_h)
    yd, ydc = ssm_mixer(z, xbc, dt, zc, xbcc, dtc, lp, with_ctx)
    y_lat = merge([ya, yb, yc, yd], gl, lp)
    if not with_ctx:
        return y_lat, None
    yac = context_attention(hs(aqc), akc_h, avc_h, lp['attn_sink'])
    ybc = context_attention(hs(bqc), bkc_h, bvc_h, None)
    ycc = context_attention(qn(cqc), ckc_h, cvc_h, None)
    y_ctx = merge([yac, ybc, ycc, ydc], gc, lp)
    return y_lat, y_ctx

def layer(x, xc, c_act, cc_act, lp, cos, sin, with_ctx):
    mod = (c_act @ lp['w_mod'] + lp['b_mod']).reshape(c_act.shape[0], 1, 9, D_MODEL)
    modc = (cc_act @ lp['w_mod'] + lp['b_mod']).reshape(9, D_MODEL)
    m = lambda i: mod[:, :, i]
    mc = lambda i: modc[i]
    ada = lambda t, g, shift, scale: rms_norm(t, g) * (1 + scale) + shift
    ffn = lambda t, pre: swiglu(t, lp[pre + '_w_gate'], lp[pre + '_w_up'], lp[pre + '_w_down'])
    x = x + 0.5 * m(2) * ffn(ada(x, lp['norm_ffn1'], m(0), m(1)), 'ffn1')
    xc = xc + 0.5 * mc(2) * ffn(ada(xc, lp['norm_ffn1'], mc(0), mc(1)), 'ffn1')
    y, yc = token_mix(ada(x, lp['norm_mix'], m(3), m(4)), ada(xc, lp['norm_mix'], mc(3), mc(4)),
                      lp, cos, sin, with_ctx)
    x = x + m(5) * y
    x = x + 0.5 * m(8) * ffn(ada(x, lp['norm_ffn2'], m(6), m(7)), 'ffn2')
    if with_ctx:
        xc = xc + mc(5) * yc
        xc = xc + 0.5 * mc(8) * ffn(ada(xc, lp['norm_ffn2'], mc(6), mc(7)), 'ffn2')
    return x, xc

def setup_inputs(seed: int = 0) -> dict:
    key = jax.random.key(seed)
    k = jax.random.split(key, 32)
    f32 = jnp.float32
    D = D_MODEL
    L = DEPTH
    n_in = sum(IN_SIZES)
    nrm = lambda kk, shape, scale: jax.random.normal(kk, shape, f32) * scale
    gain = lambda kk, shape: 1.0 + 0.05 * jax.random.normal(kk, shape, f32)
    dt0 = jnp.exp(jax.random.uniform(k[19], (L, 2, SSM_HEADS), f32, math.log(1e-3), math.log(1e-1)))
    return {
        'x': nrm(k[0], (BATCH, SEQ, D), 1.0),
        'c': nrm(k[1], (BATCH, D), 1.0),
        'ctx': nrm(k[2], (BATCH, CTX_LEN, D), 1.0),
        'c_ctx': nrm(k[3], (D,), 1.0),
        'w_mod': nrm(k[4], (L, D, 9 * D), 0.5 * D ** -0.5),
        'b_mod': nrm(k[5], (L, 9 * D), 0.02),
        'norm_ffn1': gain(k[6], (L, D)),
        'ffn1_w_gate': nrm(k[7], (L, D, D_FF), D ** -0.5),
        'ffn1_w_up': nrm(k[8], (L, D, D_FF), D ** -0.5),
        'ffn1_w_down': nrm(k[9], (L, D_FF, D), D_FF ** -0.5),
        'norm_mix': gain(k[10], (L, D)),
        'w_in': nrm(k[11], (L, D, n_in), D ** -0.5),
        'b_gate': nrm(k[12], (L, N_BRANCH * D), 0.02),
        'attn_sink': nrm(k[13], (L, WA_Q_HEADS), 0.5),
        'na_rpb': nrm(k[14], (L, NA_HEADS, 2 * NA_ROWS - 1, 2 * NA_COLS - 1), 0.1),
        'qk_norm_q': gain(k[15], (L, HEAD_DIM)),
        'qk_norm_k': gain(k[16], (L, HEAD_DIM)),
        'ssm_conv_w': nrm(k[17], (L, SSM_CONV, SSM_CONV_CH), SSM_CONV ** -0.5),
        'ssm_conv_b': nrm(k[18], (L, SSM_CONV_CH), 0.02),
        'ssm_dt_bias': dt0 + jnp.log(-jnp.expm1(-dt0)),
        'ssm_a_log': jnp.log(jax.random.uniform(k[20], (L, 2, SSM_HEADS), f32, 1.0, 16.0)),
        'ssm_d': 1.0 + nrm(k[21], (L, SSM_HEADS), 0.1),
        'ssm_norm': gain(k[22], (L, SSM_INNER)),
        'w_branch': nrm(k[23], (L, N_BRANCH, BRANCH_W, D), BRANCH_W ** -0.5),
        'w_out': nrm(k[24], (L, D, D), D ** -0.5),
        'norm_ffn2': gain(k[25], (L, D)),
        'ffn2_w_gate': nrm(k[26], (L, D, D_FF), D ** -0.5),
        'ffn2_w_up': nrm(k[27], (L, D, D_FF), D ** -0.5),
        'ffn2_w_down': nrm(k[28], (L, D_FF, D), D_FF ** -0.5),
        'final_norm': gain(k[29], (D,)),
    }

def reference(x, c, ctx, c_ctx, w_mod, b_mod, norm_ffn1, ffn1_w_gate, ffn1_w_up, ffn1_w_down,
              norm_mix, w_in, b_gate, attn_sink, na_rpb, qk_norm_q, qk_norm_k,
              ssm_conv_w, ssm_conv_b, ssm_dt_bias, ssm_a_log, ssm_d, ssm_norm,
              w_branch, w_out, norm_ffn2, ffn2_w_gate, ffn2_w_up, ffn2_w_down, final_norm):
    cos, sin = rope_tables(x.shape[1])
    c_act = jax.nn.silu(c)
    cc_act = jax.nn.silu(c_ctx)
    xc = ctx
    for l in range(DEPTH):
        lp = {
            'w_mod': w_mod[l], 'b_mod': b_mod[l],
            'norm_ffn1': norm_ffn1[l], 'ffn1_w_gate': ffn1_w_gate[l], 'ffn1_w_up': ffn1_w_up[l],
            'ffn1_w_down': ffn1_w_down[l],
            'norm_mix': norm_mix[l], 'w_in': w_in[l], 'b_gate': b_gate[l],
            'attn_sink': attn_sink[l], 'na_rpb': na_rpb[l],
            'qk_norm_q': qk_norm_q[l], 'qk_norm_k': qk_norm_k[l],
            'ssm_conv_w': ssm_conv_w[l], 'ssm_conv_b': ssm_conv_b[l], 'ssm_dt_bias': ssm_dt_bias[l],
            'ssm_a_log': ssm_a_log[l], 'ssm_d': ssm_d[l], 'ssm_norm': ssm_norm[l],
            'w_branch': w_branch[l], 'w_out': w_out[l],
            'norm_ffn2': norm_ffn2[l], 'ffn2_w_gate': ffn2_w_gate[l], 'ffn2_w_up': ffn2_w_up[l],
            'ffn2_w_down': ffn2_w_down[l],
        }
        x, xc = layer(x, xc, c_act, cc_act, lp, cos, sin, l < DEPTH - 1)
    return rms_norm(x, final_norm)


_drawn_inputs = setup_inputs


def setup_inputs(seed=0):
    import zlib

    import numpy as np

    out = dict(_drawn_inputs(seed))
    spreads = {}
    factors = {'norm_ffn1': 5.025,
     'norm_mix': 3.06,
     'b_gate': 8.0,
     'attn_sink': 64.0,
     'na_rpb': 8.0,
     'qk_norm_q': 8.0,
     'qk_norm_k': 8.0,
     'ssm_conv_b': 8.0,
     'ssm_d': 64.0,
     'ssm_norm': 4.45,
     'norm_ffn2': 5.344}
    for name, (base, spread) in spreads.items():
        noise = np.random.default_rng([zlib.crc32(name.encode()), seed]).standard_normal(out[name].shape)
        drawn = base * np.exp(spread * noise) if base else spread * noise
        out[name] = jnp.asarray(drawn.astype(out[name].dtype))
    for name, factor in factors.items():
        out[name] = (out[name] * factor).astype(out[name].dtype)
    return out
```

```python
from contextlib import ExitStack

import numpy as np

import concourse.bass as bass
from concourse import mybir

F32 = mybir.dt.float32
F32R = mybir.dt.float32r
ALU = mybir.AluOpType
ACT = mybir.ActivationFunctionType
AX_X = mybir.AxisListType.X

P = 128
LAYERS = 2
D = 1024
DC = D // P
LAT, CTX = 256, 256
TOK = LAT + CTX
FF = 2816
HD = 64
EPS = 1e-6
NEG = -1e30
BIG = 8.0
SCALE = HD ** -0.5
GRID_W, NA_ROWS, NA_COLS = 64, 8, 16
ROWS = LAT // GRID_W
CONV = 5
DT_COL = 2816
GATE_COL = DT_COL + 8
MOD_CHUNKS = 9 * DC

AQ, AK, AV, BQ, BK, BV, CQ, CK, CV, Z, XS, SB_, SC_ = 0, 2, 3, 4, 6, 8, 10, 12, 13, 14, 16, 18, 20
IN_CHUNKS = 22
QCHUNKS = [AQ, AQ + 1, BQ, BQ + 1, CQ, CQ + 1, Z, Z + 1]
KCHUNKS = [c for c in range(IN_CHUNKS) if c not in QCHUNKS]
VCHUNKS = [AV, BV, BV + 1, CV]

V_BMOD, V_NORM, V_BGATE = 0, 72, 96
V_CONVW, V_CONVB, V_SNORM, V_QG, V_KG, V_FIN, V_C, V_CC = 0, 30, 36, 38, 39, 40, 48, 56
PACK2 = 64

CONST_COLS = {}
_at = 0
for _name, _w in (("ident", 128), ("ones", 128), ("blockones", 128), ("rot", 128), ("swap", 128), ("trif", 384),
                  ("trib", 384), ("maskf", 384), ("maskb", 384), ("wmask", 512), ("nvalid", 256), ("nneg", 256),
                  ("ropec", 256), ("ropes", 256), ("sel", 1024)):
    CONST_COLS[_name] = (_at, _at + _w)
    _at += _w
CONSTS = _at


def constants():
    c = np.zeros((P, CONSTS), np.float32)

    def put(name, a):
        lo, hi = CONST_COLS[name]
        c[:a.shape[0], lo:hi] = a

    p = np.arange(P)[:, None]
    f = np.arange(P)[None, :]
    put("ident", (p == f).astype(np.float32))
    put("ones", np.ones((P, P), np.float32))
    put("blockones", (p // HD == f // HD).astype(np.float32))
    rot = np.zeros((P, P), np.float32)
    for i in range(P):
        if i % 32 < 16:
            rot[i + 16, i] = -1.0
        else:
            rot[i - 16, i] = 1.0
    put("rot", rot)
    put("swap", ((p + HD) % P == f).astype(np.float32))
    q = np.arange(384)[None, :] - P
    put("trif", (q >= p).astype(np.float32))
    put("trib", (q <= p).astype(np.float32))
    put("maskf", np.where(q >= p, 0.0, NEG).astype(np.float32))
    put("maskb", np.where(q <= p, 0.0, NEG).astype(np.float32))
    k = np.arange(LAT)[None, :]
    put("wmask", np.concatenate([np.where(np.abs(t * P + p - k) <= 128, 0.0, NEG) for t in range(2)], 1).astype(np.float32))
    qc, kc = p % GRID_W, k % GRID_W
    start = np.clip(qc - NA_COLS // 2, 0, GRID_W - NA_COLS)
    ok = (kc >= start) & (kc < start + NA_COLS)
    put("nvalid", np.where(ok, BIG, 0.0).astype(np.float32))
    put("nneg", np.where(ok, 0.0, NEG).astype(np.float32))
    pos = np.arange(LAT)
    axes = np.stack([pos // GRID_W, pos % GRID_W], 0).astype(np.float32)
    inv = (np.float32(1.0) / (np.float32(10000.0) ** (np.arange(HD // 4, dtype=np.float32) * np.float32(4.0) / np.float32(HD)))).astype(np.float32)
    ang = np.zeros((P, LAT), np.float32)
    for i in range(P):
        ang[i] = axes[(i % HD) // 32] * inv[i % 16]
    put("ropec", np.cos(ang))
    put("ropes", np.sin(ang))
    sel = np.zeros((8, 8, P), np.float32)
    for r in range(8):
        sel[r, r] = 1.0
    put("sel", sel.reshape(8, 8 * P))
    return c


class Signal:

    def __init__(self, nc, ctx, name, values, by=1):
        self.sem = ctx.enter_context(nc.semaphore(name))
        self.name, self.values, self.by, self.count = name, values, by, 0

    def done(self, ins, step=None):
        ins.then_inc(self.sem, self.by)
        self.count += self.by
        self.values[self.name, step] = self.count

    def mark(self, step):
        self.values[self.name, step] = self.count

    def wait(self, eng, step):
        eng.wait_ge(self.sem, self.values.get((self.name, step), self.by))


class Unit:

    def __init__(self, kind, rows, dmas):
        self.kind, self.rows, self.dmas = kind, rows, dmas


SLOTS = 4
SLOT_ROWS = 10
PARTS = [(0, 8), (8, 8), (16, 6)]
MOD_FIRST = 28
MOD_AT = {(0, 1, 0): (0, 28), (0, 1, 1): (0, 44), (0, 1, 2): (0, 60),
          (0, 2, 0): (1, 0), (0, 2, 1): (1, 16), (0, 2, 2): (1, 32),
          (1, 1, 0): (1, 44), (1, 1, 2): (1, 60)}
MOD_EARLY = 3 * DC


def plan_units():
    units, first = [], {}

    def stage(name, n, kind, rows, dmas=1):
        first[name] = len(units)
        units.extend(Unit(kind, rows, dmas) for _ in range(n))

    for l in range(LAYERS):
        if l == 0:
            stage("mod", MOD_FIRST, "mod", DC)
        for ffn in (1, 2):
            if ffn == 2:
                stage(("in", l), IN_CHUNKS, "product", DC)
                stage(("merge", l), 4 * DC, "product", DC + 2, 2)
                stage(("out", l), DC, "product", DC)
            for part, (_, n) in enumerate(PARTS):
                first["up", l, ffn, part] = len(units)
                for _ in range(2 * n):
                    if (l, ffn, part) in MOD_AT:
                        units.append(Unit("mod", DC, 1))
                    units.append(Unit("product", DC, 1))
                stage(("down", l, ffn, part), DC, "product", n)
    count, products = [0] * SLOTS, 0
    for u, unit in enumerate(units):
        unit.slot = u % SLOTS
        count[unit.slot] += 16 * unit.dmas
        unit.loaded = count[unit.slot]
        unit.product = products
        products += unit.kind == "product"
    return units, first


def build(nc, values, x, c, ctx_tokens, c_ctx, w_mod, b_mod, norm_ffn1, ffn1_w_gate, ffn1_w_up, ffn1_w_down,
          norm_mix, w_in, b_gate, attn_sink, na_rpb, qk_norm_q, qk_norm_k, ssm_conv_w, ssm_conv_b, ssm_dt_bias,
          ssm_a_log, ssm_d, ssm_norm, w_branch, w_out, norm_ffn2, ffn2_w_gate, ffn2_w_up, ffn2_w_down, final_norm,
          consts, out):
    units, first = plan_units()
    product_units = [u for u, unit in enumerate(units) if unit.kind == "product"]
    ffn_weights = {1: (ffn1_w_gate, ffn1_w_up, ffn1_w_down), 2: (ffn2_w_gate, ffn2_w_up, ffn2_w_down)}

    with ExitStack() as ctx:
        def sb(name, shape, dt=F32, where=ctx):
            return where.enter_context(nc.sbuf_tensor(name, shape, dt))

        def signal(name, by=1):
            return Signal(nc, ctx, name, values, by)

        X = sb("X", [P, DC, TOK])
        h_hi = sb("h_hi", [P, DC, TOK], F32R)
        h_lo = sb("h_lo", [P, DC, TOK], F32R)
        raw = [sb(f"raw{s}", [P, SLOT_ROWS, P]) for s in range(SLOTS)]
        w_hi = [sb(f"w_hi{s}", [P, SLOT_ROWS, P], F32R) for s in range(2)]
        w_lo = [sb(f"w_lo{s}", [P, SLOT_ROWS, P], F32R) for s in range(2)]
        cst = sb("cst", [P, CONSTS])
        vec1 = sb("vec1", [P, LAYERS, P])
        vec2 = sb("vec2", [P, LAYERS, PACK2])
        skip_all = sb("skip_all", [P, LAYERS * 4])
        skip_w = sb("skip_w", [P, LAYERS, 2])
        cact = sb("cact", [P, DC, 32])
        mod_row = sb("mod_row", [P, TOK])
        mod = sb("mod", [P, MOD_CHUNKS, 2])
        gain = sb("gain", [P, 3, DC, 2])
        rstd = sb("rstd", [P, TOK])
        wa = sb("wa", [P, 2, TOK])
        wb = sb("wb", [P, 2, TOK])
        wsmall = sb("wsmall", [P, 8])
        nbias = sb("nbias", [P, 4, 2, LAT])
        scores = sb("scores", [P, 2, TOK])
        probs = sb("probs", [P, 2, TOK])
        probs_t = sb("probs_t", [P, 4, LAT])
        sink8 = sb("sink8", [P, 4])
        eps_col = sb("eps_col", [P, 1])
        gatev = sb("gatev", [P, 3, DC, 2])
        smax = sb("smax", [P, 2, 4])
        srcp = sb("srcp", [P, 2, 2])
        dt_t = sb("dt_t", [8, TOK])
        da_t = sb("da_t", [8, TOK])
        dtv = sb("dtv", [8, 4])
        tok = sb("tok", [P, 4, 16])
        tokf = sb("tokf", [P, 4, 8])
        tokb = sb("tokb", [P, 4, 8])
        nct = sb("nct", [P, 4, 8])
        tct = sb("tct", [P, 2, 8])
        tot = sb("tot", [P, 8])
        wdt_raw = sb("wdt_raw", [P, DC, 8])
        wdt_hi = sb("wdt_hi", [P, DC, 8], F32R)
        wdt_lo = sb("wdt_lo", [P, DC, 8], F32R)
        with ExitStack() as region:
            inner_hi = sb("inner_hi", [P, 8, TOK], F32R, region)
            inner_lo = sb("inner_lo", [P, 8, TOK], F32R, region)
        with ExitStack() as region:
            Q = sb("Q", [P, 8, TOK], F32, region)
            with ExitStack() as mixer:
                K = sb("K", [P, 14, TOK], F32, mixer)
                v_tok = sb("v_tok", [P, 4, 4 * P], F32, mixer)
                x_tok = sb("x_tok", [P, 4, 2 * P], F32, mixer)
                k_swap = sb("k_swap", [P, 2, TOK], F32, mixer)
            with ExitStack() as merge:
                y_hi = sb("y_hi", [P, 8, TOK], F32R, merge)
                y_lo = sb("y_lo", [P, 8, TOK], F32R, merge)
        with ExitStack() as region:
            x_in = sb("x_in", [P, 4, D], F32, region)
            pack1 = sb("pack1", [P, LAYERS, P], F32, region)
            pack2 = sb("pack2", [PACK2, LAYERS, P], F32, region)
            out_rows = sb("out_rows", [P, 2, D], F32, region)
        bias_rows = nc.dram_tensor("bias_rows", (LAYERS, 4, 2 * ROWS - 1, GRID_W, P), F32, kind="Internal").ap()
        mod_rows = nc.dram_tensor("mod_rows", (LAYERS, 2, 4, MOD_CHUNKS * P), F32, kind="Internal").ap()
        bank = [ctx.enter_context(nc.psum_tensor(f"bank{b}", [P, TOK], F32)) for b in range(8)]

        def const(name):
            lo, hi = CONST_COLS[name]
            return cst[:, lo:hi]

        def chunk(c):
            return Q[:, QCHUNKS.index(c)] if c in QCHUNKS else K[:, KCHUNKS.index(c)]

        loaded = [ctx.enter_context(nc.semaphore(f"loaded{s}")) for s in range(SLOTS)]
        unit_done = ctx.enter_context(nc.semaphore("unit_done"))
        hi_made = ctx.enter_context(nc.semaphore("hi_made"))
        lo_made = ctx.enter_context(nc.semaphore("lo_made"))
        silu_done = ctx.enter_context(nc.semaphore("silu_done"))
        inner_made = ctx.enter_context(nc.semaphore("inner_made"))
        inner_hi_made = ctx.enter_context(nc.semaphore("inner_hi_made"))
        inner_lo_made = ctx.enter_context(nc.semaphore("inner_lo_made"))
        added = ctx.enter_context(nc.semaphore("added"))
        gate_done = ctx.enter_context(nc.semaphore("gate_done"))
        gated = ctx.enter_context(nc.semaphore("gated"))
        branch_added = ctx.enter_context(nc.semaphore("branch_added"))
        mod_copied = ctx.enter_context(nc.semaphore("mod_copied"))
        mod_stored = ctx.enter_context(nc.semaphore("mod_stored"))
        mod_loads = signal("mod_loads", 16)
        mod_turned = signal("mod_turned")
        start_loads = signal("start_loads", 16)
        pack_loads = signal("pack_loads", 16)
        layer_loads = signal("layer_loads", 16)
        bias_loads = signal("bias_loads", 16)
        rows_written = signal("rows_written", 16)
        out_stored = signal("out_stored", 16)
        pe_start = signal("pe_start")
        start_copied = signal("start_copied")
        cond_ready = signal("cond_ready")
        vectors = signal("vectors")
        squares = signal("squares")
        sums = signal("sums")
        roots = signal("roots")
        normed = signal("normed")
        modulated = signal("modulated")
        h_hi_made = signal("h_hi_made")
        h_made = signal("h_made")
        act_chain = signal("act_chain")
        dve_chain = signal("dve_chain")
        pool_chain = signal("pool_chain")
        projected = signal("projected")
        prep_done = signal("prep_done")
        prep_read = signal("prep_read")
        prepared = signal("prepared")
        act_read = signal("act_read")
        act_prepared = signal("act_prepared")
        conv_in = signal("conv_in")
        conv_out = signal("conv_out")
        scored = signal("scored")
        masked = signal("masked")
        ctx_copied = signal("ctx_copied")
        bounded = signal("bounded")
        exped = signal("exped")
        normalised = signal("normalised")
        turned = signal("turned")
        turned_copied = signal("turned_copied")
        mixed = signal("mixed")
        y_stored = signal("y_stored")
        cb_done = signal("cb_done")
        cum_spread = signal("cum_spread")
        spread = signal("spread")
        decay_arg = signal("decay_arg")
        decayed = signal("decayed")
        weighed = signal("weighed")
        ssm_done = signal("ssm_done")
        ssm_read = signal("ssm_read")
        y_hi_made = signal("y_hi_made")
        y_made = signal("y_made")
        cleared = signal("cleared")
        soft = signal("soft")
        convolved = signal("convolved")
        pads_cleared = signal("pads_cleared")
        sunk = signal("sunk")
        skipped = signal("skipped")
        ssm_out = signal("ssm_out")
        z_done = signal("z_done")

        scores_flat = scores[:, :, :].rearrange("p a b -> p (a b)")
        probs_flat = probs[:, :, :].rearrange("p a b -> p (a b)")
        weighed_flat = probs_t[:, :, :].rearrange("p a b -> p (a b)")
        padded = [f[:, 0:2 * (LAT + CONV - 1)].rearrange("p (s t) -> p s t", s=2) for f in (scores_flat, probs_flat)]

        def attention_tasks(last_layer):
            return [(br, h, st, qt) for br in range(3) for h in range(4) for st in range(1 if last_layer else 2) for qt in range(2)]

        def value_column(br, h):
            return (h // 2 * HD, P + h * HD, 3 * P + h // 2 * HD)[br]

        def dve_link(dve, ins):
            dve_chain.done(ins, dve_chain.count)
            dve.wait_ge(dve_chain.sem, dve_chain.count)

        def act_link(act, ins):
            act_chain.done(ins, act_chain.count)
            act.wait_ge(act_chain.sem, act_chain.count)

        block = ctx.enter_context(nc.Block())

        def tokens(l, name):
            return LAT if l == LAYERS - 1 and name in ("q", "merge", "ffn2") else TOK

        def streams(n):
            return range(n // LAT)

        inner_first = {}
        n_inner = 0
        for l in range(LAYERS):
            for ffn in (1, 2):
                for part, (_, n) in enumerate(PARTS):
                    inner_first[l, ffn, part] = n_inner
                    n_inner += n
        add_first = {}
        n_add = 0
        for l in range(LAYERS):
            for step in [(1, 0), (1, 1), (1, 2), "out", (2, 0), (2, 1), (2, 2)]:
                add_first[l, step] = n_add
                n_add += DC

        @block.sync
        def _(sp):
            def columns(w, l, col, rows=None, row0=0):
                v = w[l].rearrange("(c p) n -> p c n", p=P)
                if rows is not None:
                    v = v[:, row0:row0 + rows, :]
                return v[:, :, bass.ds(col, P)]

            def load(u, i, per, *sources):
                unit = units[u]
                if u >= SLOTS or not isinstance(i, int):
                    old = units[u - SLOTS] if isinstance(i, int) else unit
                    if old.kind == "mod":
                        sp.wait_ge(unit_done, u - SLOTS + 1 + i * per[0])
                    else:
                        n = old.product if isinstance(i, int) else unit.product - SLOTS * per[1] // per[0]
                        sp.wait_ge(lo_made, n + 1 + i * per[1])
                for rows, src in sources:
                    sp.dma_start(raw[unit.slot][:, rows[0]:rows[1], :], src).then_inc(loaded[unit.slot], 16)

            def stage(u0, n, source):
                for j in range(SLOTS):
                    load(u0 + j, 0, (0, 0), *source(j))
                turns = (n - SLOTS) // SLOTS
                if turns > 0:
                    with sp.Fori(1, turns + 1) as i:
                        for j in range(SLOTS):
                            load(u0 + j, i, (SLOTS, SLOTS), *source(i * SLOTS + j))
                for j in range(SLOTS * (turns + 1), n):
                    load(u0 + j, 0, (0, 0), *source(j))

            for l in range(LAYERS):
                for h in range(4):
                    row = na_rpb[l, h, NA_ROWS - ROWS, 0:1]
                    src = bass.AP(row.tensor, row.offset, [[2 * NA_COLS - 1, 2 * ROWS - 1], [0, GRID_W], [1, P]])
                    rows_written.done(sp.dma_start(bias_rows[l, h], src), "all")
            start_loads.done(sp.dma_start(pack1[0:MOD_CHUNKS, :, :], b_mod.rearrange("l (r c) -> r l c", c=P)))
            for n, w in enumerate((norm_ffn1, norm_mix, norm_ffn2)):
                r = V_NORM + n * DC
                start_loads.done(sp.dma_start(pack1[r:r + DC, :, :], w.rearrange("l (r c) -> r l c", c=P)))
            start_loads.done(sp.dma_start(pack1[V_BGATE:V_BGATE + 4 * DC, :, :], b_gate.rearrange("l (r c) -> r l c", c=P)))
            for j in range(CONV):
                r = V_CONVW + j * 6
                start_loads.done(sp.dma_start(pack2[r:r + 6, :, :], ssm_conv_w[:, j, :].rearrange("l (r c) -> r l c", c=P)))
            start_loads.done(sp.dma_start(pack2[V_CONVB:V_CONVB + 6, :, :], ssm_conv_b.rearrange("l (r c) -> r l c", c=P)))
            start_loads.done(sp.dma_start(pack2[V_SNORM:V_SNORM + 2, :, :], ssm_norm.rearrange("l (r c) -> r l c", c=P)))
            for v, w in ((V_QG, qk_norm_q), (V_KG, qk_norm_k)):
                for half in range(2):
                    start_loads.done(sp.dma_start(pack2[v:v + 1, :, half * HD:(half + 1) * HD],
                                                  w.rearrange("(a l) c -> a l c", a=1)))
            start_loads.done(sp.dma_start(skip_all[:, :], ssm_d.rearrange("(a l) h -> a (l h)", a=1).to_broadcast([P, LAYERS * 4])))
            for l in range(LAYERS):
                start_loads.done(sp.dma_start(pack2[V_FIN:V_FIN + DC, l, :], final_norm.rearrange("(r c) -> r c", c=P)))
                start_loads.done(sp.dma_start(pack2[V_C:V_C + DC, l, :], c.rearrange("a (r c) -> (a r) c", c=P)))
                start_loads.done(sp.dma_start(pack2[V_CC:V_CC + DC, l, :], c_ctx.rearrange("(r c) -> r c", c=P)))
            start_loads.done(sp.dma_start(cst[:, :], consts), "all")
            pack_loads.done(sp.dma_start(x_in[:, 0:2, :], x[0].rearrange("(t p) d -> p t d", p=P)))
            pack_loads.done(sp.dma_start(x_in[:, 2:4, :], ctx_tokens[0].rearrange("(t p) d -> p t d", p=P)), "all")

            for l in range(LAYERS):
                if l > 0:
                    y_made.wait(sp, (l - 1, 7))
                layer_loads.done(sp.dma_start(sink8[:, :], attn_sink[l:l + 1, :].to_broadcast([P, 4])))
                layer_loads.done(sp.dma_start(dtv[:, 0:1], ssm_dt_bias[l].rearrange("a (b o) -> (a b) o", o=1)))
                layer_loads.done(sp.dma_start(dtv[:, 1:2], ssm_a_log[l].rearrange("a (b o) -> (a b) o", o=1)))
                layer_loads.done(sp.dma_start(wdt_raw[:, :, :], w_in[l].rearrange("(c p) n -> p c n", p=P)[:, :, DT_COL:GATE_COL]), l)
                if l == 0:
                    rows_written.wait(sp, "all")
                for h in range(4):
                    for qr in range(ROWS):
                        t, a = qr // 2, qr % 2
                        src = bass.AP(bias_rows.tensor, bias_rows[l, h, ROWS - 1 - qr, 0, NA_COLS - 1:NA_COLS].offset,
                                      [[P - 1, GRID_W], [GRID_W * P, ROWS], [1, GRID_W]])
                        bias_loads.done(sp.dma_start(
                            nbias[a * GRID_W:(a + 1) * GRID_W, h, t, :].rearrange("p (r c) -> p r c", r=ROWS), src), l)
                if l == 0:
                    stage(first["mod"], MOD_FIRST, lambda j: [((0, DC), columns(w_mod, 0, j * P))])
                for ffn in (1, 2):
                    wg, wu, wd = ffn_weights[ffn]
                    if ffn == 2:
                        stage(first["in", l], IN_CHUNKS, lambda j: [((0, DC), columns(w_in, l, j * P))])

                        u0 = first["merge", l]

                        def merge_unit(k, d, i):
                            load(u0 + k, i, (SLOTS, SLOTS) if not isinstance(i, int) else (0, 0),
                                 ((0, DC), columns(w_in, l, GATE_COL + k * D + d * P)),
                                 ((DC, DC + 2), w_branch[l, k].rearrange("(c p) n -> p c n", p=P)[:, :, bass.ds(d * P, P)]))
                        for k in range(4):
                            merge_unit(k, 0, 0)
                        with sp.Fori(1, DC) as d:
                            for k in range(4):
                                merge_unit(k, d, d)
                        stage(first["out", l], DC, lambda j: [((0, DC), columns(w_out, l, j * P))])
                    for part, (c0, n) in enumerate(PARTS):
                        u0 = first["up", l, ffn, part]

                        extra = MOD_AT.get((l, ffn, part))
                        step = 2 if extra else 1

                        def turn_loads(i, per):
                            for j in range(4):
                                if extra:
                                    load(u0 + 2 * j, i, per, ((0, DC), columns(w_mod, extra[0], i * (4 * P) + (extra[1] + j) * P)))
                                load(u0 + step * j + step - 1, i, per,
                                     ((0, DC), columns((wg, wu)[j % 2], l, i * (2 * P) + (c0 + j // 2) * P)))
                        turn_loads(0, (0, 0))
                        with sp.Fori(1, n // 2) as i:
                            turn_loads(i, (4 * step, 4))
                        stage(first["down", l, ffn, part], DC, lambda j: [((0, n), columns(wd, l, j * P, n, c0))])
            for t in range(2):
                start_copied.wait(sp, ("out", t))
                out_stored.done(sp.dma_start(out[0, t * P:(t + 1) * P, :], out_rows[:, t, :]), t)
            out_stored.wait(sp, 1)

        def split_hi(act, n, i=0, per=(0, 0)):
            if n >= len(product_units):
                return
            unit = units[product_units[n]]
            act.wait_ge(loaded[unit.slot], unit.loaded + i * (16 * unit.dmas * per[0] // SLOTS))
            if n >= 2:
                act.wait_ge(unit_done, product_units[n - 2] + 1 + i * per[0])
            act.activation(w_hi[n % 2][:, 0:unit.rows, :], raw[unit.slot][:, 0:unit.rows, :], ACT.Copy).then_inc(hi_made, 1)

        def split_lo(dve, n, i=0, per=(0, 0)):
            if n >= len(product_units):
                return
            unit = units[product_units[n]]
            dve.wait_ge(hi_made, n + 1 + i * per[1])
            dve.tensor_tensor(w_lo[n % 2][:, 0:unit.rows, :], raw[unit.slot][:, 0:unit.rows, :],
                              w_hi[n % 2][:, 0:unit.rows, :].bitcast(F32), ALU.subtract).then_inc(lo_made, 1)

        def turns(eng, n_turns, body):
            body(0)
            if n_turns > 2:
                with eng.Fori(1, n_turns - 1) as i:
                    body(i)
            if n_turns > 1:
                body(n_turns - 1)

        def at(u0, j, i, step=1):
            j = step * j + step - 1
            return (u0 + 4 * step * i + j, 0, (0, 0)) if isinstance(i, int) else (u0 + j, i, (4 * step, 4))

        def step_of(l, ffn, part):
            return 2 if (l, ffn, part) in MOD_AT else 1

        mod_first = {"start": 0}
        n_mod = MOD_FIRST // 4
        for key in sorted(MOD_AT):
            mod_first[key] = n_mod
            n_mod += PARTS[key[2]][1] // 2
        mod_first["end"] = n_mod

        @block.tensor
        def _(pe):
            def product(u, i, per, psum, rows, rhs, before=None, row0=0, signal_it=True):
                unit = units[u]
                pe.wait_ge(lo_made, unit.product + 1 + i * per[1])
                s = unit.product % 2
                for k in range(rows):
                    if before:
                        before(k)
                    hi, lo = rhs(k)
                    pe.matmul(psum, w_hi[s][:, row0 + k, :], hi, start=(k == 0), stop=False)
                    pe.matmul(psum, w_hi[s][:, row0 + k, :], lo, start=False, stop=False)
                    mm = pe.matmul(psum, w_lo[s][:, row0 + k, :], hi, start=False, stop=(k == rows - 1))
                if signal_it:
                    mm.then_inc(unit_done, 1)

            def h_rhs(n):
                return lambda k: (h_hi[:, k, 0:n], h_lo[:, k, 0:n])

            def sum_squares(key, n):
                for k in range(DC):
                    squares.wait(pe, (key, k))
                    mm = pe.matmul(bank[6][:, 0:n], const("ones"), wa[:, k % 2, 0:n], start=(k == 0), stop=(k == DC - 1))
                    sums.done(mm, (key, k))

            def modulation(u, i, per, j, m):
                unit = units[u]
                pe.wait_ge(loaded[unit.slot], unit.loaded + i * (16 * per[0] // SLOTS))
                if j == 0 and m is not None:
                    pe.wait_ge(mod_copied, m)
                for k in range(DC):
                    rows = slice(32 * (k % 4), 32 * (k % 4) + 32)
                    mm = pe.matmul(bank[7][rows, j * P:(j + 1) * P], cact[:, k, :], raw[unit.slot][:, k, :],
                                   start=(k < 4), stop=(k >= 4))
                mm.then_inc(unit_done, 1)

            def turn_modulation(l, half):
                mod_loads.wait(pe, (l, half))
                r0, r1 = ((0, MOD_EARLY), (MOD_EARLY, MOD_CHUNKS))[half]
                n = r1 - r0
                pe.wait_ge(mod_copied, MOD_FIRST // 4 if (l, half) == (0, 0) else mod_first[{(0, 1): (0, 2, 0), (1, 0): (1, 1, 0), (1, 1): "end"}[l, half]])
                for s in range(2):
                    for j in range(4):
                        mm = pe.matmul(bank[7][:, s * MOD_CHUNKS + r0:s * MOD_CHUNKS + r1], scores_flat[0:n, (4 * s + j) * P:(4 * s + j + 1) * P],
                                       const("ident")[0:n, 0:n], start=(j == 0), stop=(j == 3))
                mod_turned.done(mm, (l, half))

            def up(l, ffn, part, n):
                u0, c0 = first["up", l, ffn, part], inner_first[l, ffn, part]
                step = step_of(l, ffn, part)

                if (ffn, part) == (1, 0):
                    vectors.wait(pe, (l, 0))

                def body(i):
                    for j in range(4):
                        if step == 2:
                            u, ii, per = at(u0, j, i, 2)
                            m0 = mod_first[l, ffn, part]
                            modulation(u - 1, ii, per, j, i + m0)
                        if not (isinstance(i, int) and i == 0):
                            read = silu_done if j % 2 == 0 else inner_made
                            pe.wait_ge(read, i * 2 + (c0 + j // 2 - 1))
                        wait_h = part == 0 and isinstance(i, int) and i == 0 and j == 0
                        product(*at(u0, j, i, step), bank[j][:, 0:n], DC, h_rhs(n),
                                (lambda k: h_made.wait(pe, (l, ffn, k))) if wait_h else None)
                turns(pe, PARTS[part][1] // 2, body)

            def down(l, ffn, part, n):
                u0, a0 = first["down", l, ffn, part], add_first[l, (ffn, part)]
                rows = PARTS[part][1]
                last = inner_first[l, ffn, part] + rows
                for d in range(DC):
                    if a0 + d >= 2:
                        pe.wait_ge(added, a0 + d - 1)
                    product(u0 + d, 0, (0, 0), bank[4 + d % 2][:, 0:n], rows, lambda k: (inner_hi[:, k, 0:n], inner_lo[:, k, 0:n]),
                            (lambda k: pe.wait_ge(inner_lo_made, last - rows + k + 1)) if d == 0 else None)

            start_loads.wait(pe, "all")
            pack_loads.wait(pe, "all")
            for l in range(LAYERS):
                pe.transpose(bank[0][:, l * P:(l + 1) * P], pack1[:, l, :], const("ident"))
            for l in range(LAYERS):
                mm = pe.transpose(bank[0][:, 256 + l * PACK2:256 + (l + 1) * PACK2], pack2[:, l, :], const("ident")[0:PACK2, 0:PACK2])
            pe_start.done(mm, "packs")
            for k in range(DC):
                if k >= 3:
                    start_copied.wait(pe, ("x", k - 3))
                for t in range(4):
                    mm = pe.transpose(bank[1 + k % 3][:, t * P:(t + 1) * P], x_in[:, t, k * P:(k + 1) * P], const("ident"))
                pe_start.done(mm, ("x", k))

            for l in range(LAYERS):
                last_layer = l == LAYERS - 1
                if l == 0:
                    cond_ready.wait(pe, "c")
                    cleared.wait(pe, "all")

                    def mod_turn(i):
                        for j in range(4):
                            u, ii, per = at(first["mod"], j, i)
                            modulation(u, ii, (4, 4) if per[0] else per, j, None if isinstance(i, int) and i == 0 else i)
                    turns(pe, MOD_FIRST // 4, mod_turn)
                turn_modulation(l, 0)

                sum_squares((l, 1), TOK)
                for part in range(len(PARTS)):
                    up(l, 1, part, TOK)
                    down(l, 1, part, TOK)

                turn_modulation(l, 1)
                sum_squares((l, "mix"), TOK)
                u0 = first["in", l]
                for c in range(IN_CHUNKS):
                    if c >= 4:
                        projected.wait(pe, (l, c - 4))
                    n = tokens(l, "q") if c in QCHUNKS or c >= SC_ else TOK
                    product(u0 + c, 0, (0, 0), bank[c % 4][:, 0:n], DC, h_rhs(n),
                            (lambda k: h_made.wait(pe, (l, "mix", k))) if c == 0 else None)
                prepared.wait(pe, (l, "wdt"))
                for k in range(DC):
                    pe.matmul(bank[4][0:8, :], wdt_hi[:, k, :], h_hi[:, k, :], start=(k == 0), stop=False)
                    pe.matmul(bank[4][0:8, :], wdt_hi[:, k, :], h_lo[:, k, :], start=False, stop=False)
                    mm = pe.matmul(bank[4][0:8, :], wdt_lo[:, k, :], h_hi[:, k, :], start=False, stop=(k == DC - 1))
                prep_done.done(mm, (l, "dt"))

                for v, c in enumerate(VCHUNKS):
                    b = 5 + v % 2
                    if v >= 2:
                        prep_read.wait(pe, (l, "v", v - 2))
                    projected.wait(pe, (l, c))
                    for t in range(4):
                        mm = pe.transpose(bank[b][:, t * P:(t + 1) * P], chunk(c)[:, t * P:(t + 1) * P], const("ident"))
                    prep_done.done(mm, (l, "v", v))
                for i, c in enumerate((CQ, CQ + 1, CK)):
                    n = TOK if c == CK else tokens(l, "q")
                    if i == 0:
                        prep_read.wait(pe, (l, "v", 2))
                    else:
                        act_read.wait(pe, (l, "qk", i - 1))
                    squares.wait(pe, (l, "qk", i))
                    mm = pe.matmul(bank[5][:, 0:n], const("blockones"), wa[:, i % 2, 0:n], start=True, stop=True)
                    prep_done.done(mm, (l, "qk", i))
                for i, c in enumerate((AQ, AQ + 1, AK, CQ, CQ + 1, CK)):
                    b = 6 + i % 2
                    if i == 0:
                        prep_read.wait(pe, (l, "v", 3))
                    if i >= 2:
                        prep_read.wait(pe, (l, "rope", i - 2))
                    if c >= CQ:
                        prepared.wait(pe, (l, "qk", {CQ: 0, CQ + 1: 1, CK: 2}[c]))
                    mm = pe.matmul(bank[b][:, 0:LAT], const("rot"), chunk(c)[:, 0:LAT], start=True, stop=True)
                    prep_done.done(mm, (l, "rope", i))
                for i, c in enumerate((AK, CK)):
                    prepared.wait(pe, (l, "rope", 2 if c == AK else 5))
                    projected.wait(pe, (l, IN_CHUNKS - 1))
                    mm = pe.matmul(bank[i][:, :], const("swap"), chunk(c), start=True, stop=True)
                    prep_done.done(mm, (l, "swap", i))

                tasks = attention_tasks(last_layer)
                n_tasks = len(tasks)

                def mix(job):
                    br, h, st, _ = tasks[2 * job]
                    if job >= 2:
                        y_stored.wait(pe, (l, job - 2))
                    turned_copied.wait(pe, (l, 2 * job + 1))
                    row = HD * (h % 2)
                    v0 = value_column(br, h)
                    tiles = range(4) if st == 0 else range(2, 4)
                    for t in tiles:
                        mm = pe.matmul(bank[4 + job % 2][row:row + HD, 0:LAT], v_tok[:, t, v0:v0 + HD], probs_t[:, t, :],
                                       start=(t == tiles[0]), stop=(t == tiles[-1]))
                    mixed.done(mm, (l, job))

                for t in range(n_tasks + 2):
                    if t < n_tasks:
                        br, h, st, qt = tasks[t]
                        if t == 0:
                            act_prepared.wait(pe, (l, "swap", 1))
                            prep_read.wait(pe, (l, "rope", 5))
                            prepared.wait(pe, (l, "dt"))
                        if t >= 2:
                            exped.wait(pe, (l, t - 2))
                        row = HD * (h % 2)
                        q = chunk((AQ, BQ, CQ)[br] + h // 2)[row:row + HD, st * LAT + qt * P:st * LAT + (qt + 1) * P]
                        if br == 1:
                            k = chunk(BK + h // 2)
                        elif h // 2 == h % 2:
                            k = chunk((AK, None, CK)[br])
                        else:
                            k = k_swap[:, br // 2]
                        keys = slice(0, TOK) if st == 0 else slice(LAT, TOK)
                        mm = pe.matmul(bank[t % 2][:, 0:TOK - keys.start], q, k[row:row + HD, keys], start=True, stop=True)
                        scored.done(mm, (l, t))
                    if t >= 3 and t % 2 == 1:
                        mix((t - 3) // 2)
                    if 1 <= t <= n_tasks:
                        s = t - 1
                        if s >= 2:
                            turned_copied.wait(pe, (l, s - 2))
                        normalised.wait(pe, (l, s))
                        _, _, st, _ = tasks[s]
                        for kt in range(4 if st == 0 else 2):
                            mm = pe.transpose(bank[2 + s % 2][:, kt * P:(kt + 1) * P], probs[:, s % 2, kt * P:(kt + 1) * P], const("ident"))
                        turned.done(mm, (l, s))

                for g in range(2):
                    conv_out.wait(pe, (l, g))
                    if g == 0:
                        turned_copied.wait(pe, (l, n_tasks - 1))
                        y_stored.wait(pe, (l, n_tasks // 2 - 1))
                    for t in range(4):
                        mm = pe.transpose(bank[g][:, t * P:(t + 1) * P], chunk(XS + g)[:, t * P:(t + 1) * P], const("ident"))
                    prep_done.done(mm, (l, "x", g))
                prepared.wait(pe, (l, "dt"))
                for t in range(4):
                    pe.transpose(bank[2][:, t * 16:t * 16 + 8], dt_t[:, t * P:(t + 1) * P], const("ident")[0:8, 0:8])
                    mm = pe.transpose(bank[2][:, t * 16 + 8:t * 16 + 16], da_t[:, t * P:(t + 1) * P], const("ident")[0:8, 0:8])
                prep_done.done(mm, (l, "tok"))
                prepared.wait(pe, (l, "tok"))
                for st in range(2):
                    n_mm = 0
                    for j in range(2):
                        for src, tri in ((tokf, "trif"), (tokb, "trib")):
                            strip = const(tri)[:, P - j * P:P - j * P + LAT]
                            mm = pe.matmul(bank[3][0:8, st * LAT:(st + 1) * LAT], src[:, 2 * st + j, :], strip,
                                           start=(n_mm == 0), stop=(n_mm == 3))
                            n_mm += 1
                prep_done.done(mm, (l, "cum"))
                for j in range(2):
                    mm = pe.matmul(bank[4][:, 0:8], const("ones"), tok[:, 2 + j, 8:16], start=(j == 0), stop=(j == 1))
                prep_done.done(mm, (l, "tot"))
                prepared.wait(pe, (l, "cum"))
                for t in range(4):
                    mm = pe.transpose(bank[5][:, t * 8:t * 8 + 8], dt_t[:, t * P:(t + 1) * P], const("ident")[0:8, 0:8])
                prep_done.done(mm, (l, "cumtok"))

                n = tokens(l, "q")
                prepared.wait(pe, (l, "x", 1))
                prepared.wait(pe, (l, "cumtok"))
                conv_out.wait(pe, (l, 5))
                for g in range(2):
                    if g == 1:
                        weighed.wait(pe, (l, 1, 1))
                    for i, s in enumerate((2, 3)):
                        pe.matmul(bank[i][:, 0:n], chunk(SB_ + g)[:, s * P:(s + 1) * P], chunk(SC_ + g)[:, 0:n], start=True, stop=True)
                    for s in range(2):
                        mm = pe.matmul(bank[2][:, s * LAT:(s + 1) * LAT], chunk(SB_ + g)[:, s * P:(s + 1) * P],
                                       chunk(SC_ + g)[:, 0:LAT], start=True, stop=True)
                    cb_done.done(mm, (l, g))
                    for hh in range(2):
                        h = 2 * g + hh
                        if h > 0:
                            spread.wait(pe, (l, h - 1))
                        for r in range(2):
                            mm = pe.matmul(bank[3 + r][:, :], const("sel")[0:8, (4 * r + h) * P:(4 * r + h + 1) * P], dt_t[:, :],
                                           start=True, stop=True)
                        cum_spread.done(mm, (l, h))
                        if h == 2:
                            ssm_read.wait(pe, (l, "y", 0))
                        row = HD * hh
                        for i, s in enumerate((2, 3, 0, 1)):
                            nn = n if s >= 2 else LAT
                            weighed.wait(pe, (l, h, s))
                            mm = pe.matmul(bank[5][row:row + HD, 0:nn], x_tok[:, s, h * HD:(h + 1) * HD], weighed_flat[:, (i % 2) * TOK:(i % 2) * TOK + nn],
                                           start=(i == 0), stop=(i == 3))
                            ssm_done.done(mm, (l, h, s))
                for g in range(2):
                    squares.wait(pe, (l, "ssm", g))
                    mm = pe.matmul(bank[6][:, 0:n], const("ones"), wa[:, g, 0:n], start=(g == 0), stop=(g == 1))
                prep_done.done(mm, (l, "ssm"))

                u0 = first["merge", l]
                g0 = l * 4 * DC

                def merge_turn(d):
                    straight = isinstance(d, int)
                    for k in range(4):
                        if not (straight and d == 0):
                            pe.wait_ge(gated, d * 4 + (g0 + k - 3))
                        u, ii, per = at(u0, k, d)
                        if straight and d == 0 and k == 0:
                            y_made.wait(pe, (l, 7))
                        product(u, ii, per, bank[4 + k][:, 0:n], 2, lambda c: (y_hi[:, 2 * k + c, 0:n], y_lo[:, 2 * k + c, 0:n]),
                                row0=DC, signal_it=False)
                        product(u, ii, per, bank[k][:, 0:n], DC, h_rhs(n))
                turns(pe, DC, merge_turn)

                u0, a0 = first["out", l], add_first[l, "out"]
                for d in range(DC):
                    pe.wait_ge(added, a0 + d - 1)
                    if d == 0:
                        pe.wait_ge(gated, g0 + 4 * DC)
                    product(u0 + d, 0, (0, 0), bank[4 + d % 2][:, 0:n], DC, h_rhs(n),
                            (lambda k: h_made.wait(pe, (l, "merged", k))) if d == 0 else None)

                n = tokens(l, "ffn2")
                sum_squares((l, 2), n)
                for part in range(len(PARTS)):
                    up(l, 2, part, n)
                    down(l, 2, part, n)

            sum_squares(("final", 0), LAT)
            for t in range(2):
                for half in range(2):
                    for k in range(4 * half, 4 * half + 4):
                        if t == 0:
                            normed.wait(pe, ("final", k))
                        mm = pe.transpose(bank[2 * t + half][:, (k % 4) * P:(k % 4 + 1) * P], X[:, k, t * P:(t + 1) * P], const("ident"))
                    pe_start.done(mm, ("out", t, half))

        @block.scalar
        def _(act):
            def squares_of(key, n, source):
                for k in range(DC):
                    source(k)
                    if k >= 2:
                        sums.wait(act, (key, k - 2))
                    squares.done(act.activation(wa[:, k % 2, 0:n], X[:, k, 0:n], ACT.Square), (key, k))

            def root(key, psum_signal, step, psum, dst, scale):
                psum_signal.wait(act, step)
                roots.done(act.activation(dst, psum, ACT.Sqrt, bias=eps_col[0:psum.shape[0], 0:1], scale=scale), key)

            def norm_block(l, which, n, a_last, mod_i):
                def ready(k):
                    if a_last is None:
                        if k == 0:
                            start_copied.wait(act, ("x", DC - 1))
                    else:
                        act.wait_ge(added, a_last + k + 1)
                squares_of((l, which), n, ready)
                root((l, which), sums, ((l, which), DC - 1), bank[6][:, 0:n], rstd[:, 0:n], 1.0 / D)
                vectors.wait(act, (l, min(mod_i, 1)))
                for k in range(DC):
                    normed.wait(act, (l, which, k))
                    if k >= 2:
                        h_made.wait(act, (l, which, k - 2))
                    for st in streams(n):
                        cols = slice(st * LAT, (st + 1) * LAT)
                        ins = act.activation(wb[:, k % 2, cols], wa[:, k % 2, cols], ACT.Identity,
                                             bias=mod[:, 3 * mod_i * DC + k, st:st + 1],
                                             scale=gain[:, mod_i, k, st:st + 1])
                        modulated.done(ins, (l, which, k))
                    modulated.wait(act, (l, which, k))
                    h_hi_made.done(act.activation(h_hi[:, k, 0:n], wb[:, k % 2, 0:n], ACT.Copy), (l, which, k))

            def up(l, ffn, part, n):
                u0, c0 = first["up", l, ffn, part], inner_first[l, ffn, part]
                n0 = units[u0].product

                step = step_of(l, ffn, part)

                def body(i):
                    straight = isinstance(i, int)
                    for j in range(4):
                        _, ii, per = at(u0, j, i, step)
                        c = c0 + j // 2
                        if j % 2 == 0:
                            act.wait_ge(unit_done, u0 + step * (j + 1) + i * (4 * step))
                            if not (straight and c + 2 * i < 2):
                                act.wait_ge(inner_made, i * 2 + (c - 1))
                            act.activation(wa[:, (j // 2) % 2, 0:n], bank[j][:, 0:n], ACT.Silu).then_inc(silu_done, 1)
                        split_hi(act, n0 + j + 2 + (4 * i if straight else 0), ii, per)
                        if j % 2 == 1:
                            act.wait_ge(inner_made, i * 2 + (c + 1))
                            act.activation(inner_hi[:, bass.ds(i * 2 + j // 2, 1), 0:n], wb[:, (j // 2) % 2:(j // 2) % 2 + 1, 0:n],
                                           ACT.Copy).then_inc(inner_hi_made, 1)
                    if step == 2:
                        copy_modulation(u0 + 7 + i * 8, i + mod_first[l, ffn, part])
                turns(act, PARTS[part][1] // 2, body)

            def copy_modulation(done, m):
                act.wait_ge(unit_done, done)
                if not (isinstance(m, int) and m == 0):
                    act.wait_ge(mod_stored, m * 32)
                act.activation(mod_row[:, :], bank[7][:, :], ACT.Copy).then_inc(mod_copied, 1)

            def plain_splits(u0, count):
                for j in range(count):
                    split_hi(act, units[u0].product + j + 2)

            cleared.wait(act, "all")
            pe_start.wait(act, "packs")
            act_link(act, act.activation(vec1[:, :, :], bank[0][:, 0:2 * P].rearrange("p (l r) -> p l r", l=LAYERS), ACT.Copy))
            start_copied.done(act.activation(vec2[:, :, :], bank[0][:, 256:256 + 2 * PACK2].rearrange("p (l r) -> p l r", l=LAYERS),
                                             ACT.Copy), "packs")
            start_copied.wait(act, "packs")
            cleared.wait(act, "all")
            act_link(act, act.activation(cact[:, :, 0], vec2[:, 0, V_C:V_C + DC], ACT.Silu))
            cond_ready.done(act.activation(cact[:, :, 1], vec2[:, 0, V_CC:V_CC + DC], ACT.Silu), "c")
            for k in range(DC):
                pe_start.wait(act, ("x", k))
                start_copied.done(act.activation(X[:, k, :], bank[1 + k % 3][:, :], ACT.Copy), ("x", k))

            for l in range(LAYERS):
                last_layer = l == LAYERS - 1
                if l == 0:
                    turns(act, MOD_FIRST // 4, lambda i: copy_modulation(first["mod"] + 4 + i * 4, i))
                    for s in range(2):
                        split_hi(act, s)
                norm_block(l, 1, TOK, None if l == 0 else add_first[l - 1, (2, 2)], 0)
                for part in range(len(PARTS)):
                    up(l, 1, part, TOK)
                    plain_splits(first["down", l, 1, part], DC)

                norm_block(l, "mix", TOK, add_first[l, (1, 2)], 1)
                layer_loads.wait(act, l)
                act_prepared.done(act.activation(wdt_hi[:, :, :], wdt_raw[:, :, :], ACT.Copy), (l, "wdt_hi"))
                u0 = first["in", l]
                for c in range(IN_CHUNKS):
                    n = tokens(l, "q") if c in QCHUNKS or c >= SC_ else TOK
                    act.wait_ge(unit_done, u0 + c + 1)
                    projected.done(act.activation(chunk(c)[:, 0:n], bank[c % 4][:, 0:n], ACT.Copy), (l, c))
                    split_hi(act, units[u0 + c].product + 2)

                prep_done.wait(act, (l, "dt"))
                act_link(act, act.activation(wb[0:8, 0, :], bank[4][0:8, :], ACT.Identity, bias=dtv[:, 0:1]))
                act_link(act, act.activation(dt_t[:, :], wb[0:8, 0, :], ACT.Abs))
                act_link(act, act.activation(dt_t[:, :], dt_t[:, :], ACT.Exp, scale=-1.0))
                act_link(act, act.activation(dtv[:, 2:3], dtv[:, 1:2], ACT.Exp))
                soft.done(act.activation(da_t[:, :], dt_t[:, :], ACT.Ln, bias=const("ones")[0:8, 0:1]), (l, "dt"))

                for i, c in enumerate((CQ, CQ + 1, CK)):
                    n = TOK if c == CK else tokens(l, "q")
                    projected.wait(act, (l, c))
                    if i >= 2:
                        prep_done.wait(act, (l, "qk", i - 2))
                    squares.done(act.activation(wa[:, i % 2, 0:n], chunk(c)[:, 0:n], ACT.Square), (l, "qk", i))
                for i, c in enumerate((CQ, CQ + 1, CK)):
                    n = TOK if c == CK else tokens(l, "q")
                    prep_done.wait(act, (l, "qk", i))
                    if i >= 1:
                        prepared.wait(act, (l, "qk", i - 1))
                    act_read.done(act.activation(rstd[:, 0:n], bank[5][:, 0:n], ACT.Sqrt, bias=eps_col[:, 0:1], scale=1.0 / HD), (l, "qk", i))
                for i in range(2):
                    prep_done.wait(act, (l, "swap", i))
                    act_prepared.done(act.activation(k_swap[:, i, :], bank[i][:, :], ACT.Copy), (l, "swap", i))

                n = tokens(l, "q")
                for i in range(6):
                    nn = n if i >= 4 else TOK
                    projected.wait(act, (l, XS + i))
                    dst = padded[i % 2][:, 0:nn // LAT, 2:2 + LAT]
                    if i >= 2:
                        convolved.wait(act, (l, i - 2))
                    else:
                        pads_cleared.wait(act, l)
                    conv_in.done(act.activation(dst, chunk(XS + i)[:, 0:nn].rearrange("p (s t) -> p s t", t=LAT), ACT.Copy), (l, i))
                    if i >= 1:
                        j = i - 1
                        m = n if j >= 4 else TOK
                        convolved.wait(act, (l, j))
                        conv_out.done(act.activation(chunk(XS + j)[:, 0:m], wb[:, j % 2, 0:m], ACT.Silu, bias=vec2[:, l, V_CONVB + j:V_CONVB + j + 1]), (l, j))
                convolved.wait(act, (l, 5))
                conv_out.done(act.activation(chunk(XS + 5)[:, 0:n], wb[:, 1, 0:n], ACT.Silu, bias=vec2[:, l, V_CONVB + 5:V_CONVB + 6]), (l, 5))
                for g in range(2):
                    z_done.done(act.activation(chunk(Z + g)[:, 0:n], chunk(Z + g)[:, 0:n], ACT.Silu), (l, g))

                tasks = attention_tasks(last_layer)
                n_tasks = len(tasks)

                def store_y(job):
                    br, h, st, _ = tasks[2 * job]
                    row = HD * (h % 2)
                    mixed.wait(act, (l, job))
                    y_stored.done(act.activation(chunk((AQ, BQ, CQ)[br] + h // 2)[row:row + HD, st * LAT:(st + 1) * LAT],
                                                 bank[4 + job % 2][row:row + HD, 0:LAT], ACT.Copy), (l, job))

                for t in range(n_tasks + 2):
                    if t < n_tasks:
                        br, h, st, qt = tasks[t]
                        s = t % 2
                        scored.wait(act, (l, t))
                        if br < 2 and st == 0:
                            masked.wait(act, (l, t))
                            ctx_copied.done(act.activation(scores[:, s, LAT:TOK], bank[s][:, LAT:TOK], ACT.Copy), (l, t))
                        nk = TOK if st == 0 else CTX
                        src = scores[:, s, 0:nk] if br < 2 and st == 0 else bank[s][:, 0:nk]
                        bounded.wait(act, (l, t))
                        ins = act.activation(probs[:, s, 0:nk], src, ACT.Exp, bias=smax[:, s, 1:2], scale=SCALE, accum_out=smax[:, s, 2:3])
                        if br == 0:
                            sunk.done(act.activation(smax[:, s, 3:4], sink8[:, h:h + 1], ACT.Exp, bias=smax[:, s, 1:2], scale=SCALE), (l, t))
                        exped.done(ins, (l, t))
                    if 1 <= t <= n_tasks:
                        s = t - 1
                        _, _, st, qt = tasks[s]
                        turned.wait(act, (l, s))
                        if s >= 2:
                            mixed.wait(act, (l, s // 2 - 1))
                        k0 = 0 if st == 0 else 2
                        turned_copied.done(act.activation(probs_t[:, k0:4, qt * P:(qt + 1) * P],
                                                          bank[2 + s % 2][:, 0:(4 - k0) * P].rearrange("p (k q) -> p k q", q=P), ACT.Copy), (l, s))
                    if t >= 3 and t % 2 == 1:
                        store_y((t - 3) // 2)

                for h in range(4):
                    cum_spread.wait(act, (l, h))
                    if h > 0:
                        decay_arg.wait(act, (l, h - 1, 1, 1))
                    if h == 2:
                        skipped.wait(act, (l, 0))
                    for r in range(2):
                        spread.done(act.activation(wa[:, r, :], bank[3 + r][:, :], ACT.Copy), (l, h))
                    spread.wait(act, (l, h))
                    for i, s in enumerate((2, 3, 0, 1)):
                        st, j = s // 2, s % 2
                        step = 4 * h + i
                        if step >= 2:
                            prev = (h, (2, 3, 0, 1)[i - 2]) if i >= 2 else (h - 1, (2, 3, 0, 1)[i + 2])
                            weighed.wait(act, (l, *prev))
                        for r, dst in enumerate((scores, probs)):
                            col = 4 * r + h
                            if not (last_layer and st == 1):
                                decay_arg.wait(act, (l, h, s, r))
                                decayed.done(act.activation(dst[:, i % 2, st * LAT:(st + 1) * LAT], wb[:, r, (i % 2) * LAT:(i % 2 + 1) * LAT], ACT.Exp), (l, h, s, r, "own"))
                            if st == 1:
                                decayed.done(act.activation(dst[:, i % 2, 0:LAT], wa[:, r, 0:LAT], ACT.Exp, bias=tct[:, j, col:col + 1]), (l, h, s, r, "ctx"))
                        decayed.mark((l, h, s))

                for g in range(2):
                    skipped.wait(act, (l, g))
                    squares.done(act.activation(wa[:, g, 0:n], chunk(Z + g)[:, 0:n], ACT.Square), (l, "ssm", g))
                root((l, "ssm"), prep_done, (l, "ssm"), bank[6][:, 0:n], rstd[:, 0:n], 1.0 / 256)

                for b, c in enumerate(QCHUNKS):
                    ssm_out.wait(act, (l, 1))
                    y_stored.wait(act, (l, n_tasks // 2 - 1))
                    y_hi_made.done(act.activation(y_hi[:, b, 0:n], chunk(c)[:, 0:n], ACT.Copy), (l, b))

                u0 = first["merge", l]
                n0, g0 = units[u0].product, l * 4 * DC

                def merge_turn(d):
                    straight = isinstance(d, int)
                    for k in range(4):
                        _, ii, per = at(u0, k, d)
                        act.wait_ge(unit_done, u0 + k + 1 + d * 4)
                        if not (straight and d == 0 and k < 2):
                            act.wait_ge(gated, d * 4 + (g0 + k - 1))
                        act.activation(wa[:, k % 2, 0:n], bank[k][:, 0:n], ACT.Sigmoid,
                                       bias=vec1[:, l, bass.ds(d + (V_BGATE + k * DC), 1)]).then_inc(gate_done, 1)
                        split_hi(act, n0 + k + 2 + (4 * d if straight else 0), ii, per)
                turns(act, DC, merge_turn)

                for k in range(DC):
                    act.wait_ge(branch_added, 3 * (l * DC + k + 1))
                    if k == 0:
                        act.wait_ge(unit_done, first["out", l])
                    h_hi_made.done(act.activation(h_hi[:, k, 0:n], Q[:, k, 0:n], ACT.Copy), (l, "merged", k))
                plain_splits(first["out", l], DC)

                n = tokens(l, "ffn2")
                norm_block(l, 2, n, add_first[l, "out"], 2)
                for part in range(len(PARTS)):
                    up(l, 2, part, n)
                    plain_splits(first["down", l, 2, part], DC)

            a_last = add_first[LAYERS - 1, (2, 2)]
            squares_of(("final", 0), LAT, lambda k: act.wait_ge(added, a_last + k + 1))
            root("final", sums, (("final", 0), DC - 1), bank[6][:, 0:LAT], rstd[:, 0:LAT], 1.0 / D)
            for t in range(2):
                for half in range(2):
                    pe_start.wait(act, ("out", t, half))
                    ins = act.activation(out_rows[:, t, half * 512:(half + 1) * 512], bank[2 * t + half][:, :], ACT.Copy)
                    start_copied.done(ins, ("out", t))

        @block.vector
        def _(dve):
            def link(ins):
                dve_link(dve, ins)

            def split_h(key, n, source, k):
                h_hi_made.wait(dve, (*key, k))
                h_made.done(dve.tensor_tensor(h_lo[:, k, 0:n], source, h_hi[:, k, 0:n].bitcast(F32), ALU.subtract), (*key, k))

            def norm_block(l, which, n):
                key = (l, which)
                roots.wait(dve, key)
                link(dve.reciprocal(rstd[:, 0:n], rstd[:, 0:n]))
                for k in range(DC + 1):
                    if k < DC:
                        if k >= 2:
                            modulated.wait(dve, (l, which, k - 2))
                        normed.done(dve.tensor_tensor(wa[:, k % 2, 0:n], X[:, k, 0:n], rstd[:, 0:n], ALU.mult), (l, which, k))
                    if k >= 1:
                        split_h(key, n, wb[:, (k - 1) % 2, 0:n], k - 1)

            def up(l, ffn, part, n):
                u0, c0 = first["up", l, ffn, part], inner_first[l, ffn, part]
                n0 = units[u0].product

                step = step_of(l, ffn, part)

                def body(i):
                    straight = isinstance(i, int)
                    for j in range(4):
                        _, ii, per = at(u0, j, i, step)
                        c = c0 + j // 2
                        b = (j // 2) % 2
                        if j % 2 == 1:
                            dve.wait_ge(unit_done, u0 + step * (j + 1) + i * (4 * step))
                            dve.wait_ge(silu_done, i * 2 + (c + 1))
                            if not (straight and c + 2 * i < 2):
                                dve.wait_ge(inner_lo_made, i * 2 + (c - 1))
                            dve.tensor_tensor(wb[:, b, 0:n], bank[j][:, 0:n], wa[:, b, 0:n], ALU.mult).then_inc(inner_made, 1)
                        split_lo(dve, n0 + j + 2 + (4 * i if straight else 0), ii, per)
                        if j % 2 == 1:
                            dve.wait_ge(inner_hi_made, i * 2 + (c + 1))
                            at_chunk = bass.ds(i * 2 + j // 2, 1)
                            dve.tensor_tensor(inner_lo[:, at_chunk, 0:n], wb[:, b:b + 1, 0:n],
                                              inner_hi[:, at_chunk, 0:n].bitcast(F32), ALU.subtract).then_inc(inner_lo_made, 1)
                turns(dve, PARTS[part][1] // 2, body)

            def add_block(l, name, u0, n, gate_i):
                for d in range(DC):
                    dve.wait_ge(unit_done, u0 + d + 1)
                    for st in streams(n):
                        cols = slice(st * LAT, (st + 1) * LAT)
                        ins = dve.scalar_tensor_tensor(out=X[:, d, cols], in0=bank[4 + d % 2][:, cols], scalar=gatev[:, gate_i, d, st:st + 1],
                                                       in1=X[:, d, cols], op0=ALU.mult, op1=ALU.add)
                    ins.then_inc(added, 1)
                    split_lo(dve, units[u0 + d].product + 2)

            def modulation_vectors(l, half):
                start_copied.wait(dve, "packs")
                mod_turned.wait(dve, (l, half))
                if l > 0 and half == 0:
                    dve.wait_ge(added, add_first[l - 1, (2, 2)] + DC)
                r0, r1 = ((0, MOD_EARLY), (MOD_EARLY, MOD_CHUNKS))[half]
                for s in range(2):
                    link(dve.tensor_tensor(mod[:, r0:r1, s], bank[7][:, s * MOD_CHUNKS + r0:s * MOD_CHUNKS + r1],
                                           vec1[:, l, V_BMOD + r0:V_BMOD + r1], ALU.add))
                for i in ((0,), (1, 2))[half]:
                    for s in range(2):
                        link(dve.scalar_tensor_tensor(out=gain[:, i, :, s], in0=mod[:, (3 * i + 1) * DC:(3 * i + 2) * DC, s], scalar=1.0,
                                                      in1=vec1[:, l, V_NORM + i * DC:V_NORM + (i + 1) * DC], op0=ALU.add, op1=ALU.mult))
                    ins = dve.tensor_scalar(gatev[:, i, :, :], mod[:, (3 * i + 2) * DC:(3 * i + 3) * DC, :],
                                            1.0 if i == 1 else 0.5, None, ALU.mult)
                vectors.done(ins, (l, half))
                vectors.wait(dve, (l, half))

            start_loads.wait(dve, "all")
            for l in range(LAYERS):
                for g in range(2):
                    for half in range(2):
                        rows = slice(half * HD, (half + 1) * HD)
                        head = 4 * l + 2 * g + half
                        ins = dve.tensor_copy(skip_w[rows, l, g:g + 1], skip_all[rows, head:head + 1])
            link(ins)
            for l in range(LAYERS):
                last_layer = l == LAYERS - 1
                nq = tokens(l, "q")
                if l == 0:
                    for s in range(2):
                        split_lo(dve, s)
                modulation_vectors(l, 0)

                norm_block(l, 1, TOK)
                for part in range(len(PARTS)):
                    up(l, 1, part, TOK)
                    add_block(l, (1, part), first["down", l, 1, part], TOK, 0)

                modulation_vectors(l, 1)
                norm_block(l, "mix", TOK)
                act_prepared.wait(dve, (l, "wdt_hi"))
                prepared.done(dve.tensor_tensor(wdt_lo[:, :, :], wdt_raw[:, :, :], wdt_hi[:, :, :].bitcast(F32), ALU.subtract), (l, "wdt"))
                u0 = first["in", l]
                for c in range(IN_CHUNKS):
                    split_lo(dve, units[u0 + c].product + 2)

                bias_loads.wait(dve, l)
                for h in range(4):
                    for t in range(2):
                        link(dve.tensor_tensor(nbias[:, h, t, :], nbias[:, h, t, :], const("nvalid"), ALU.mult))
                        link(dve.tensor_tensor(nbias[:, h, t, :], nbias[:, h, t, :], const("nneg"), ALU.add))
                layer_loads.wait(dve, l)
                link(dve.tensor_scalar(sink8[:, :], sink8[:, :], BIG, None, ALU.mult))

                soft.wait(dve, (l, "dt"))
                link(dve.scalar_tensor_tensor(out=dt_t[:, :], in0=wb[0:8, 0, :], scalar=0.0, in1=da_t[:, :], op0=ALU.max, op1=ALU.add))
                prepared.done(dve.tensor_scalar(da_t[:, :], dt_t[:, :], dtv[:, 2:3], -1.0, ALU.mult, ALU.mult), (l, "dt"))

                for v in range(4):
                    prep_done.wait(dve, (l, "v", v))
                    prep_read.done(dve.tensor_copy(v_tok[:, :, v * P:(v + 1) * P], bank[5 + v % 2][:, :].rearrange("p (t f) -> p t f", t=4)), (l, "v", v))
                for i, c in enumerate((CQ, CQ + 1, CK)):
                    n = TOK if c == CK else nq
                    act_read.wait(dve, (l, "qk", i))
                    link(dve.reciprocal(rstd[:, 0:n], rstd[:, 0:n]))
                    g = V_KG if c == CK else V_QG
                    prepared.done(dve.scalar_tensor_tensor(out=chunk(c)[:, 0:n], in0=chunk(c)[:, 0:n], scalar=vec2[:, l, g:g + 1],
                                                           in1=rstd[:, 0:n], op0=ALU.mult, op1=ALU.mult), (l, "qk", i))
                for i, c in enumerate((AQ, AQ + 1, AK, CQ, CQ + 1, CK)):
                    prep_done.wait(dve, (l, "rope", i))
                    if i == 0:
                        prepared.wait(dve, (l, "qk", 2))
                    lat = chunk(c)[:, 0:LAT]
                    ins = dve.tensor_tensor(rstd[:, 0:LAT], bank[6 + i % 2][:, 0:LAT], const("ropes"), ALU.mult)
                    prep_read.done(ins, (l, "rope", i))
                    link(dve.tensor_tensor(lat, lat, const("ropec"), ALU.mult))
                    prep_read.wait(dve, (l, "rope", i))
                    ins = dve.tensor_tensor(lat, lat, rstd[:, 0:LAT], ALU.add)
                    prepared.done(ins, (l, "rope", i))
                    prepared.wait(dve, (l, "rope", i))

                for i in range(2):
                    ins = dve.memset(padded[i][:, :, 0:2], 0.0)
                    ins = dve.memset(padded[i][:, :, 2 + LAT:4 + LAT], 0.0)
                pads_cleared.done(ins, l)
                for i in range(6):
                    nn = nq if i >= 4 else TOK
                    ns = nn // LAT
                    conv_in.wait(dve, (l, i))
                    if i >= 2:
                        conv_out.wait(dve, (l, i - 2))
                    acc = wb[:, i % 2, 0:nn].rearrange("p (s t) -> p s t", t=LAT)
                    for j in range(CONV):
                        src = padded[i % 2][:, 0:ns, j:j + LAT]
                        w = vec2[:, l, V_CONVW + 6 * j + i:V_CONVW + 6 * j + i + 1]
                        if j == 0:
                            ins = dve.tensor_scalar(acc, src, w, None, ALU.mult)
                        else:
                            ins = dve.scalar_tensor_tensor(out=acc, in0=src, scalar=w, in1=acc, op0=ALU.mult, op1=ALU.add)
                        if j < CONV - 1:
                            link(ins)
                    convolved.done(ins, (l, i))
                convolved.wait(dve, (l, 5))

                tasks = attention_tasks(last_layer)
                n_tasks = len(tasks)
                for t in range(n_tasks + 1):
                    if t < n_tasks:
                        br, h, st, qt = tasks[t]
                        s = t % 2
                        scored.wait(dve, (l, t))
                        nk = TOK if st == 0 else CTX
                        src = bank[s][:, 0:nk]
                        if br < 2 and st == 0:
                            mask = const("wmask")[:, qt * LAT:(qt + 1) * LAT] if br == 0 else nbias[:, h, qt, :]
                            masked.done(dve.tensor_tensor(scores[:, s, 0:LAT], bank[s][:, 0:LAT], mask, ALU.add), (l, t))
                            masked.wait(dve, (l, t))
                            ctx_copied.wait(dve, (l, t))
                            src = scores[:, s, :]
                        link(dve.reduce_max(smax[:, s, 0:1], src, AX_X))
                        if br == 0:
                            link(dve.tensor_tensor(smax[:, s, 0:1], smax[:, s, 0:1], sink8[:, h:h + 1], ALU.max))
                        bounded.done(dve.tensor_scalar(smax[:, s, 1:2], smax[:, s, 0:1], -SCALE, None, ALU.mult), (l, t))
                    if t >= 1:
                        br, h, st, qt = tasks[t - 1]
                        s = (t - 1) % 2
                        nk = TOK if st == 0 else CTX
                        exped.wait(dve, (l, t - 1))
                        if br == 0:
                            sunk.wait(dve, (l, t - 1))
                            link(dve.tensor_tensor(smax[:, s, 2:3], smax[:, s, 2:3], smax[:, s, 3:4], ALU.add))
                        link(dve.reciprocal(smax[:, s, 2:3], smax[:, s, 2:3]))
                        normalised.done(dve.tensor_scalar(probs[:, s, 0:nk], probs[:, s, 0:nk], smax[:, s, 2:3], None, ALU.mult), (l, t - 1))

                for g in range(2):
                    prep_done.wait(dve, (l, "x", g))
                    prepared.done(dve.tensor_copy(x_tok[:, :, g * P:(g + 1) * P], bank[g][:, :].rearrange("p (t f) -> p t f", t=4)), (l, "x", g))
                prep_done.wait(dve, (l, "tok"))
                link(dve.tensor_copy(tok[:, :, :], bank[2][:, 0:64].rearrange("p (t r) -> p t r", t=4)))
                dve.tensor_copy(tokf[:, :, 0:4], tok[:, :, 8:12])
                prepared.done(dve.tensor_copy(tokb[:, :, 4:8], tok[:, :, 12:16]), (l, "tok"))
                prep_done.wait(dve, (l, "cum"))
                prepared.done(dve.tensor_copy(dt_t[:, :], bank[3][0:8, :]), (l, "cum"))
                prep_done.wait(dve, (l, "tot"))
                link(dve.tensor_copy(tot[:, :], bank[4][:, 0:8]))
                prep_done.wait(dve, (l, "cumtok"))
                link(dve.tensor_scalar(nct[:, :, :], bank[5][:, 0:32].rearrange("p (t r) -> p t r", t=4), -1.0, None, ALU.mult))
                for j in range(2):
                    ins = dve.tensor_tensor(tct[:, j, :], tot[:, :], nct[:, 2 + j, :], ALU.add)
                prepared.done(ins, (l, "cumtok"))

                order = (2, 3, 0, 1)
                steps = [(h, i) for h in range(4) for i in range(4)]

                def exponents(h, i):
                    s = order[i]
                    st, j = s // 2, s % 2
                    if last_layer and st == 1:
                        return
                    for r, mask in enumerate(("maskf", "maskb")):
                        strip = const(mask)[:, P - j * P:P - j * P + LAT]
                        col = 4 * r + h
                        decay_arg.done(dve.scalar_tensor_tensor(
                            out=wb[:, r, (i % 2) * LAT:(i % 2 + 1) * LAT], in0=wa[:, r, st * LAT:(st + 1) * LAT],
                            scalar=nct[:, s, col:col + 1], in1=strip, op0=ALU.add, op1=ALU.add), (l, h, s, r))

                def weigh(h, i):
                    s = order[i]
                    g = h // 2
                    n = nq if s >= 2 else LAT
                    step = 4 * h + i
                    decayed.wait(dve, (l, h, s))
                    if step >= 2:
                        ph, pi = steps[step - 2]
                        ssm_done.wait(dve, (l, ph, order[pi]))
                    if i == 0:
                        cb_done.wait(dve, (l, g))
                    f, b = scores[:, i % 2, 0:n], probs[:, i % 2, 0:n]
                    link(dve.tensor_scalar(b, b, tok[:, s, 4 + h:5 + h], None, ALU.mult))
                    link(dve.scalar_tensor_tensor(out=f, in0=f, scalar=tok[:, s, h:h + 1], in1=b, op0=ALU.mult, op1=ALU.add))
                    cb = bank[s - 2][:, 0:n] if s >= 2 else bank[2][:, s * LAT:(s + 1) * LAT]
                    weighed.done(dve.tensor_tensor(weighed_flat[:, (i % 2) * TOK:(i % 2) * TOK + n], f, cb, ALU.mult), (l, h, s))

                for h in range(4):
                    spread.wait(dve, (l, h))
                    for i in range(4):
                        if i == 0:
                            exponents(h, 0)
                        if i + 1 < 4:
                            if i + 1 >= 2:
                                decayed.wait(dve, (l, h, order[i - 1]))
                            exponents(h, i + 1)
                        weigh(h, i)
                    if h % 2 == 1:
                        g = h // 2
                        ssm_done.wait(dve, (l, h, 1))
                        ssm_read.done(dve.scalar_tensor_tensor(out=wa[:, g, 0:nq], in0=chunk(XS + g)[:, 0:nq], scalar=skip_w[:, l, g:g + 1],
                                                               in1=bank[5][:, 0:nq], op0=ALU.mult, op1=ALU.add), (l, "y", g))
                        ssm_read.wait(dve, (l, "y", g))
                        z_done.wait(dve, (l, g))
                        skipped.done(dve.tensor_tensor(chunk(Z + g)[:, 0:nq], wa[:, g, 0:nq], chunk(Z + g)[:, 0:nq], ALU.mult), (l, g))
                roots.wait(dve, (l, "ssm"))
                link(dve.reciprocal(rstd[:, 0:nq], rstd[:, 0:nq]))
                for g in range(2):
                    ssm_out.done(dve.scalar_tensor_tensor(out=chunk(Z + g)[:, 0:nq], in0=chunk(Z + g)[:, 0:nq], scalar=vec2[:, l, V_SNORM + g:V_SNORM + g + 1],
                                                          in1=rstd[:, 0:nq], op0=ALU.mult, op1=ALU.mult), (l, g))
                for b, c in enumerate(QCHUNKS):
                    y_hi_made.wait(dve, (l, b))
                    y_made.done(dve.tensor_tensor(y_lo[:, b, 0:nq], chunk(c)[:, 0:nq], y_hi[:, b, 0:nq].bitcast(F32), ALU.subtract), (l, b))
                y_made.wait(dve, (l, 7))

                u0 = first["merge", l]
                n0, g0 = units[u0].product, l * 4 * DC

                def merge_turn(d):
                    straight = isinstance(d, int)
                    for k in range(4):
                        _, ii, per = at(u0, k, d)
                        dve.wait_ge(unit_done, u0 + k + 1 + d * 4)
                        dve.wait_ge(gate_done, d * 4 + (g0 + k + 1))
                        merged = Q[:, bass.ds(d, 1), 0:nq]
                        work = wb[:, k % 2:k % 2 + 1, 0:nq]
                        branch = bank[4 + k][:, 0:nq].unsqueeze(1)
                        gate = wa[:, k % 2:k % 2 + 1, 0:nq]
                        if k == 1 and not (straight and d == 0):
                            dve.wait_ge(branch_added, d * 3 + 3 * l * DC)
                        dve.tensor_tensor(merged if k == 0 else work, gate, branch, ALU.mult).then_inc(gated, 1)
                        split_lo(dve, n0 + k + 2 + (4 * d if straight else 0), ii, per)
                        if k > 0:
                            dve.wait_ge(gated, d * 4 + (g0 + k + 1))
                            if k > 1:
                                dve.wait_ge(branch_added, d * 3 + (3 * l * DC + k - 1))
                            dve.tensor_tensor(merged, merged, work, ALU.add).then_inc(branch_added, 1)
                turns(dve, DC, merge_turn)
                for k in range(DC):
                    split_h((l, "merged"), nq, Q[:, k, 0:nq], k)
                add_block(l, "out", first["out", l], nq, 1)

                n = tokens(l, "ffn2")
                norm_block(l, 2, n)
                for part in range(len(PARTS)):
                    up(l, 2, part, n)
                    add_block(l, (2, part), first["down", l, 2, part], n, 2)

            roots.wait(dve, "final")
            link(dve.reciprocal(rstd[:, 0:LAT], rstd[:, 0:LAT]))
            for k in range(DC):
                normed.done(dve.scalar_tensor_tensor(out=X[:, k, 0:LAT], in0=X[:, k, 0:LAT], scalar=vec2[:, 0, V_FIN + k:V_FIN + k + 1],
                                                     in1=rstd[:, 0:LAT], op0=ALU.mult, op1=ALU.mult), ("final", k))

        @block.gpsimd
        def _(pool):
            pool.memset(eps_col[:, :], EPS)
            pool.memset(tokf[:, :, :], 0.0)
            pool.memset(tokb[:, :, :], 0.0)
            cleared.done(pool.memset(cact[:, :, :], 0.0), "all")

            def store_modulation(l, chunk0, m):
                pool.wait_ge(mod_copied, m + 1)
                for s in range(2):
                    pool.dma_start(mod_rows[l, s, :, bass.ds(chunk0 * P, 4 * P)], mod_row[s::32, :]).then_inc(mod_stored, 16)

            def load_modulation(l, half, m):
                pool.wait_ge(mod_stored, 32 * m)
                r0, r1 = ((0, MOD_EARLY), (MOD_EARLY, MOD_CHUNKS))[half]
                if half == 1:
                    mod_turned.wait(pool, (l, 0))
                elif l > 0:
                    y_made.wait(pool, (l - 1, 7))
                mod_loads.done(pool.dma_start(scores_flat[0:r1 - r0, :].rearrange("r (q c) -> r q c", c=P),
                                              mod_rows[l].rearrange("s j (r c) -> r (s j) c", c=P)[r0:r1]), (l, half))

            with pool.Fori(0, MOD_FIRST // 4) as i:
                store_modulation(0, i * 4, i)
            load_modulation(0, 0, MOD_FIRST // 4)
            for key in sorted(MOD_AT):
                l, chunk0 = MOD_AT[key]
                if key == (0, 2, 0):
                    load_modulation(0, 1, mod_first[key])
                if key == (1, 1, 0):
                    load_modulation(1, 0, mod_first[key])
                m0 = mod_first[key]
                with pool.Fori(0, PARTS[key[2]][1] // 2) as i:
                    store_modulation(l, i * 4 + chunk0, i + m0)
            load_modulation(1, 1, mod_first["end"])


_INS = ['x', 'c', 'ctx', 'c_ctx', 'w_mod', 'b_mod', 'norm_ffn1', 'ffn1_w_gate', 'ffn1_w_up', 'ffn1_w_down',
        'norm_mix', 'w_in', 'b_gate', 'attn_sink', 'na_rpb', 'qk_norm_q', 'qk_norm_k', 'ssm_conv_w', 'ssm_conv_b',
        'ssm_dt_bias', 'ssm_a_log', 'ssm_d', 'ssm_norm', 'w_branch', 'w_out', 'norm_ffn2', 'ffn2_w_gate',
        'ffn2_w_up', 'ffn2_w_down', 'final_norm']
_OUTS = [((1, LAT, D), 'float32')]


def kernel(**inputs):
    import numpy as _np
    import concourse.bacc as _bacc
    from concourse import mybir as _mybir
    from concourse.bass_utils import run_bass_kernel_spmd as _run

    arrays = {f"in_{name}_dram": _np.ascontiguousarray(inputs[name]) for name in _INS}
    arrays["in_consts_dram"] = constants()
    values = {}
    for _ in range(2):
        nc = _bacc.Bacc("TRN2", target_bir_lowering=False, num_devices=1)
        args = [nc.dram_tensor(n, a.shape, _mybir.dt.from_np(a.dtype), kind="ExternalInput").ap() for n, a in arrays.items()]
        for i, (shape, dtype) in enumerate(_OUTS):
            args.append(nc.dram_tensor(f"out_{i}_dram", shape, _mybir.dt.from_np(_np.dtype(dtype)), kind="ExternalOutput").ap())
        build(nc, values, *args)
    r = _run(nc, [arrays], core_ids=[0])
    return r.results[0]["out_0_dram"]
```

```python
from contextlib import ExitStack

import numpy as np

import concourse.bass as bass
from concourse import mybir

F32 = mybir.dt.float32
F32R = mybir.dt.float32r
ALU = mybir.AluOpType
ACT = mybir.ActivationFunctionType
AX_X = mybir.AxisListType.X

P = 128
LAYERS = 2
D = 1024
DC = D // P
LAT, CTX = 256, 256
TOK = LAT + CTX
FF = 2816
HD = 64
EPS = 1e-6
NEG = -1e30
BIG = 8.0
SCALE = HD ** -0.5
GRID_W, NA_ROWS, NA_COLS = 64, 8, 16
ROWS = LAT // GRID_W
CONV = 5
DT_COL = 2816
GATE_COL = DT_COL + 8
MOD_CHUNKS = 9 * DC

AQ, AK, AV, BQ, BK, BV, CQ, CK, CV, Z, XS, SB_, SC_ = 0, 2, 3, 4, 6, 8, 10, 12, 13, 14, 16, 18, 20
IN_CHUNKS = 22
QCHUNKS = [AQ, AQ + 1, BQ, BQ + 1, CQ, CQ + 1, Z, Z + 1]
KCHUNKS = [c for c in range(IN_CHUNKS) if c not in QCHUNKS]
VCHUNKS = [AV, BV, BV + 1, CV]
NORMED = [CQ, CQ + 1, CK]
ROTATED = [CQ, CQ + 1, CK, AQ, AQ + 1, AK]
SWAPPED = [AK, CK]
IN_ORDER = [XS, XS + 1, SB_, SB_ + 1, SC_, SC_ + 1, CQ, CQ + 1, CK, AQ, AQ + 1, AK, AV, BV, BV + 1, CV,
            Z, Z + 1, BQ, BQ + 1, BK, BK + 1]
PREP = {0: [("conv", 0)], 1: [("conv", 1)], 2: [("conv", 2)], 3: [("conv", 3)], 4: [("conv", 4)], 5: [("conv", 5)],
        6: [("convend", 5), ("square", 0)], 7: [("square", 1), ("qk", 0)], 8: [("square", 2), ("qk", 1)],
        9: [("qk", 2), ("rope", 0)], 10: [("rope", 1)], 11: [("rope", 2)], 12: [("rope", 3), ("swap", 1)],
        13: [("rope", 4), ("v", 0)], 14: [("rope", 5), ("v", 1)], 15: [("v", 2), ("dt", 0)], 16: [("v", 3)],
        17: [("x", 0), ("swap", 0), ("tok", 0)], 18: [("x", 1), ("cum", 0)], 19: [("tot", 0), ("cumtok", 0)]}

V_BMOD, V_NORM, V_BGATE = 0, 72, 96
V_CONVW, V_CONVB, V_SNORM, V_QG, V_KG, V_FIN, V_C, V_CC = 0, 30, 36, 38, 39, 40, 48, 56
PACK2 = 64

CONST_COLS = {}
_at = 0
for _name, _w in (("ident", 128), ("ones", 128), ("blockones", 128), ("rot", 128), ("swap", 128), ("trif", 384),
                  ("trib", 384), ("maskf", 384), ("maskb", 384), ("wmask", 512), ("nvalid", 256), ("nneg", 256),
                  ("ropec", 256), ("ropes", 256), ("sel", 1024)):
    CONST_COLS[_name] = (_at, _at + _w)
    _at += _w
CONSTS = _at


def constants():
    c = np.zeros((P, CONSTS), np.float32)

    def put(name, a):
        lo, hi = CONST_COLS[name]
        c[:a.shape[0], lo:hi] = a

    p = np.arange(P)[:, None]
    f = np.arange(P)[None, :]
    put("ident", (p == f).astype(np.float32))
    put("ones", np.ones((P, P), np.float32))
    put("blockones", (p // HD == f // HD).astype(np.float32))
    rot = np.zeros((P, P), np.float32)
    for i in range(P):
        if i % 32 < 16:
            rot[i + 16, i] = -1.0
        else:
            rot[i - 16, i] = 1.0
    put("rot", rot)
    put("swap", ((p + HD) % P == f).astype(np.float32))
    q = np.arange(384)[None, :] - P
    put("trif", (q >= p).astype(np.float32))
    put("trib", (q <= p).astype(np.float32))
    put("maskf", np.where(q >= p, 0.0, NEG).astype(np.float32))
    put("maskb", np.where(q <= p, 0.0, NEG).astype(np.float32))
    k = np.arange(LAT)[None, :]
    put("wmask", np.concatenate([np.where(np.abs(t * P + p - k) <= 128, 0.0, NEG) for t in range(2)], 1).astype(np.float32))
    qc, kc = p % GRID_W, k % GRID_W
    start = np.clip(qc - NA_COLS // 2, 0, GRID_W - NA_COLS)
    ok = (kc >= start) & (kc < start + NA_COLS)
    put("nvalid", np.where(ok, BIG, 0.0).astype(np.float32))
    put("nneg", np.where(ok, 0.0, NEG).astype(np.float32))
    pos = np.arange(LAT)
    axes = np.stack([pos // GRID_W, pos % GRID_W], 0).astype(np.float32)
    inv = (np.float32(1.0) / (np.float32(10000.0) ** (np.arange(HD // 4, dtype=np.float32) * np.float32(4.0) / np.float32(HD)))).astype(np.float32)
    ang = np.zeros((P, LAT), np.float32)
    for i in range(P):
        ang[i] = axes[(i % HD) // 32] * inv[i % 16]
    put("ropec", np.cos(ang))
    put("ropes", np.sin(ang))
    sel = np.zeros((8, 8, P), np.float32)
    for r in range(8):
        sel[r, r] = 1.0
    put("sel", sel.reshape(8, 8 * P))
    return c


class Signal:

    def __init__(self, nc, ctx, name, values, by=1):
        self.sem = ctx.enter_context(nc.semaphore(name))
        self.name, self.values, self.by, self.count = name, values, by, 0

    def done(self, ins, step=None):
        ins.then_inc(self.sem, self.by)
        self.count += self.by
        self.values[self.name, step] = self.count

    def mark(self, step):
        self.values[self.name, step] = self.count

    def wait(self, eng, step):
        eng.wait_ge(self.sem, self.values.get((self.name, step), self.by))


class Unit:

    def __init__(self, kind, rows, dmas):
        self.kind, self.rows, self.dmas = kind, rows, dmas


SLOTS = 4
SLOT_ROWS = 10
PARTS = [(0, 8), (8, 8), (16, 6)]
MOD_FIRST = 28
MOD_AT = {(0, 1, 0): (0, 28), (0, 1, 1): (0, 44), (0, 1, 2): (0, 60),
          (0, 2, 0): (1, 0), (0, 2, 1): (1, 16), (0, 2, 2): (1, 32),
          (1, 1, 0): (1, 44), (1, 1, 2): (1, 60)}
MOD_EARLY = 3 * DC


def plan_units():
    units, first = [], {}

    def stage(name, n, kind, rows, dmas=1):
        first[name] = len(units)
        units.extend(Unit(kind, rows, dmas) for _ in range(n))

    for l in range(LAYERS):
        if l == 0:
            stage("mod", MOD_FIRST, "mod", DC)
        for ffn in (1, 2):
            if ffn == 2:
                stage(("in", l), IN_CHUNKS, "product", DC)
                stage(("merge", l), 4 * DC, "product", DC + 2, 2)
                stage(("out", l), DC, "product", DC)
            for part, (_, n) in enumerate(PARTS):
                first["up", l, ffn, part] = len(units)
                for _ in range(2 * n):
                    if (l, ffn, part) in MOD_AT:
                        units.append(Unit("mod", DC, 1))
                    units.append(Unit("product", DC, 1))
                stage(("down", l, ffn, part), DC, "product", n)
    count, products = [0] * SLOTS, 0
    for u, unit in enumerate(units):
        unit.slot = u % SLOTS
        count[unit.slot] += 16 * unit.dmas
        unit.loaded = count[unit.slot]
        unit.product = products
        products += unit.kind == "product"
    return units, first


def build(nc, values, x, c, ctx_tokens, c_ctx, w_mod, b_mod, norm_ffn1, ffn1_w_gate, ffn1_w_up, ffn1_w_down,
          norm_mix, w_in, b_gate, attn_sink, na_rpb, qk_norm_q, qk_norm_k, ssm_conv_w, ssm_conv_b, ssm_dt_bias,
          ssm_a_log, ssm_d, ssm_norm, w_branch, w_out, norm_ffn2, ffn2_w_gate, ffn2_w_up, ffn2_w_down, final_norm,
          consts, out):
    units, first = plan_units()
    product_units = [u for u, unit in enumerate(units) if unit.kind == "product"]
    ffn_weights = {1: (ffn1_w_gate, ffn1_w_up, ffn1_w_down), 2: (ffn2_w_gate, ffn2_w_up, ffn2_w_down)}

    with ExitStack() as ctx:
        def sb(name, shape, dt=F32, where=ctx):
            return where.enter_context(nc.sbuf_tensor(name, shape, dt))

        def signal(name, by=1):
            return Signal(nc, ctx, name, values, by)

        X = sb("X", [P, DC, TOK])
        h_hi = sb("h_hi", [P, DC, TOK], F32R)
        h_lo = sb("h_lo", [P, DC, TOK], F32R)
        raw = [sb(f"raw{s}", [P, SLOT_ROWS, P]) for s in range(SLOTS)]
        w_hi = [sb(f"w_hi{s}", [P, SLOT_ROWS, P], F32R) for s in range(2)]
        w_lo = [sb(f"w_lo{s}", [P, SLOT_ROWS, P], F32R) for s in range(2)]
        cst = sb("cst", [P, CONSTS])
        vec1 = sb("vec1", [P, LAYERS, P])
        vec2 = sb("vec2", [P, LAYERS, PACK2])
        skip_all = sb("skip_all", [P, LAYERS * 4])
        skip_w = sb("skip_w", [P, LAYERS, 2])
        cact = sb("cact", [P, DC, 32])
        mod_row = sb("mod_row", [P, TOK])
        mod = sb("mod", [P, MOD_CHUNKS, 2])
        gain = sb("gain", [P, 3, DC, 2])
        rstd = sb("rstd", [P, TOK])
        wa = sb("wa", [P, 2, TOK])
        wb = sb("wb", [P, 2, TOK])
        early_root = sb("early_root", [P, 8])
        nbias = sb("nbias", [P, 4, 2, LAT])
        scores = sb("scores", [P, 2, TOK])
        probs = sb("probs", [P, 2, TOK])
        probs_t = sb("probs_t", [P, 4, LAT])
        sink8 = sb("sink8", [P, 4])
        eps_col = sb("eps_col", [P, 1])
        gatev = sb("gatev", [P, 3, DC, 2])
        smax = sb("smax", [P, 2, 4])
        dt_t = sb("dt_t", [8, TOK])
        da_t = sb("da_t", [8, TOK])
        dtv = sb("dtv", [8, 4])
        tok = sb("tok", [P, 4, 16])
        tokf = sb("tokf", [P, 4, 8])
        tokb = sb("tokb", [P, 4, 8])
        nct = sb("nct", [P, 4, 8])
        tct = sb("tct", [P, 2, 8])
        tot = sb("tot", [P, 8])
        wdt_raw = sb("wdt_raw", [P, DC, 8])
        wdt_hi = sb("wdt_hi", [P, DC, 8], F32R)
        wdt_lo = sb("wdt_lo", [P, DC, 8], F32R)
        with ExitStack() as region:
            inner_hi = sb("inner_hi", [P, 8, TOK], F32R, region)
            inner_lo = sb("inner_lo", [P, 8, TOK], F32R, region)
        with ExitStack() as region:
            Q = sb("Q", [P, 8, TOK], F32, region)
            with ExitStack() as mixer:
                K = sb("K", [P, 14, TOK], F32, mixer)
                v_tok = sb("v_tok", [P, 4, 4 * P], F32, mixer)
                x_tok = sb("x_tok", [P, 4, 2 * P], F32, mixer)
                k_swap = sb("k_swap", [P, 2, TOK], F32, mixer)
            with ExitStack() as merge:
                y_hi = sb("y_hi", [P, 8, TOK], F32R, merge)
                y_lo = sb("y_lo", [P, 8, TOK], F32R, merge)
        with ExitStack() as region:
            x_in = sb("x_in", [P, 4, D], F32, region)
            pack1 = sb("pack1", [P, LAYERS, P], F32, region)
            pack2 = sb("pack2", [PACK2, LAYERS, P], F32, region)
            out_rows = sb("out_rows", [P, 2, D], F32, region)
        bias_rows = nc.dram_tensor("bias_rows", (LAYERS, 4, 2 * ROWS - 1, GRID_W, P), F32, kind="Internal").ap()
        mod_rows = nc.dram_tensor("mod_rows", (LAYERS, 2, 4, MOD_CHUNKS * P), F32, kind="Internal").ap()
        bank = [ctx.enter_context(nc.psum_tensor(f"bank{b}", [P, TOK], F32)) for b in range(8)]

        def const(name):
            lo, hi = CONST_COLS[name]
            return cst[:, lo:hi]

        def chunk(c):
            return Q[:, QCHUNKS.index(c)] if c in QCHUNKS else K[:, KCHUNKS.index(c)]

        loaded = [ctx.enter_context(nc.semaphore(f"loaded{s}")) for s in range(SLOTS)]
        unit_done = ctx.enter_context(nc.semaphore("unit_done"))
        hi_made = ctx.enter_context(nc.semaphore("hi_made"))
        lo_made = ctx.enter_context(nc.semaphore("lo_made"))
        silu_done = ctx.enter_context(nc.semaphore("silu_done"))
        inner_made = ctx.enter_context(nc.semaphore("inner_made"))
        inner_hi_made = ctx.enter_context(nc.semaphore("inner_hi_made"))
        inner_lo_made = ctx.enter_context(nc.semaphore("inner_lo_made"))
        added = ctx.enter_context(nc.semaphore("added"))
        gate_done = ctx.enter_context(nc.semaphore("gate_done"))
        gated = ctx.enter_context(nc.semaphore("gated"))
        branch_added = ctx.enter_context(nc.semaphore("branch_added"))
        mod_copied = ctx.enter_context(nc.semaphore("mod_copied"))
        mod_stored = ctx.enter_context(nc.semaphore("mod_stored"))
        mod_loads = signal("mod_loads", 16)
        mod_turned = signal("mod_turned")
        start_loads = signal("start_loads", 16)
        const_loads = signal("const_loads", 16)
        pack_loads = signal("pack_loads", 16)
        layer_loads = signal("layer_loads", 16)
        bias_loads = signal("bias_loads", 16)
        rows_written = signal("rows_written", 16)
        out_stored = signal("out_stored", 16)
        pe_start = signal("pe_start")
        start_copied = signal("start_copied")
        cond_ready = signal("cond_ready")
        vectors = signal("vectors")
        squares = signal("squares")
        sums = signal("sums")
        roots = signal("roots")
        normed = signal("normed")
        h_hi_made = signal("h_hi_made")
        h_made = signal("h_made")
        act_chain = signal("act_chain")
        dve_chain = signal("dve_chain")
        pool_chain = signal("pool_chain")
        projected = signal("projected")
        prep_done = signal("prep_done")
        prep_read = signal("prep_read")
        prepared = signal("prepared")
        act_read = signal("act_read")
        act_prepared = signal("act_prepared")
        conv_out = signal("conv_out")
        scored = signal("scored")
        bounded = signal("bounded")
        exped = signal("exped")
        normalised = signal("normalised")
        turned = signal("turned")
        turned_copied = signal("turned_copied")
        mixed = signal("mixed")
        y_stored = signal("y_stored")
        cb_done = signal("cb_done")
        cum_spread = signal("cum_spread")
        spread = signal("spread")
        decay_arg = signal("decay_arg")
        decayed = signal("decayed")
        weighed = signal("weighed")
        ssm_done = signal("ssm_done")
        ssm_read = signal("ssm_read")
        y_hi_made = signal("y_hi_made")
        y_made = signal("y_made")
        cleared = signal("cleared")
        soft = signal("soft")
        convolved = signal("convolved")
        pads_cleared = signal("pads_cleared")
        sunk = signal("sunk")
        skipped = signal("skipped")
        ssm_out = signal("ssm_out")
        bias_ready = signal("bias_ready")

        scores_flat = scores[:, :, :].rearrange("p a b -> p (a b)")
        probs_flat = probs[:, :, :].rearrange("p a b -> p (a b)")
        turned_probs = (probs_t, scores_flat.rearrange("p (k q) -> p k q", k=4))
        decay_f = (chunk(BV), chunk(BV + 1))
        decay_b = (chunk(AV), chunk(CV))
        weighed_by = (mod_row[:, :], rstd[:, :])
        padded = [f[:, 0:2 * (LAT + CONV - 1)].rearrange("p (s t) -> p s t", s=2) for f in (scores_flat, probs_flat)]

        def attention_tasks(last_layer):
            return [(br, h, st, qt) for br in range(3) for h in range(4) for st in range(1 if last_layer else 2) for qt in range(2)]

        SOURCES = (2, 3, 0, 1)

        def first_part(last_layer, t):
            per = 1 if last_layer else 2
            return t // per if t % per == 0 else None

        def second_part(last_layer, t):
            per = 1 if last_layer else 2
            return t // per if t % per == per - 1 else None

        def spread_head(slot):
            return slot // 5 if slot is not None and slot % 5 == 0 and slot < 20 else None

        def source_step(slot):
            if slot is None or slot < 0 or slot >= 20 or slot % 5 == 0:
                return None
            h, i = slot // 5, slot % 5 - 1
            return 4 * h + i, h, SOURCES[i]

        def behind(slot, lag):
            return None if slot is None else slot - lag

        def value_column(br, h):
            return (h // 2 * HD, P + h * HD, 3 * P + h // 2 * HD)[br]

        def dve_link(dve, ins):
            dve_chain.done(ins, dve_chain.count)
            dve.wait_ge(dve_chain.sem, dve_chain.count)

        def act_link(act, ins):
            act_chain.done(ins, act_chain.count)
            act.wait_ge(act_chain.sem, act_chain.count)

        block = ctx.enter_context(nc.Block())

        def tokens(l, name):
            return LAT if l == LAYERS - 1 and name in ("q", "merge", "ffn2") else TOK

        def in_tokens(l, c):
            return tokens(l, "q") if c in QCHUNKS or c >= SC_ else TOK

        def streams(n):
            return range(n // LAT)

        inner_first = {}
        n_inner = 0
        for l in range(LAYERS):
            for ffn in (1, 2):
                for part, (_, n) in enumerate(PARTS):
                    inner_first[l, ffn, part] = n_inner
                    n_inner += n
        add_first = {}
        n_add = 0
        for l in range(LAYERS):
            for step in [(1, 0), (1, 1), (1, 2), "out", (2, 0), (2, 1), (2, 2)]:
                add_first[l, step] = n_add
                n_add += DC

        TURN_AT = 5

        def next_norm(l, name):
            if name == (1, 2):
                return (l, "mix"), TOK
            if name == "out":
                return (l, 2), tokens(l, "ffn2")
            if name == (2, 2):
                return ((l + 1, 1), TOK) if l + 1 < LAYERS else (("final", 0), LAT)
            return None, 0

        n_roots = {next_norm(l, name)[0]: 3 * l + i for l in range(LAYERS) for i, name in enumerate([(1, 2), "out", (2, 2)])}

        def next_modulation(l, name):
            if name == (1, 2):
                return [(l, 1)]
            return [(l + 1, 0)] if name == (2, 2) and l + 1 < LAYERS else []

        @block.sync
        def _(sp):
            def columns(w, l, col, rows=None, row0=0):
                v = w[l].rearrange("(c p) n -> p c n", p=P)
                if rows is not None:
                    v = v[:, row0:row0 + rows, :]
                return v[:, :, bass.ds(col, P)]

            def load(u, i, per, *sources):
                unit = units[u]
                if u >= SLOTS or not isinstance(i, int):
                    old = units[u - SLOTS] if isinstance(i, int) else unit
                    if old.kind == "mod":
                        sp.wait_ge(unit_done, u - SLOTS + 1 + i * per[0])
                    else:
                        n = old.product if isinstance(i, int) else unit.product - SLOTS * per[1] // per[0]
                        sp.wait_ge(lo_made, n + 1 + i * per[1])
                for rows, src in sources:
                    sp.dma_start(raw[unit.slot][:, rows[0]:rows[1], :], src).then_inc(loaded[unit.slot], 16)

            def stage(u0, n, source):
                for j in range(SLOTS):
                    load(u0 + j, 0, (0, 0), *source(j))
                turns = (n - SLOTS) // SLOTS
                if turns > 0:
                    with sp.Fori(1, turns + 1) as i:
                        for j in range(SLOTS):
                            load(u0 + j, i, (SLOTS, SLOTS), *source(i * SLOTS + j))
                for j in range(SLOTS * (turns + 1), n):
                    load(u0 + j, 0, (0, 0), *source(j))

            start_loads.done(sp.dma_start(pack1[0:MOD_CHUNKS, :, :], b_mod.rearrange("l (r c) -> r l c", c=P)))
            for n, w in enumerate((norm_ffn1, norm_mix, norm_ffn2)):
                r = V_NORM + n * DC
                start_loads.done(sp.dma_start(pack1[r:r + DC, :, :], w.rearrange("l (r c) -> r l c", c=P)))
            start_loads.done(sp.dma_start(pack1[V_BGATE:V_BGATE + 4 * DC, :, :], b_gate.rearrange("l (r c) -> r l c", c=P)))
            for j in range(CONV):
                r = V_CONVW + j * 6
                start_loads.done(sp.dma_start(pack2[r:r + 6, :, :], ssm_conv_w[:, j, :].rearrange("l (r c) -> r l c", c=P)))
            start_loads.done(sp.dma_start(pack2[V_CONVB:V_CONVB + 6, :, :], ssm_conv_b.rearrange("l (r c) -> r l c", c=P)))
            start_loads.done(sp.dma_start(pack2[V_SNORM:V_SNORM + 2, :, :], ssm_norm.rearrange("l (r c) -> r l c", c=P)))
            for v, w in ((V_QG, qk_norm_q), (V_KG, qk_norm_k)):
                for half in range(2):
                    start_loads.done(sp.dma_start(pack2[v:v + 1, :, half * HD:(half + 1) * HD],
                                                  w.rearrange("(a l) c -> a l c", a=1)))
            start_loads.done(sp.dma_start(skip_all[:, :], ssm_d.rearrange("(a l) h -> a (l h)", a=1).to_broadcast([P, LAYERS * 4])))
            for l in range(LAYERS):
                start_loads.done(sp.dma_start(pack2[V_FIN:V_FIN + DC, l, :], final_norm.rearrange("(r c) -> r c", c=P)))
                start_loads.done(sp.dma_start(pack2[V_C:V_C + DC, l, :], c.rearrange("a (r c) -> (a r) c", c=P)))
                start_loads.done(sp.dma_start(pack2[V_CC:V_CC + DC, l, :], c_ctx.rearrange("(r c) -> r c", c=P)))
            start_loads.mark("all")

            for l in range(LAYERS):
                if l == 0:
                    stage(first["mod"], MOD_FIRST, lambda j: [((0, DC), columns(w_mod, 0, j * P))])
                for ffn in (1, 2):
                    wg, wu, wd = ffn_weights[ffn]
                    if ffn == 2:
                        for pos, col in enumerate(IN_ORDER):
                            load(first["in", l] + pos, 0, (0, 0), ((0, DC), columns(w_in, l, col * P)))

                        u0 = first["merge", l]

                        def merge_unit(k, d, i):
                            load(u0 + k, i, (SLOTS, SLOTS) if not isinstance(i, int) else (0, 0),
                                 ((0, DC), columns(w_in, l, GATE_COL + k * D + d * P)),
                                 ((DC, DC + 2), w_branch[l, k].rearrange("(c p) n -> p c n", p=P)[:, :, bass.ds(d * P, P)]))
                        for k in range(4):
                            merge_unit(k, 0, 0)
                        with sp.Fori(1, DC) as d:
                            for k in range(4):
                                merge_unit(k, d, d)
                        stage(first["out", l], DC, lambda j: [((0, DC), columns(w_out, l, j * P))])
                    for part, (c0, n) in enumerate(PARTS):
                        u0 = first["up", l, ffn, part]

                        extra = MOD_AT.get((l, ffn, part))
                        step = 2 if extra else 1

                        def turn_loads(i, per):
                            for j in range(4):
                                if extra:
                                    load(u0 + 2 * j, i, per, ((0, DC), columns(w_mod, extra[0], i * (4 * P) + (extra[1] + j) * P)))
                                load(u0 + step * j + step - 1, i, per,
                                     ((0, DC), columns((wg, wu)[j % 2], l, i * (2 * P) + (c0 + j // 2) * P)))
                        turn_loads(0, (0, 0))
                        with sp.Fori(1, n // 2) as i:
                            turn_loads(i, (4 * step, 4))
                        stage(first["down", l, ffn, part], DC, lambda j: [((0, n), columns(wd, l, j * P, n, c0))])
            for t in range(2):
                start_copied.wait(sp, ("out", t))
                out_stored.done(sp.dma_start(out[0, t * P:(t + 1) * P, :], out_rows[:, t, :]), t)
            out_stored.wait(sp, 1)

        def split_hi(act, n, i=0, per=(0, 0)):
            if n >= len(product_units):
                return
            unit = units[product_units[n]]
            act.wait_ge(loaded[unit.slot], unit.loaded + i * (16 * unit.dmas * per[0] // SLOTS))
            if n >= 2:
                act.wait_ge(unit_done, product_units[n - 2] + 1 + i * per[0])
            act.activation(w_hi[n % 2][:, 0:unit.rows, :], raw[unit.slot][:, 0:unit.rows, :], ACT.Copy).then_inc(hi_made, 1)

        def split_lo(dve, n, i=0, per=(0, 0)):
            if n >= len(product_units):
                return
            unit = units[product_units[n]]
            dve.wait_ge(hi_made, n + 1 + i * per[1])
            dve.tensor_tensor(w_lo[n % 2][:, 0:unit.rows, :], raw[unit.slot][:, 0:unit.rows, :],
                              w_hi[n % 2][:, 0:unit.rows, :].bitcast(F32), ALU.subtract).then_inc(lo_made, 1)

        def turns(eng, n_turns, body):
            body(0)
            if n_turns > 2:
                with eng.Fori(1, n_turns - 1) as i:
                    body(i)
            if n_turns > 1:
                body(n_turns - 1)

        def at(u0, j, i, step=1):
            j = step * j + step - 1
            return (u0 + 4 * step * i + j, 0, (0, 0)) if isinstance(i, int) else (u0 + j, i, (4 * step, 4))

        def step_of(l, ffn, part):
            return 2 if (l, ffn, part) in MOD_AT else 1

        mod_first = {"start": 0}
        n_mod = MOD_FIRST // 4
        for key in sorted(MOD_AT):
            mod_first[key] = n_mod
            n_mod += PARTS[key[2]][1] // 2
        mod_first["end"] = n_mod

        @block.tensor
        def _(pe):
            def product(u, i, per, psum, rows, rhs, before=None, row0=0, signal_it=True):
                unit = units[u]
                pe.wait_ge(lo_made, unit.product + 1 + i * per[1])
                s = unit.product % 2
                for k in range(rows):
                    if before:
                        before(k)
                    hi, lo = rhs(k)
                    pe.matmul(psum, w_hi[s][:, row0 + k, :], hi, start=(k == 0), stop=False)
                    pe.matmul(psum, w_hi[s][:, row0 + k, :], lo, start=False, stop=False)
                    mm = pe.matmul(psum, w_lo[s][:, row0 + k, :], hi, start=False, stop=(k == rows - 1))
                if signal_it:
                    mm.then_inc(unit_done, 1)

            def h_rhs(n):
                return lambda k: (h_hi[:, k, 0:n], h_lo[:, k, 0:n])

            def sum_square(key, n, k):
                squares.wait(pe, (key, k))
                mm = pe.matmul(bank[6][:, 0:n], const("ones"), wa[:, k % 2, 0:n], start=(k == 0), stop=(k == DC - 1))
                sums.done(mm, (key, k))

            def modulation(u, i, per, j, m):
                unit = units[u]
                pe.wait_ge(loaded[unit.slot], unit.loaded + i * (16 * per[0] // SLOTS))
                if j == 0 and m is not None:
                    pe.wait_ge(mod_copied, m)
                for k in range(DC):
                    rows = slice(32 * (k % 4), 32 * (k % 4) + 32)
                    mm = pe.matmul(bank[7][rows, j * P:(j + 1) * P], cact[:, k, :], raw[unit.slot][:, k, :],
                                   start=(k < 4), stop=(k >= 4))
                mm.then_inc(unit_done, 1)

            def turn_modulation(l, half):
                mod_loads.wait(pe, (l, half))
                r0, r1 = ((0, MOD_EARLY), (MOD_EARLY, MOD_CHUNKS))[half]
                n = r1 - r0
                pe.wait_ge(mod_copied, MOD_FIRST // 4 if (l, half) == (0, 0) else mod_first[{(0, 1): (0, 2, 0), (1, 0): (1, 1, 0), (1, 1): "end"}[l, half]])
                for s in range(2):
                    for j in range(4):
                        mm = pe.matmul(bank[7][:, s * MOD_CHUNKS + r0:s * MOD_CHUNKS + r1], scores_flat[0:n, (4 * s + j) * P:(4 * s + j + 1) * P],
                                       const("ident")[0:n, 0:n], start=(j == 0), stop=(j == 3))
                mod_turned.done(mm, (l, half))

            def up(l, ffn, part, n):
                u0, c0 = first["up", l, ffn, part], inner_first[l, ffn, part]
                step = step_of(l, ffn, part)

                if (ffn, part) == (1, 0):
                    vectors.wait(pe, (l, 0))

                def body(i):
                    for j in range(4):
                        if step == 2:
                            u, ii, per = at(u0, j, i, 2)
                            m0 = mod_first[l, ffn, part]
                            modulation(u - 1, ii, per, j, i + m0)
                        if not (isinstance(i, int) and i == 0):
                            read = silu_done if j % 2 == 0 else inner_made
                            pe.wait_ge(read, i * 2 + (c0 + j // 2 - 1))
                        wait_h = part == 0 and isinstance(i, int) and i == 0 and j == 0
                        product(*at(u0, j, i, step), bank[j][:, 0:n], DC, h_rhs(n),
                                (lambda k: h_made.wait(pe, (l, ffn, k))) if wait_h else None)
                turns(pe, PARTS[part][1] // 2, body)

            def between(l, name, d):
                key, n = next_norm(l, name)
                if key and d > 0:
                    sum_square(key, n, d - 1)
                if d == TURN_AT:
                    for args in next_modulation(l, name):
                        turn_modulation(*args)
                if key and d == DC - 1:
                    sum_square(key, n, d)

            def down(l, ffn, part, n):
                u0, a0 = first["down", l, ffn, part], add_first[l, (ffn, part)]
                rows = PARTS[part][1]
                last = inner_first[l, ffn, part] + rows
                for d in range(DC):
                    if a0 + d >= 2:
                        pe.wait_ge(added, a0 + d - 1)
                    product(u0 + d, 0, (0, 0), bank[4 + d % 2][:, 0:n], rows, lambda k: (inner_hi[:, k, 0:n], inner_lo[:, k, 0:n]),
                            (lambda k: pe.wait_ge(inner_lo_made, last - rows + k + 1)) if d == 0 else None)
                    between(l, (ffn, part), d)

            def prepare(l, step, i):
                if step == "qk":
                    n = in_tokens(l, NORMED[i])
                    if i > 0:
                        act_read.wait(pe, (l, "qk", i - 1))
                    squares.wait(pe, (l, "qk", i))
                    mm = pe.matmul(bank[5][:, 0:n], const("blockones"), wa[:, i % 2, 0:n], start=True, stop=True)
                elif step == "rope":
                    c = ROTATED[i]
                    if i >= 2:
                        prep_read.wait(pe, (l, "rope", i - 2))
                    if c in NORMED:
                        prepared.wait(pe, (l, "qk", NORMED.index(c)))
                    else:
                        projected.wait(pe, (l, c))
                    mm = pe.matmul(bank[6 + i % 2][:, 0:LAT], const("rot"), chunk(c)[:, 0:LAT], start=True, stop=True)
                elif step == "swap":
                    c = SWAPPED[i]
                    prepared.wait(pe, (l, "rope", ROTATED.index(c)))
                    if c == CK:
                        act_read.wait(pe, (l, "qk", 2))
                    else:
                        prep_read.wait(pe, (l, "v", 3))
                    mm = pe.matmul(bank[5][:, :], const("swap"), chunk(c), start=True, stop=True)
                elif step == "v":
                    if i == 0:
                        act_prepared.wait(pe, (l, "swap", 1))
                    else:
                        prep_read.wait(pe, (l, "v", i - 1))
                    projected.wait(pe, (l, VCHUNKS[i]))
                    for t in range(4):
                        mm = pe.transpose(bank[5][:, t * P:(t + 1) * P], chunk(VCHUNKS[i])[:, t * P:(t + 1) * P], const("ident"))
                elif step == "dt":
                    prepared.wait(pe, (l, "wdt"))
                    for k in range(DC):
                        pe.matmul(bank[4][0:8, :], wdt_hi[:, k, :], h_hi[:, k, :], start=(k == 0), stop=False)
                        pe.matmul(bank[4][0:8, :], wdt_hi[:, k, :], h_lo[:, k, :], start=False, stop=False)
                        mm = pe.matmul(bank[4][0:8, :], wdt_lo[:, k, :], h_hi[:, k, :], start=False, stop=(k == DC - 1))
                elif step == "x":
                    conv_out.wait(pe, (l, i))
                    prep_read.wait(pe, (l, "rope", 4 + i))
                    for t in range(4):
                        mm = pe.transpose(bank[6 + i][:, t * P:(t + 1) * P], chunk(XS + i)[:, t * P:(t + 1) * P], const("ident"))
                elif step == "tok":
                    prepared.wait(pe, (l, "dt", 0))
                    for t in range(4):
                        pe.transpose(bank[4][:, t * 16:t * 16 + 8], dt_t[:, t * P:(t + 1) * P], const("ident")[0:8, 0:8])
                        mm = pe.transpose(bank[4][:, t * 16 + 8:t * 16 + 16], da_t[:, t * P:(t + 1) * P], const("ident")[0:8, 0:8])
                elif step == "cum":
                    prepared.wait(pe, (l, "tok", 0))
                    act_prepared.wait(pe, (l, "swap", 0))
                    for st in range(2):
                        n_mm = 0
                        for j in range(2):
                            for src, tri in ((tokf, "trif"), (tokb, "trib")):
                                strip = const(tri)[:, P - j * P:P - j * P + LAT]
                                mm = pe.matmul(bank[5][0:8, st * LAT:(st + 1) * LAT], src[:, 2 * st + j, :], strip,
                                               start=(n_mm == 0), stop=(n_mm == 3))
                                n_mm += 1
                elif step == "tot":
                    prepared.wait(pe, (l, "x", 0))
                    for j in range(2):
                        mm = pe.matmul(bank[6][:, 0:8], const("ones"), tok[:, 2 + j, 8:16], start=(j == 0), stop=(j == 1))
                elif step == "cumtok":
                    prepared.wait(pe, (l, "cum", 0))
                    for t in range(4):
                        mm = pe.transpose(bank[4][:, t * 8:t * 8 + 8], dt_t[:, t * P:(t + 1) * P], const("ident")[0:8, 0:8])
                else:
                    return
                prep_done.done(mm, (l, step, i))

            start_loads.wait(pe, "all")
            const_loads.wait(pe, "all")
            for l in range(LAYERS):
                pe.transpose(bank[0][:, l * P:(l + 1) * P], pack1[:, l, :], const("ident"))
            for l in range(LAYERS):
                mm = pe.transpose(bank[0][:, 256 + l * PACK2:256 + (l + 1) * PACK2], pack2[:, l, :], const("ident")[0:PACK2, 0:PACK2])
            pe_start.done(mm, "packs")
            pack_loads.wait(pe, "all")
            for k in range(DC):
                if k >= 3:
                    start_copied.wait(pe, ("x", k - 3))
                for t in range(4):
                    mm = pe.transpose(bank[1 + k % 3][:, t * P:(t + 1) * P], x_in[:, t, k * P:(k + 1) * P], const("ident"))
                pe_start.done(mm, ("x", k))

            for l in range(LAYERS):
                last_layer = l == LAYERS - 1
                if l == 0:
                    for k in range(DC):
                        sum_square((0, 1), TOK, k)
                    cond_ready.wait(pe, "c")
                    cleared.wait(pe, "all")

                    def mod_turn(i):
                        for j in range(4):
                            u, ii, per = at(first["mod"], j, i)
                            modulation(u, ii, (4, 4) if per[0] else per, j, None if isinstance(i, int) and i == 0 else i)
                    turns(pe, MOD_FIRST // 4, mod_turn)
                    turn_modulation(0, 0)

                for part in range(len(PARTS)):
                    up(l, 1, part, TOK)
                    down(l, 1, part, TOK)

                u0 = first["in", l]
                for pos, c in enumerate(IN_ORDER):
                    if pos >= 4:
                        projected.wait(pe, (l, IN_ORDER[pos - 4]))
                    product(u0 + pos, 0, (0, 0), bank[pos % 4][:, 0:in_tokens(l, c)], DC, h_rhs(in_tokens(l, c)),
                            (lambda k: h_made.wait(pe, (l, "mix", k))) if pos == 0 else None)
                    for step, i in PREP.get(pos, ()):
                        prepare(l, step, i)

                tasks = attention_tasks(last_layer)
                n_tasks = len(tasks)

                n = tokens(l, "q")

                def mix(job):
                    br, h, st, _ = tasks[2 * job]
                    if job >= 1:
                        y_stored.wait(pe, (l, job - 1))
                    turned_copied.wait(pe, (l, 2 * job + 1))
                    row = HD * (h % 2)
                    v0 = value_column(br, h)
                    tiles = range(4) if st == 0 else range(2, 4)
                    for t in tiles:
                        mm = pe.matmul(bank[4][row:row + HD, 0:LAT], v_tok[:, t, v0:v0 + HD], turned_probs[job % 2][:, t, :],
                                       start=(t == tiles[0]), stop=(t == tiles[-1]))
                    mixed.done(mm, (l, job))

                def spread_sums(h, r):
                    if h > 0 or r > 0:
                        spread.wait(pe, (l, h - 1 + r, 1 - r))
                    mm = pe.matmul(bank[6][:, :], const("sel")[0:8, (4 * r + h) * P:(4 * r + h + 1) * P], dt_t[:, :],
                                   start=True, stop=True)
                    cum_spread.done(mm, (l, h, r))

                for t in range(n_tasks + 5):
                    head = spread_head(first_part(last_layer, t))
                    if t == 0:
                        projected.wait(pe, (l, IN_ORDER[-1]))
                        act_prepared.wait(pe, (l, "swap", 0))
                        prepared.wait(pe, (l, "cumtok", 0))
                    if head is not None:
                        spread_sums(head, 0)
                    if t < n_tasks:
                        br, h, st, qt = tasks[t]
                        if t >= 2:
                            exped.wait(pe, (l, t - 2))
                        row = HD * (h % 2)
                        q = chunk((AQ, BQ, CQ)[br] + h // 2)[row:row + HD, st * LAT + qt * P:st * LAT + (qt + 1) * P]
                        if br == 1:
                            k = chunk(BK + h // 2)
                        elif h // 2 == h % 2:
                            k = chunk((AK, None, CK)[br])
                        else:
                            k = k_swap[:, br // 2]
                        keys = slice(0, TOK) if st == 0 else slice(LAT, TOK)
                        mm = pe.matmul(bank[t % 2][:, 0:TOK - keys.start], q, k[row:row + HD, keys], start=True, stop=True)
                        scored.done(mm, (l, t))
                    if 2 <= t < n_tasks + 2:
                        s = t - 2
                        if s >= 2:
                            turned_copied.wait(pe, (l, s - 2))
                        normalised.wait(pe, (l, s))
                        for kt in range(4 if tasks[s][2] == 0 else 2):
                            mm = pe.transpose(bank[2 + s % 2][:, kt * P:(kt + 1) * P], probs[:, s % 2, kt * P:(kt + 1) * P], const("ident"))
                        turned.done(mm, (l, s))
                    if t % 2 == 0 and 0 <= (t - 4) // 2 < n_tasks // 2:
                        mix((t - 4) // 2)
                    slot = second_part(last_layer, t)
                    head = spread_head(slot)
                    if head is not None:
                        spread_sums(head, 1)
                    found = source_step(behind(slot, 1))
                    if found:
                        step, h, s = found
                        nn = n if s >= 2 else LAT
                        if step > 0:
                            weighed.wait(pe, (l, step - 1))
                        g = h // 2
                        mm = pe.matmul(bank[5][:, 0:nn], chunk(SB_ + g)[:, s * P:(s + 1) * P], chunk(SC_ + g)[:, 0:nn], start=True, stop=True)
                        cb_done.done(mm, (l, step))
                    found = source_step(behind(slot, 2))
                    if found:
                        step, h, s = found
                        nn = n if s >= 2 else LAT
                        if step == 8:
                            ssm_read.wait(pe, (l, "y", 0))
                        weighed.wait(pe, (l, step))
                        row = HD * (h % 2)
                        mm = pe.matmul(bank[7][row:row + HD, 0:nn], x_tok[:, s, h * HD:(h + 1) * HD], weighed_by[step % 2][:, 0:nn],
                                       start=(step % 4 == 0), stop=(step % 4 == 3))
                        ssm_done.done(mm, (l, step))
                for g in range(2):
                    squares.wait(pe, (l, "ssm", g))
                    mm = pe.matmul(bank[6][:, 0:n], const("ones"), wa[:, g, 0:n], start=(g == 0), stop=(g == 1))
                prep_done.done(mm, (l, "ssm"))

                u0 = first["merge", l]
                g0 = l * 4 * DC
                turned_copied.wait(pe, (l, n_tasks - 1))

                def merge_turn(d):
                    straight = isinstance(d, int)
                    for k in range(4):
                        if not (straight and d == 0):
                            pe.wait_ge(gated, d * 4 + (g0 + k - 3))
                        u, ii, per = at(u0, k, d)
                        product(u, ii, per, bank[k][:, 0:n], DC, h_rhs(n), signal_it=False)
                        if straight and d == 0:
                            y_made.wait(pe, (l, 2 * k + 1))
                            if k == 0:
                                y_stored.wait(pe, (l, n_tasks // 2 - 1))
                            if k == 2:
                                roots.wait(pe, (l, "ssm"))
                        product(u, ii, per, bank[4 + k][:, 0:n], 2, lambda c: (y_hi[:, 2 * k + c, 0:n], y_lo[:, 2 * k + c, 0:n]),
                                row0=DC)
                turns(pe, DC, merge_turn)

                u0, a0 = first["out", l], add_first[l, "out"]
                for d in range(DC):
                    pe.wait_ge(added, a0 + d - 1)
                    if d == 0:
                        pe.wait_ge(gated, g0 + 4 * DC)
                    product(u0 + d, 0, (0, 0), bank[4 + d % 2][:, 0:n], DC, h_rhs(n),
                            (lambda k: h_made.wait(pe, (l, "merged", k))) if d == 0 else None)
                    between(l, "out", d)

                n = tokens(l, "ffn2")
                for part in range(len(PARTS)):
                    up(l, 2, part, n)
                    down(l, 2, part, n)

            for t in range(2):
                for half in range(2):
                    for k in range(4 * half, 4 * half + 4):
                        if t == 0:
                            normed.wait(pe, ("final", k))
                        mm = pe.transpose(bank[2 * t + half][:, (k % 4) * P:(k % 4 + 1) * P], X[:, k, t * P:(t + 1) * P], const("ident"))
                    pe_start.done(mm, ("out", t, half))

        @block.scalar
        def _(act):
            def square(key, n, k):
                if k >= 2:
                    sums.wait(act, (key, k - 2))
                squares.done(act.activation(wa[:, k % 2, 0:n], X[:, k, 0:n], ACT.Square), (key, k))

            def root(key, psum_signal, step, psum, dst, scale):
                psum_signal.wait(act, step)
                roots.done(act.activation(dst, psum, ACT.Sqrt, bias=eps_col[0:psum.shape[0], 0:1], scale=scale), key)

            def norm_block(l, which, n, mod_i):
                root((l, which), sums, ((l, which), DC - 1), bank[6][:, 0:n], rstd[:, 0:n], 1.0 / D)
                vectors.wait(act, (l, min(mod_i, 1)))
                for k in range(DC):
                    normed.wait(act, (l, which, k))
                    for st in streams(n):
                        cols = slice(st * LAT, (st + 1) * LAT)
                        ins = act.activation(h_hi[:, k, cols], wa[:, k % 2, cols], ACT.Identity,
                                             bias=mod[:, 3 * mod_i * DC + k, st:st + 1])
                    h_hi_made.done(ins, (l, which, k))

            def up(l, ffn, part, n):
                u0, c0 = first["up", l, ffn, part], inner_first[l, ffn, part]
                n0 = units[u0].product

                step = step_of(l, ffn, part)

                def body(i):
                    straight = isinstance(i, int)
                    for j in range(4):
                        _, ii, per = at(u0, j, i, step)
                        c = c0 + j // 2
                        if step == 2 and j == 3:
                            copy_modulation(u0 + 7 + i * 8, i + mod_first[l, ffn, part])
                        split_hi(act, n0 + j + 2 + (4 * i if straight else 0), ii, per)
                        if j % 2 == 0:
                            act.wait_ge(unit_done, u0 + step * (j + 1) + i * (4 * step))
                            if not (straight and c + 2 * i < 2):
                                act.wait_ge(inner_made, i * 2 + (c - 1))
                            act.activation(wa[:, (j // 2) % 2, 0:n], bank[j][:, 0:n], ACT.Silu).then_inc(silu_done, 1)
                        if j % 2 == 1:
                            act.wait_ge(inner_made, i * 2 + (c + 1))
                            act.activation(inner_hi[:, bass.ds(i * 2 + j // 2, 1), 0:n], wb[:, (j // 2) % 2:(j // 2) % 2 + 1, 0:n],
                                           ACT.Copy).then_inc(inner_hi_made, 1)
                turns(act, PARTS[part][1] // 2, body)

            def copy_modulation(done, m):
                act.wait_ge(unit_done, done)
                if not (isinstance(m, int) and m == 0):
                    act.wait_ge(mod_stored, m * 32)
                act.activation(mod_row[:, :], bank[7][:, :], ACT.Copy).then_inc(mod_copied, 1)

            def block_splits(l, name, u0):
                key, n = next_norm(l, name)
                for d in range(DC):
                    if key and d == 0:
                        act.activation(early_root[:, n_roots[key]:n_roots[key] + 1], eps_col[:, 0:1], ACT.Sqrt)
                    split_hi(act, units[u0].product + d + 2)
                    if key:
                        act.wait_ge(added, add_first[l, name] + d + 1)
                        square(key, n, d)

            def prepare(l, step, i):
                if step == "square":
                    c = NORMED[i]
                    n = in_tokens(l, c)
                    projected.wait(act, (l, c))
                    if i >= 2:
                        prep_done.wait(act, (l, "qk", i - 2))
                    squares.done(act.activation(wa[:, i % 2, 0:n], chunk(c)[:, 0:n], ACT.Square), (l, "qk", i))
                elif step == "qk":
                    n = in_tokens(l, NORMED[i])
                    prep_done.wait(act, (l, "qk", i))
                    if i >= 1:
                        prepared.wait(act, (l, "qk", i - 1))
                    act_read.done(act.activation(rstd[:, 0:n], bank[5][:, 0:n], ACT.Sqrt, bias=eps_col[:, 0:1], scale=1.0 / HD), (l, "qk", i))
                elif step == "swap":
                    prep_done.wait(act, (l, "swap", i))
                    act_prepared.done(act.activation(k_swap[:, i, :], bank[5][:, :], ACT.Copy), (l, "swap", i))
                elif step == "conv" and i > 0 or step == "convend":
                    j = i if step == "convend" else i - 1
                    m = in_tokens(l, XS + j)
                    convolved.wait(act, (l, j))
                    conv_out.done(act.activation(chunk(XS + j)[:, 0:m], wb[:, j % 2, 0:m], ACT.Silu,
                                                 bias=vec2[:, l, V_CONVB + j:V_CONVB + j + 1]), (l, j))
                elif step == "dt":
                    prep_done.wait(act, (l, "dt", 0))
                    prep_done.wait(act, (l, "qk", 2))
                    act_link(act, act.activation(wa[0:8, 0, :], bank[4][0:8, :], ACT.Identity, bias=dtv[:, 0:1]))
                    act_link(act, act.activation(dt_t[:, :], wa[0:8, 0, :], ACT.Abs))
                    act_link(act, act.activation(dt_t[:, :], dt_t[:, :], ACT.Exp, scale=-1.0))
                    act_link(act, act.activation(dtv[:, 2:3], dtv[:, 1:2], ACT.Exp))
                    soft.done(act.activation(da_t[:, :], dt_t[:, :], ACT.Ln, bias=const("ones")[0:8, 0:1]), (l, "dt"))

            const_loads.done(act.dma_start(cst[:, :], consts), "all")
            pack_loads.done(act.dma_start(x_in[:, 0:2, :], x[0].rearrange("(t p) d -> p t d", p=P)))
            pack_loads.done(act.dma_start(x_in[:, 2:4, :], ctx_tokens[0].rearrange("(t p) d -> p t d", p=P)), "all")
            cleared.wait(act, "all")
            pe_start.wait(act, "packs")
            act_link(act, act.activation(vec1[:, :, :], bank[0][:, 0:2 * P].rearrange("p (l r) -> p l r", l=LAYERS), ACT.Copy))
            start_copied.done(act.activation(vec2[:, :, :], bank[0][:, 256:256 + 2 * PACK2].rearrange("p (l r) -> p l r", l=LAYERS),
                                             ACT.Copy), "packs")
            start_copied.wait(act, "packs")
            cleared.wait(act, "all")
            act_link(act, act.activation(cact[:, :, 0], vec2[:, 0, V_C:V_C + DC], ACT.Silu))
            cond_ready.done(act.activation(cact[:, :, 1], vec2[:, 0, V_CC:V_CC + DC], ACT.Silu), "c")
            for k in range(DC):
                pe_start.wait(act, ("x", k))
                start_copied.done(act.activation(X[:, k, :], bank[1 + k % 3][:, :], ACT.Copy), ("x", k))

            for l in range(LAYERS):
                last_layer = l == LAYERS - 1
                if l == 0:
                    start_copied.wait(act, ("x", DC - 1))
                    for k in range(DC):
                        square((0, 1), TOK, k)
                    turns(act, MOD_FIRST // 4, lambda i: copy_modulation(first["mod"] + 4 + i * 4, i))
                    for s in range(2):
                        split_hi(act, s)
                norm_block(l, 1, TOK, 0)
                for part in range(len(PARTS)):
                    up(l, 1, part, TOK)
                    block_splits(l, (1, part), first["down", l, 1, part])

                norm_block(l, "mix", TOK, 1)
                layer_loads.wait(act, l)
                act_prepared.done(act.activation(wdt_hi[:, :, :], wdt_raw[:, :, :], ACT.Copy), (l, "wdt_hi"))
                u0 = first["in", l]
                for pos, c in enumerate(IN_ORDER):
                    n = in_tokens(l, c)
                    split_hi(act, units[u0 + pos].product + 2)
                    act.wait_ge(unit_done, u0 + pos + 1)
                    src = bank[pos % 4][:, 0:n]
                    if XS <= c < XS + 6:
                        i = c - XS
                        if i >= 2:
                            convolved.wait(act, (l, i - 2))
                        else:
                            pads_cleared.wait(act, l)
                        ins = act.activation(padded[i % 2][:, 0:n // LAT, 2:2 + LAT], src.rearrange("p (s t) -> p s t", t=LAT), ACT.Copy)
                    else:
                        ins = act.activation(chunk(c)[:, 0:n], src, ACT.Silu if c in (Z, Z + 1) else ACT.Copy)
                    projected.done(ins, (l, c))
                    for step, i in PREP.get(pos, ()):
                        prepare(l, step, i)
                n = tokens(l, "q")

                tasks = attention_tasks(last_layer)
                n_tasks = len(tasks)

                def store_y(job):
                    br, h, st, _ = tasks[2 * job]
                    row = HD * (h % 2)
                    mixed.wait(act, (l, job))
                    y_stored.done(act.activation(chunk((AQ, BQ, CQ)[br] + h // 2)[row:row + HD, st * LAT:(st + 1) * LAT],
                                                 bank[4][row:row + HD, 0:LAT], ACT.Copy), (l, job))

                def copy_spread(h, r):
                    cum_spread.wait(act, (l, h, r))
                    if h > 0:
                        decay_arg.wait(act, (l, 4 * h - 1, r))
                    spread.done(act.activation(wa[:, r, :], bank[6][:, :], ACT.Copy), (l, h, r))

                for t in range(n_tasks + 5):
                    slot = first_part(last_layer, t)
                    head = spread_head(slot)
                    if head is not None:
                        copy_spread(head, 0)
                    found = source_step(slot)
                    if found:
                        step, h, s = found
                        if step >= 2:
                            weighed.wait(act, (l, step - 2))
                        if s >= 2:
                            spread.wait(act, (l, h, 1))
                            for r, dst in enumerate((decay_f, decay_b)):
                                decayed.done(act.activation(dst[step % 2][:, 0:LAT], wa[:, r, 0:LAT], ACT.Exp,
                                                            bias=tct[:, s % 2, 4 * r + h:4 * r + h + 1]), (l, step))
                    if t < n_tasks:
                        br, h, st, qt = tasks[t]
                        s = t % 2
                        nk = TOK if st == 0 else CTX
                        bounded.wait(act, (l, t))
                        if t >= 2:
                            turned.wait(act, (l, t - 2))
                        ins = act.activation(probs[:, s, 0:nk], bank[s][:, 0:nk], ACT.Exp, bias=smax[:, s, 1:2], scale=SCALE, accum_out=smax[:, s, 2:3])
                        if br == 0:
                            sunk.done(act.activation(smax[:, s, 3:4], sink8[:, h:h + 1], ACT.Exp, bias=smax[:, s, 1:2], scale=SCALE), (l, t))
                        exped.done(ins, (l, t))
                    if 2 <= t < n_tasks + 2:
                        s = t - 2
                        _, _, st, qt = tasks[s]
                        turned.wait(act, (l, s))
                        if s // 2 >= 2:
                            mixed.wait(act, (l, s // 2 - 2))
                        k0 = 0 if st == 0 else 2
                        turned_copied.done(act.activation(turned_probs[s // 2 % 2][:, k0:4, qt * P:(qt + 1) * P],
                                                          bank[2 + s % 2][:, 0:(4 - k0) * P].rearrange("p (k q) -> p k q", q=P), ACT.Copy), (l, s))
                    if t % 2 == 1 and 0 <= (t - 5) // 2 < n_tasks // 2:
                        store_y((t - 5) // 2)
                    slot = second_part(last_layer, t)
                    head = spread_head(slot)
                    if head is not None:
                        copy_spread(head, 1)
                    found = source_step(slot)
                    if found:
                        step, h, s = found
                        st = s // 2
                        if not (last_layer and st == 1):
                            for r, dst in enumerate((decay_f, decay_b)):
                                decay_arg.wait(act, (l, step, r))
                                decayed.done(act.activation(dst[step % 2][:, st * LAT:(st + 1) * LAT],
                                                            wb[:, r, (step % 2) * LAT:(step % 2 + 1) * LAT], ACT.Exp), (l, step))
                        decayed.mark((l, step))

                for g in range(2):
                    skipped.wait(act, (l, g))
                    squares.done(act.activation(wa[:, g, 0:n], chunk(Z + g)[:, 0:n], ACT.Square), (l, "ssm", g))

                weighed.wait(act, (l, 15))
                y_stored.wait(act, (l, n_tasks // 2 - 1))
                for b, c in enumerate(QCHUNKS):
                    if b == 2:
                        root((l, "ssm"), prep_done, (l, "ssm"), bank[6][:, 0:n], rstd[:, 0:n], 1.0 / 256)
                    if c == Z:
                        ssm_out.wait(act, (l, 1))
                    y_hi_made.done(act.activation(y_hi[:, b, 0:n], chunk(c)[:, 0:n], ACT.Copy), (l, b))

                u0 = first["merge", l]
                n0, g0 = units[u0].product, l * 4 * DC

                def merge_turn(d):
                    straight = isinstance(d, int)
                    for k in range(4):
                        _, ii, per = at(u0, k, d)
                        split_hi(act, n0 + k + 2 + (4 * d if straight else 0), ii, per)
                        act.wait_ge(unit_done, u0 + k + 1 + d * 4)
                        if not (straight and d == 0 and k < 2):
                            act.wait_ge(gated, d * 4 + (g0 + k - 1))
                        act.activation(wa[:, k % 2, 0:n], bank[k][:, 0:n], ACT.Sigmoid,
                                       bias=vec1[:, l, bass.ds(d + (V_BGATE + k * DC), 1)]).then_inc(gate_done, 1)
                turns(act, DC, merge_turn)

                for k in range(DC):
                    act.wait_ge(branch_added, 3 * (l * DC + k + 1))
                    if k == 0:
                        act.wait_ge(unit_done, first["out", l])
                    h_hi_made.done(act.activation(h_hi[:, k, 0:n], Q[:, k, 0:n], ACT.Copy), (l, "merged", k))
                block_splits(l, "out", first["out", l])

                n = tokens(l, "ffn2")
                norm_block(l, 2, n, 2)
                for part in range(len(PARTS)):
                    up(l, 2, part, n)
                    block_splits(l, (2, part), first["down", l, 2, part])

            root("final", sums, (("final", 0), DC - 1), bank[6][:, 0:LAT], rstd[:, 0:LAT], 1.0 / D)
            for t in range(2):
                for half in range(2):
                    pe_start.wait(act, ("out", t, half))
                    ins = act.activation(out_rows[:, t, half * 512:(half + 1) * 512], bank[2 * t + half][:, :], ACT.Copy)
                    start_copied.done(ins, ("out", t))

        @block.vector
        def _(dve):
            def link(ins):
                dve_link(dve, ins)

            def split_h(key, n, source, k):
                h_hi_made.wait(dve, (*key, k))
                h_made.done(dve.tensor_tensor(h_lo[:, k, 0:n], source, h_hi[:, k, 0:n].bitcast(F32), ALU.subtract), (*key, k))

            def norm_block(l, which, n, mod_i):
                key = (l, which)
                roots.wait(dve, key)
                link(dve.reciprocal(rstd[:, 0:n], rstd[:, 0:n]))
                for k in range(DC + 1):
                    if k < DC:
                        if k >= 2:
                            h_hi_made.wait(dve, (l, which, k - 2))
                            h_made.wait(dve, (l, which, k - 2))
                        for st in streams(n):
                            cols = slice(st * LAT, (st + 1) * LAT)
                            ins = dve.scalar_tensor_tensor(out=wa[:, k % 2, cols], in0=X[:, k, cols], scalar=gain[:, mod_i, k, st:st + 1],
                                                           in1=rstd[:, cols], op0=ALU.mult, op1=ALU.mult)
                        normed.done(ins, (l, which, k))
                    if k >= 1:
                        j = k - 1
                        normed.wait(dve, (l, which, j))
                        h_hi_made.wait(dve, (l, which, j))
                        for st in streams(n):
                            cols = slice(st * LAT, (st + 1) * LAT)
                            ins = dve.scalar_tensor_tensor(out=h_lo[:, j, cols], in0=wa[:, j % 2, cols],
                                                           scalar=mod[:, 3 * mod_i * DC + j, st:st + 1],
                                                           in1=h_hi[:, j, cols].bitcast(F32), op0=ALU.add, op1=ALU.subtract)
                        h_made.done(ins, (l, which, j))

            def up(l, ffn, part, n):
                u0, c0 = first["up", l, ffn, part], inner_first[l, ffn, part]
                n0 = units[u0].product

                step = step_of(l, ffn, part)

                def body(i):
                    straight = isinstance(i, int)
                    for j in range(4):
                        _, ii, per = at(u0, j, i, step)
                        c = c0 + j // 2
                        b = (j // 2) % 2
                        split_lo(dve, n0 + j + 2 + (4 * i if straight else 0), ii, per)
                        if j % 2 == 1:
                            dve.wait_ge(unit_done, u0 + step * (j + 1) + i * (4 * step))
                            dve.wait_ge(silu_done, i * 2 + (c + 1))
                            if not (straight and c + 2 * i < 2):
                                dve.wait_ge(inner_lo_made, i * 2 + (c - 1))
                            dve.tensor_tensor(wb[:, b, 0:n], bank[j][:, 0:n], wa[:, b, 0:n], ALU.mult).then_inc(inner_made, 1)
                        if j % 2 == 1:
                            dve.wait_ge(inner_hi_made, i * 2 + (c + 1))
                            at_chunk = bass.ds(i * 2 + j // 2, 1)
                            dve.tensor_tensor(inner_lo[:, at_chunk, 0:n], wb[:, b:b + 1, 0:n],
                                              inner_hi[:, at_chunk, 0:n].bitcast(F32), ALU.subtract).then_inc(inner_lo_made, 1)
                turns(dve, PARTS[part][1] // 2, body)

            def add_block(l, name, u0, n, gate_i):
                for d in range(DC):
                    split_lo(dve, units[u0 + d].product + 2)
                    dve.wait_ge(unit_done, u0 + d + 1)
                    for st in streams(n):
                        cols = slice(st * LAT, (st + 1) * LAT)
                        ins = dve.scalar_tensor_tensor(out=X[:, d, cols], in0=bank[4 + d % 2][:, cols], scalar=gatev[:, gate_i, d, st:st + 1],
                                                       in1=X[:, d, cols], op0=ALU.mult, op1=ALU.add)
                    ins.then_inc(added, 1)
                    if d == TURN_AT:
                        for args in next_modulation(l, name):
                            modulation_vectors(*args)

            def modulation_vectors(l, half):
                start_copied.wait(dve, "packs")
                mod_turned.wait(dve, (l, half))
                if l > 0 and half == 0:
                    dve.wait_ge(added, add_first[l - 1, (1, 2)] + DC)
                r0, r1 = ((0, MOD_EARLY), (MOD_EARLY, MOD_CHUNKS))[half]
                for s in range(2):
                    link(dve.tensor_tensor(mod[:, r0:r1, s], bank[7][:, s * MOD_CHUNKS + r0:s * MOD_CHUNKS + r1],
                                           vec1[:, l, V_BMOD + r0:V_BMOD + r1], ALU.add))
                for i in ((0,), (1, 2))[half]:
                    for s in range(2):
                        link(dve.scalar_tensor_tensor(out=gain[:, i, :, s], in0=mod[:, (3 * i + 1) * DC:(3 * i + 2) * DC, s], scalar=1.0,
                                                      in1=vec1[:, l, V_NORM + i * DC:V_NORM + (i + 1) * DC], op0=ALU.add, op1=ALU.mult))
                    ins = dve.tensor_scalar(gatev[:, i, :, :], mod[:, (3 * i + 2) * DC:(3 * i + 3) * DC, :],
                                            1.0 if i == 1 else 0.5, None, ALU.mult)
                vectors.done(ins, (l, half))
                vectors.wait(dve, (l, half))

            def prepare(l, step, i):
                if step in ("v", "rope", "x", "tok", "cum", "tot", "cumtok"):
                    prep_done.wait(dve, (l, step, i))
                if step == "conv":
                    nn = in_tokens(l, XS + i)
                    projected.wait(dve, (l, XS + i))
                    if i >= 2:
                        conv_out.wait(dve, (l, i - 2))
                    acc = wb[:, i % 2, 0:nn].rearrange("p (s t) -> p s t", t=LAT)
                    for j in range(CONV):
                        src = padded[i % 2][:, 0:nn // LAT, j:j + LAT]
                        w = vec2[:, l, V_CONVW + 6 * j + i:V_CONVW + 6 * j + i + 1]
                        if j == 0:
                            ins = dve.tensor_scalar(acc, src, w, None, ALU.mult)
                        else:
                            ins = dve.scalar_tensor_tensor(out=acc, in0=src, scalar=w, in1=acc, op0=ALU.mult, op1=ALU.add)
                        if j < CONV - 1:
                            link(ins)
                    convolved.done(ins, (l, i))
                elif step == "qk":
                    c = NORMED[i]
                    n = in_tokens(l, c)
                    act_read.wait(dve, (l, "qk", i))
                    link(dve.reciprocal(rstd[:, 0:n], rstd[:, 0:n]))
                    g = V_KG if c == CK else V_QG
                    prepared.done(dve.scalar_tensor_tensor(out=chunk(c)[:, 0:n], in0=chunk(c)[:, 0:n], scalar=vec2[:, l, g:g + 1],
                                                           in1=rstd[:, 0:n], op0=ALU.mult, op1=ALU.mult), (l, "qk", i))
                elif step == "rope":
                    if i == 0:
                        conv_out.wait(dve, (l, 5))
                    if i >= 2:
                        prepared.wait(dve, (l, "rope", i - 2))
                    lat = chunk(ROTATED[i])[:, 0:LAT]
                    work = wb[:, i % 2, 0:LAT]
                    prep_read.done(dve.tensor_tensor(work, bank[6 + i % 2][:, 0:LAT], const("ropes"), ALU.mult), (l, "rope", i))
                    link(dve.tensor_tensor(lat, lat, const("ropec"), ALU.mult))
                    prep_read.wait(dve, (l, "rope", i))
                    prepared.done(dve.tensor_tensor(lat, lat, work, ALU.add), (l, "rope", i))
                elif step == "v":
                    prep_read.done(dve.tensor_copy(v_tok[:, :, i * P:(i + 1) * P], bank[5][:, :].rearrange("p (t f) -> p t f", t=4)), (l, "v", i))
                elif step == "dt":
                    soft.wait(dve, (l, "dt"))
                    link(dve.scalar_tensor_tensor(out=dt_t[:, :], in0=wa[0:8, 0, :], scalar=0.0, in1=da_t[:, :], op0=ALU.max, op1=ALU.add))
                    prepared.done(dve.tensor_scalar(da_t[:, :], dt_t[:, :], dtv[:, 2:3], -1.0, ALU.mult, ALU.mult), (l, "dt", 0))
                elif step == "x":
                    prepared.done(dve.tensor_copy(x_tok[:, :, i * P:(i + 1) * P], bank[6 + i][:, :].rearrange("p (t f) -> p t f", t=4)), (l, "x", i))
                elif step == "tok":
                    link(dve.tensor_copy(tok[:, :, :], bank[4][:, 0:64].rearrange("p (t r) -> p t r", t=4)))
                    dve.tensor_copy(tokf[:, :, 0:4], tok[:, :, 8:12])
                    prepared.done(dve.tensor_copy(tokb[:, :, 4:8], tok[:, :, 12:16]), (l, "tok", 0))
                elif step == "cum":
                    prepared.done(dve.tensor_copy(dt_t[:, :], bank[5][0:8, :]), (l, "cum", 0))
                elif step == "tot":
                    link(dve.tensor_copy(tot[:, :], bank[6][:, 0:8]))
                elif step == "cumtok":
                    link(dve.tensor_scalar(nct[:, :, :], bank[4][:, 0:32].rearrange("p (t r) -> p t r", t=4), -1.0, None, ALU.mult))
                    for j in range(2):
                        ins = dve.tensor_tensor(tct[:, j, :], tot[:, :], nct[:, 2 + j, :], ALU.add)
                    prepared.done(ins, (l, "cumtok", 0))

            start_loads.wait(dve, "all")
            for l in range(LAYERS):
                for g in range(2):
                    for half in range(2):
                        rows = slice(half * HD, (half + 1) * HD)
                        head = 4 * l + 2 * g + half
                        ins = dve.tensor_copy(skip_w[rows, l, g:g + 1], skip_all[rows, head:head + 1])
            link(ins)
            for l in range(LAYERS):
                last_layer = l == LAYERS - 1
                nq = tokens(l, "q")
                if l == 0:
                    for s in range(2):
                        split_lo(dve, s)
                    modulation_vectors(0, 0)

                norm_block(l, 1, TOK, 0)
                for part in range(len(PARTS)):
                    up(l, 1, part, TOK)
                    add_block(l, (1, part), first["down", l, 1, part], TOK, 0)

                norm_block(l, "mix", TOK, 1)
                act_prepared.wait(dve, (l, "wdt_hi"))
                prepared.done(dve.tensor_tensor(wdt_lo[:, :, :], wdt_raw[:, :, :], wdt_hi[:, :, :].bitcast(F32), ALU.subtract), (l, "wdt"))
                u0 = first["in", l]
                for i in range(2):
                    ins = dve.memset(padded[i][:, :, 0:2], 0.0)
                    ins = dve.memset(padded[i][:, :, 2 + LAT:4 + LAT], 0.0)
                pads_cleared.done(ins, l)
                for pos in range(IN_CHUNKS):
                    split_lo(dve, units[u0 + pos].product + 2)
                    for step, i in PREP.get(pos, ()):
                        prepare(l, step, i)
                layer_loads.wait(dve, l)
                link(dve.tensor_scalar(sink8[:, :], sink8[:, :], BIG, None, ALU.mult))
                bias_ready.wait(dve, l)

                tasks = attention_tasks(last_layer)
                n_tasks = len(tasks)
                for t in range(n_tasks + 5):
                    found = source_step(first_part(last_layer, t))
                    if found:
                        step, h, s = found
                        st, j = s // 2, s % 2
                        spread.wait(dve, (l, h, 1))
                        if step >= 2:
                            decayed.wait(dve, (l, step - 2))
                        for r, mask in enumerate(("maskf", "maskb")):
                            if not (last_layer and st == 1):
                                strip = const(mask)[:, P - j * P:P - j * P + LAT]
                                decay_arg.done(dve.scalar_tensor_tensor(
                                    out=wb[:, r, (step % 2) * LAT:(step % 2 + 1) * LAT], in0=wa[:, r, st * LAT:(st + 1) * LAT],
                                    scalar=nct[:, s, 4 * r + h:4 * r + h + 1], in1=strip, op0=ALU.add, op1=ALU.add), (l, step, r))
                    if t < n_tasks:
                        br, h, st, qt = tasks[t]
                        s = t % 2
                        scored.wait(dve, (l, t))
                        nk = TOK if st == 0 else CTX
                        if br < 2 and st == 0:
                            mask = const("wmask")[:, qt * LAT:(qt + 1) * LAT] if br == 0 else nbias[:, h, qt, :]
                            link(dve.tensor_tensor(bank[s][:, 0:LAT], bank[s][:, 0:LAT], mask, ALU.add))
                        link(dve.reduce_max(smax[:, s, 0:1], bank[s][:, 0:nk], AX_X))
                        if br == 0:
                            ins = dve.tensor_scalar(smax[:, s, 1:2], smax[:, s, 0:1], sink8[:, h:h + 1], -SCALE, ALU.max, ALU.mult)
                        else:
                            ins = dve.tensor_scalar(smax[:, s, 1:2], smax[:, s, 0:1], -SCALE, None, ALU.mult)
                        bounded.done(ins, (l, t))
                    if 1 <= t <= n_tasks:
                        br, h, st, qt = tasks[t - 1]
                        s = (t - 1) % 2
                        nk = TOK if st == 0 else CTX
                        exped.wait(dve, (l, t - 1))
                        if br == 0:
                            sunk.wait(dve, (l, t - 1))
                            link(dve.tensor_tensor(smax[:, s, 2:3], smax[:, s, 2:3], smax[:, s, 3:4], ALU.add))
                        link(dve.reciprocal(smax[:, s, 2:3], smax[:, s, 2:3]))
                        normalised.done(dve.tensor_scalar(probs[:, s, 0:nk], probs[:, s, 0:nk], smax[:, s, 2:3], None, ALU.mult), (l, t - 1))
                    slot = second_part(last_layer, t)
                    found = source_step(behind(slot, 1))
                    if found:
                        step, h, s = found
                        nn = nq if s >= 2 else LAT
                        decayed.wait(dve, (l, step))
                        if step >= 2:
                            ssm_done.wait(dve, (l, step - 2))
                        f, b = decay_f[step % 2][:, 0:nn], decay_b[step % 2][:, 0:nn]
                        link(dve.tensor_scalar(b, b, tok[:, s, 4 + h:5 + h], None, ALU.mult))
                        link(dve.scalar_tensor_tensor(out=f, in0=f, scalar=tok[:, s, h:h + 1], in1=b, op0=ALU.mult, op1=ALU.add))
                        cb_done.wait(dve, (l, step))
                        weighed.done(dve.tensor_tensor(weighed_by[step % 2][:, 0:nn], f, bank[5][:, 0:nn], ALU.mult), (l, step))
                    found = source_step(behind(slot, 3))
                    if found and found[0] % 8 == 7:
                        g = found[0] // 8
                        ssm_done.wait(dve, (l, found[0]))
                        x_g, z_g = chunk(XS + g)[:, 0:nq], chunk(Z + g)[:, 0:nq]
                        ssm_read.done(dve.scalar_tensor_tensor(out=x_g, in0=x_g, scalar=skip_w[:, l, g:g + 1], in1=bank[7][:, 0:nq],
                                                               op0=ALU.mult, op1=ALU.add), (l, "y", g))
                        ssm_read.wait(dve, (l, "y", g))
                        skipped.done(dve.tensor_tensor(z_g, x_g, z_g, ALU.mult), (l, g))
                for b, c in enumerate(QCHUNKS):
                    if b == 2:
                        roots.wait(dve, (l, "ssm"))
                        link(dve.reciprocal(rstd[:, 0:nq], rstd[:, 0:nq]))
                        for g in range(2):
                            z_g = chunk(Z + g)[:, 0:nq]
                            ssm_out.done(dve.scalar_tensor_tensor(out=z_g, in0=z_g, scalar=vec2[:, l, V_SNORM + g:V_SNORM + g + 1],
                                                                  in1=rstd[:, 0:nq], op0=ALU.mult, op1=ALU.mult), (l, g))
                    y_hi_made.wait(dve, (l, b))
                    y_made.done(dve.tensor_tensor(y_lo[:, b, 0:nq], chunk(c)[:, 0:nq], y_hi[:, b, 0:nq].bitcast(F32), ALU.subtract), (l, b))
                y_made.wait(dve, (l, 7))

                u0 = first["merge", l]
                n0, g0 = units[u0].product, l * 4 * DC

                def merge_turn(d):
                    straight = isinstance(d, int)
                    for k in range(4):
                        _, ii, per = at(u0, k, d)
                        split_lo(dve, n0 + k + 2 + (4 * d if straight else 0), ii, per)
                        dve.wait_ge(unit_done, u0 + k + 1 + d * 4)
                        dve.wait_ge(gate_done, d * 4 + (g0 + k + 1))
                        merged = Q[:, bass.ds(d, 1), 0:nq]
                        work = wb[:, k % 2:k % 2 + 1, 0:nq]
                        branch = bank[4 + k][:, 0:nq].unsqueeze(1)
                        gate = wa[:, k % 2:k % 2 + 1, 0:nq]
                        if k == 1 and not (straight and d == 0):
                            dve.wait_ge(branch_added, d * 3 + 3 * l * DC)
                        dve.tensor_tensor(merged if k == 0 else work, gate, branch, ALU.mult).then_inc(gated, 1)
                        if k > 0:
                            dve.wait_ge(gated, d * 4 + (g0 + k + 1))
                            if k > 1:
                                dve.wait_ge(branch_added, d * 3 + (3 * l * DC + k - 1))
                            dve.tensor_tensor(merged, merged, work, ALU.add).then_inc(branch_added, 1)
                turns(dve, DC, merge_turn)
                for k in range(DC):
                    split_h((l, "merged"), nq, Q[:, k, 0:nq], k)
                add_block(l, "out", first["out", l], nq, 1)

                n = tokens(l, "ffn2")
                norm_block(l, 2, n, 2)
                for part in range(len(PARTS)):
                    up(l, 2, part, n)
                    add_block(l, (2, part), first["down", l, 2, part], n, 2)

            roots.wait(dve, "final")
            link(dve.reciprocal(rstd[:, 0:LAT], rstd[:, 0:LAT]))
            for k in range(DC):
                normed.done(dve.scalar_tensor_tensor(out=X[:, k, 0:LAT], in0=X[:, k, 0:LAT], scalar=vec2[:, 0, V_FIN + k:V_FIN + k + 1],
                                                     in1=rstd[:, 0:LAT], op0=ALU.mult, op1=ALU.mult), ("final", k))

        @block.gpsimd
        def _(pool):
            pool.memset(eps_col[:, :], EPS)
            pool.memset(tokf[:, :, :], 0.0)
            pool.memset(tokb[:, :, :], 0.0)
            cleared.done(pool.memset(cact[:, :, :], 0.0), "all")

            def store_modulation(l, chunk0, m):
                pool.wait_ge(mod_copied, m + 1)
                for s in range(2):
                    pool.dma_start(mod_rows[l, s, :, bass.ds(chunk0 * P, 4 * P)], mod_row[s::32, :]).then_inc(mod_stored, 16)

            def load_modulation(l, half, m):
                pool.wait_ge(mod_stored, 32 * m)
                r0, r1 = ((0, MOD_EARLY), (MOD_EARLY, MOD_CHUNKS))[half]
                if half == 1:
                    mod_turned.wait(pool, (l, 0))
                elif l > 0:
                    y_made.wait(pool, (l - 1, 7))
                mod_loads.done(pool.dma_start(scores_flat[0:r1 - r0, :].rearrange("r (q c) -> r q c", c=P),
                                              mod_rows[l].rearrange("s j (r c) -> r (s j) c", c=P)[r0:r1]), (l, half))

            def small_loads(l):
                if l > 0:
                    y_made.wait(pool, (l - 1, 7))
                layer_loads.done(pool.dma_start(sink8[:, :], attn_sink[l:l + 1, :].to_broadcast([P, 4])))
                layer_loads.done(pool.dma_start(dtv[:, 0:1], ssm_dt_bias[l].rearrange("a (b o) -> (a b) o", o=1)))
                layer_loads.done(pool.dma_start(dtv[:, 1:2], ssm_a_log[l].rearrange("a (b o) -> (a b) o", o=1)))
                layer_loads.done(pool.dma_start(wdt_raw[:, :, :], w_in[l].rearrange("(c p) n -> p c n", p=P)[:, :, DT_COL:GATE_COL]), l)
                if l == 0:
                    rows_written.wait(pool, "all")
                for h in range(4):
                    for qr in range(ROWS):
                        t, a = qr // 2, qr % 2
                        src = bass.AP(bias_rows.tensor, bias_rows[l, h, ROWS - 1 - qr, 0, NA_COLS - 1:NA_COLS].offset,
                                      [[P - 1, GRID_W], [GRID_W * P, ROWS], [1, GRID_W]])
                        bias_loads.done(pool.dma_start(
                            nbias[a * GRID_W:(a + 1) * GRID_W, h, t, :].rearrange("p (r c) -> p r c", r=ROWS), src), l)
            for l in range(LAYERS):
                for h in range(4):
                    row = na_rpb[l, h, NA_ROWS - ROWS, 0:1]
                    src = bass.AP(row.tensor, row.offset, [[2 * NA_COLS - 1, 2 * ROWS - 1], [0, GRID_W], [1, P]])
                    rows_written.done(pool.dma_start(bias_rows[l, h], src), "all")
            def neighbourhood_bias(l):
                const_loads.wait(pool, "all")
                bias_loads.wait(pool, l)
                tiles = [(h, t) for h in range(4) for t in range(2)]
                for h, t in tiles:
                    pool_chain.done(pool.tensor_tensor(nbias[:, h, t, :], nbias[:, h, t, :], const("nvalid"), ALU.mult), (l, h, t))
                for h, t in tiles:
                    pool_chain.wait(pool, (l, h, t))
                    bias_ready.done(pool.tensor_tensor(nbias[:, h, t, :], nbias[:, h, t, :], const("nneg"), ALU.add), l)

            small_loads(0)
            with pool.Fori(0, MOD_FIRST // 4) as i:
                store_modulation(0, i * 4, i)
            load_modulation(0, 0, MOD_FIRST // 4)
            neighbourhood_bias(0)
            for key in sorted(MOD_AT):
                l, chunk0 = MOD_AT[key]
                if key == (0, 2, 0):
                    load_modulation(0, 1, mod_first[key])
                if key == (1, 1, 0):
                    load_modulation(1, 0, mod_first[key])
                    small_loads(1)
                    neighbourhood_bias(1)
                m0 = mod_first[key]
                with pool.Fori(0, PARTS[key[2]][1] // 2) as i:
                    store_modulation(l, i * 4 + chunk0, i + m0)
            load_modulation(1, 1, mod_first["end"])


_INS = ['x', 'c', 'ctx', 'c_ctx', 'w_mod', 'b_mod', 'norm_ffn1', 'ffn1_w_gate', 'ffn1_w_up', 'ffn1_w_down',
        'norm_mix', 'w_in', 'b_gate', 'attn_sink', 'na_rpb', 'qk_norm_q', 'qk_norm_k', 'ssm_conv_w', 'ssm_conv_b',
        'ssm_dt_bias', 'ssm_a_log', 'ssm_d', 'ssm_norm', 'w_branch', 'w_out', 'norm_ffn2', 'ffn2_w_gate',
        'ffn2_w_up', 'ffn2_w_down', 'final_norm']
_OUTS = [((1, LAT, D), 'float32')]


def kernel(**inputs):
    import numpy as _np
    import concourse.bacc as _bacc
    from concourse import mybir as _mybir
    from concourse.bass_utils import run_bass_kernel_spmd as _run

    arrays = {f"in_{name}_dram": _np.ascontiguousarray(inputs[name]) for name in _INS}
    arrays["in_consts_dram"] = constants()
    values = {}
    for _ in range(2):
        nc = _bacc.Bacc("TRN2", target_bir_lowering=False, num_devices=1)
        args = [nc.dram_tensor(n, a.shape, _mybir.dt.from_np(a.dtype), kind="ExternalInput").ap() for n, a in arrays.items()]
        for i, (shape, dtype) in enumerate(_OUTS):
            args.append(nc.dram_tensor(f"out_{i}_dram", shape, _mybir.dt.from_np(_np.dtype(dtype)), kind="ExternalOutput").ap())
        build(nc, values, *args)
    r = _run(nc, [arrays], core_ids=[0])
    return r.results[0]["out_0_dram"]
```

```python
from contextlib import ExitStack

import numpy as np

import concourse.bass as bass
from concourse import mybir

F32 = mybir.dt.float32
F32R = mybir.dt.float32r
ALU = mybir.AluOpType
ACT = mybir.ActivationFunctionType
AX_X = mybir.AxisListType.X

P = 128
LAYERS = 2
D = 1024
DC = D // P
LAT, CTX = 256, 256
TOK = LAT + CTX
FF = 2816
HD = 64
EPS = 1e-6
NEG = -1e30
BIG = 8.0
SCALE = HD ** -0.5
GRID_W, NA_ROWS, NA_COLS = 64, 8, 16
ROWS = LAT // GRID_W
CONV = 5
DT_COL = 2816
GATE_COL = DT_COL + 8
MOD_CHUNKS = 9 * DC

AQ, AK, AV, BQ, BK, BV, CQ, CK, CV, Z, XS, SB_, SC_ = 0, 2, 3, 4, 6, 8, 10, 12, 13, 14, 16, 18, 20
IN_CHUNKS = 22
QCHUNKS = [AQ, AQ + 1, BQ, BQ + 1, CQ, CQ + 1, Z, Z + 1]
KCHUNKS = [c for c in range(IN_CHUNKS) if c not in QCHUNKS]
VCHUNKS = [AV, BV, BV + 1, CV]
NORMED = [CQ, CQ + 1, CK]
ROTATED = [CQ, CQ + 1, CK, AQ, AQ + 1, AK]
SWAPPED = [AK, CK]
IN_ORDER = [XS, XS + 1, SB_, SB_ + 1, SC_, SC_ + 1, CQ, CQ + 1, CK, AQ, AQ + 1, AK, AV, BV, BV + 1, CV,
            Z, Z + 1, BQ, BQ + 1, BK, BK + 1]
PREP = {0: [("conv", 0)], 1: [("conv", 1)], 2: [("conv", 2)], 3: [("conv", 3)], 4: [("conv", 4)], 5: [("conv", 5)],
        6: [("convend", 5), ("square", 0)], 7: [("square", 1), ("qk", 0)], 8: [("square", 2), ("qk", 1)],
        9: [("qk", 2), ("rope", 0)], 10: [("rope", 1)], 11: [("rope", 2)], 12: [("rope", 3), ("swap", 1)],
        13: [("rope", 4), ("v", 0)], 14: [("rope", 5), ("v", 1)], 15: [("v", 2), ("dt", 0)], 16: [("v", 3)],
        17: [("x", 0), ("swap", 0), ("tok", 0)], 18: [("x", 1), ("cum", 0)], 19: [("tot", 0), ("cumtok", 0)]}

V_BMOD, V_NORM, V_BGATE = 0, 72, 96
V_CONVW, V_CONVB, V_SNORM, V_QG, V_KG, V_FIN = 0, 30, 36, 38, 39, 40
PACK2 = 48

CONST_COLS = {}
_at = 0
for _name, _w in (("ident", 128), ("ones", 128), ("blockones", 128), ("rot", 128), ("swap", 128), ("trif", 384),
                  ("trib", 384), ("maskf", 384), ("maskb", 384), ("wmask", 512), ("nvalid", 256), ("nneg", 256),
                  ("ropec", 256), ("ropes", 256), ("sel", 1024)):
    CONST_COLS[_name] = (_at, _at + _w)
    _at += _w
CONSTS = _at
FIRST_CONSTS = CONST_COLS["ones"][1]


def constants():
    c = np.zeros((P, CONSTS), np.float32)

    def put(name, a):
        lo, hi = CONST_COLS[name]
        c[:a.shape[0], lo:hi] = a

    p = np.arange(P)[:, None]
    f = np.arange(P)[None, :]
    put("ident", (p == f).astype(np.float32))
    put("ones", np.ones((P, P), np.float32))
    put("blockones", (p // HD == f // HD).astype(np.float32))
    rot = np.zeros((P, P), np.float32)
    for i in range(P):
        if i % 32 < 16:
            rot[i + 16, i] = -1.0
        else:
            rot[i - 16, i] = 1.0
    put("rot", rot)
    put("swap", ((p + HD) % P == f).astype(np.float32))
    q = np.arange(384)[None, :] - P
    put("trif", (q >= p).astype(np.float32))
    put("trib", (q <= p).astype(np.float32))
    put("maskf", np.where(q >= p, 0.0, NEG).astype(np.float32))
    put("maskb", np.where(q <= p, 0.0, NEG).astype(np.float32))
    k = np.arange(LAT)[None, :]
    put("wmask", np.concatenate([np.where(np.abs(t * P + p - k) <= 128, 0.0, NEG) for t in range(2)], 1).astype(np.float32))
    qc, kc = p % GRID_W, k % GRID_W
    start = np.clip(qc - NA_COLS // 2, 0, GRID_W - NA_COLS)
    ok = (kc >= start) & (kc < start + NA_COLS)
    put("nvalid", np.where(ok, BIG, 0.0).astype(np.float32))
    put("nneg", np.where(ok, 0.0, NEG).astype(np.float32))
    pos = np.arange(LAT)
    axes = np.stack([pos // GRID_W, pos % GRID_W], 0).astype(np.float32)
    inv = (np.float32(1.0) / (np.float32(10000.0) ** (np.arange(HD // 4, dtype=np.float32) * np.float32(4.0) / np.float32(HD)))).astype(np.float32)
    ang = np.zeros((P, LAT), np.float32)
    for i in range(P):
        ang[i] = axes[(i % HD) // 32] * inv[i % 16]
    put("ropec", np.cos(ang))
    put("ropes", np.sin(ang))
    sel = np.zeros((8, 8, P), np.float32)
    for r in range(8):
        sel[r, r] = 1.0
    put("sel", sel.reshape(8, 8 * P))
    return c


class Signal:

    def __init__(self, nc, ctx, name, values, by=1):
        self.sem = ctx.enter_context(nc.semaphore(name))
        self.name, self.values, self.by, self.count = name, values, by, 0

    def done(self, ins, step=None):
        ins.then_inc(self.sem, self.by)
        self.count += self.by
        self.values[self.name, step] = self.count

    def mark(self, step):
        self.values[self.name, step] = self.count

    def wait(self, eng, step):
        eng.wait_ge(self.sem, self.values.get((self.name, step), self.by))


class Unit:

    def __init__(self, kind, rows, dmas):
        self.kind, self.rows, self.dmas = kind, rows, dmas


SLOTS = 4
SLOT_ROWS = 10
PARTS = [(0, 8), (8, 8), (16, 6)]
MOD_FIRST = 16
MOD_AT = {(0, 1, 0): (0, 16, 1), (0, 1, 1): (0, 32, 1), (0, 1, 2): (0, 48, 2),
          (0, 2, 0): (1, 0, 1), (0, 2, 1): (1, 16, 1), (0, 2, 2): (1, 32, 1),
          (1, 1, 0): (1, 44, 1), (1, 1, 2): (1, 60, 1)}
PORTIONS = {(0, "in"): (0, 2 * DC, (0,), ()), (0, "gate"): (2 * DC, 3 * DC, (), (0,)), (0, "rest"): (3 * DC, 9 * DC, (1, 2), (1, 2)),
            (1, "in"): (0, 3 * DC, (0,), (0,)), (1, "rest"): (3 * DC, 9 * DC, (1, 2), (1, 2))}


def plan_units():
    units, first = [], {}

    def stage(name, n, kind, rows, dmas=1):
        first[name] = len(units)
        units.extend(Unit(kind, rows, dmas) for _ in range(n))

    for l in range(LAYERS):
        if l == 0:
            stage("mod", MOD_FIRST, "mod", DC)
        for ffn in (1, 2):
            if ffn == 2:
                stage(("in", l), IN_CHUNKS, "product", DC)
                stage(("merge", l), 4 * DC, "product", DC + 2, 2)
                stage(("out", l), DC, "product", DC)
            for part, (_, n) in enumerate(PARTS):
                first["up", l, ffn, part] = len(units)
                for _ in range(2 * n):
                    if (l, ffn, part) in MOD_AT:
                        units.extend(Unit("mod", DC, 1) for _ in range(MOD_AT[l, ffn, part][2]))
                    units.append(Unit("product", DC, 1))
                stage(("down", l, ffn, part), DC, "product", n)
    count, products = [0] * SLOTS, 0
    for u, unit in enumerate(units):
        unit.slot = u % SLOTS
        count[unit.slot] += 16 * unit.dmas
        unit.loaded = count[unit.slot]
        unit.product = products
        products += unit.kind == "product"
    return units, first


def build(nc, values, x, c, ctx_tokens, c_ctx, w_mod, b_mod, norm_ffn1, ffn1_w_gate, ffn1_w_up, ffn1_w_down,
          norm_mix, w_in, b_gate, attn_sink, na_rpb, qk_norm_q, qk_norm_k, ssm_conv_w, ssm_conv_b, ssm_dt_bias,
          ssm_a_log, ssm_d, ssm_norm, w_branch, w_out, norm_ffn2, ffn2_w_gate, ffn2_w_up, ffn2_w_down, final_norm,
          consts, out):
    units, first = plan_units()
    product_units = [u for u, unit in enumerate(units) if unit.kind == "product"]
    ffn_weights = {1: (ffn1_w_gate, ffn1_w_up, ffn1_w_down), 2: (ffn2_w_gate, ffn2_w_up, ffn2_w_down)}

    with ExitStack() as ctx:
        def sb(name, shape, dt=F32, where=ctx):
            return where.enter_context(nc.sbuf_tensor(name, shape, dt))

        def signal(name, by=1):
            return Signal(nc, ctx, name, values, by)

        X = sb("X", [P, DC, TOK])
        h_hi = sb("h_hi", [P, DC, TOK], F32R)
        h_lo = sb("h_lo", [P, DC, TOK], F32R)
        raw = [sb(f"raw{s}", [P, SLOT_ROWS, P]) for s in range(SLOTS)]
        w_hi = [sb(f"w_hi{s}", [P, SLOT_ROWS, P], F32R) for s in range(2)]
        w_lo = [sb(f"w_lo{s}", [P, SLOT_ROWS, P], F32R) for s in range(2)]
        cst = sb("cst", [P, CONSTS])
        vec1 = sb("vec1", [P, LAYERS, P])
        vec2 = sb("vec2", [P, LAYERS, PACK2])
        skip_all = sb("skip_all", [P, LAYERS * 4])
        skip_w = sb("skip_w", [P, LAYERS, 2])
        cact = sb("cact", [P, DC, 32])
        mod_row = sb("mod_row", [P, TOK])
        mod = sb("mod", [P, MOD_CHUNKS, 2])
        gain = sb("gain", [P, 3, DC, 2])
        rstd = sb("rstd", [P, TOK])
        wa = sb("wa", [P, 2, TOK])
        wb = sb("wb", [P, 2, TOK])
        early_root = sb("early_root", [P, 8])
        nbias = sb("nbias", [P, 4, 2, LAT])
        scores = sb("scores", [P, 2, TOK])
        probs = sb("probs", [P, 3, TOK])
        probs_t = sb("probs_t", [P, 4, LAT])
        sink8 = sb("sink8", [P, 4])
        eps_col = sb("eps_col", [P, 1])
        gatev = sb("gatev", [P, 3, DC, 2])
        smax = sb("smax", [P, 2, 4])
        dt_t = sb("dt_t", [8, TOK])
        da_t = mod_row[0:8, :]
        dtv = sb("dtv", [8, 4])
        tok = sb("tok", [P, 4, 16])
        tokf = sb("tokf", [P, 4, 8])
        tokb = sb("tokb", [P, 4, 8])
        nct = sb("nct", [P, 4, 8])
        tct = sb("tct", [P, 2, 8])
        tot = sb("tot", [P, 8])
        wdt_raw = sb("wdt_raw", [P, DC, 8])
        wdt_hi = sb("wdt_hi", [P, DC, 8], F32R)
        wdt_lo = sb("wdt_lo", [P, DC, 8], F32R)
        with ExitStack() as region:
            inner_hi = sb("inner_hi", [P, 8, TOK], F32R, region)
            inner_lo = sb("inner_lo", [P, 8, TOK], F32R, region)
        with ExitStack() as region:
            Q = sb("Q", [P, 8, TOK], F32, region)
            with ExitStack() as mixer:
                K = sb("K", [P, 14, TOK], F32, mixer)
                v_tok = sb("v_tok", [P, 4, 4 * P], F32, mixer)
                x_tok = sb("x_tok", [P, 4, 2 * P], F32, mixer)
                k_swap = sb("k_swap", [P, 2, TOK], F32, mixer)
            with ExitStack() as merge:
                y_hi = sb("y_hi", [P, 8, TOK], F32R, merge)
                y_lo = sb("y_lo", [P, 8, TOK], F32R, merge)
        with ExitStack() as region:
            x_in = sb("x_in", [P, 4, D], F32, region)
            pack1 = sb("pack1", [P, LAYERS, P], F32, region)
            cond_in = sb("cond_in", [2 * DC, P], F32, region)
            pack2 = sb("pack2", [PACK2, LAYERS, P], F32, region)
            out_rows = sb("out_rows", [P, 2, D], F32, region)
        bias_rows = nc.dram_tensor("bias_rows", (LAYERS, 4, 2 * ROWS - 1, GRID_W, P), F32, kind="Internal").ap()
        mod_rows = nc.dram_tensor("mod_rows", (LAYERS, 2, 4, MOD_CHUNKS * P), F32, kind="Internal").ap()
        bank = [ctx.enter_context(nc.psum_tensor(f"bank{b}", [P, TOK], F32)) for b in range(8)]

        def const(name):
            lo, hi = CONST_COLS[name]
            return cst[:, lo:hi]

        def chunk(c):
            return Q[:, QCHUNKS.index(c)] if c in QCHUNKS else K[:, KCHUNKS.index(c)]

        loaded = [ctx.enter_context(nc.semaphore(f"loaded{s}")) for s in range(SLOTS)]
        unit_done = ctx.enter_context(nc.semaphore("unit_done"))
        hi_made = ctx.enter_context(nc.semaphore("hi_made"))
        lo_made = ctx.enter_context(nc.semaphore("lo_made"))
        hi_used = ctx.enter_context(nc.semaphore("hi_used"))
        silu_done = ctx.enter_context(nc.semaphore("silu_done"))
        inner_made = ctx.enter_context(nc.semaphore("inner_made"))
        inner_hi_made = ctx.enter_context(nc.semaphore("inner_hi_made"))
        inner_lo_made = ctx.enter_context(nc.semaphore("inner_lo_made"))
        added = ctx.enter_context(nc.semaphore("added"))
        gate_done = ctx.enter_context(nc.semaphore("gate_done"))
        gated = ctx.enter_context(nc.semaphore("gated"))
        branch_added = ctx.enter_context(nc.semaphore("branch_added"))
        mod_copied = ctx.enter_context(nc.semaphore("mod_copied"))
        mod_stored = ctx.enter_context(nc.semaphore("mod_stored"))
        mod_loads = signal("mod_loads", 16)
        mod_turned = signal("mod_turned")
        start_loads = signal("start_loads", 16)
        const_loads = signal("const_loads", 16)
        cond_loads = signal("cond_loads", 16)
        pack_loads = signal("pack_loads", 16)
        layer_loads = signal("layer_loads", 16)
        bias_loads = signal("bias_loads", 16)
        rows_written = signal("rows_written", 16)
        out_stored = signal("out_stored", 16)
        pe_start = signal("pe_start")
        start_copied = signal("start_copied")
        cond_ready = signal("cond_ready")
        vectors = signal("vectors")
        squares = signal("squares")
        summed = signal("summed")
        sums = signal("sums")
        roots = signal("roots")
        normed = signal("normed")
        h_hi_made = signal("h_hi_made")
        h_made = signal("h_made")
        act_chain = signal("act_chain")
        dve_chain = signal("dve_chain")
        pool_chain = signal("pool_chain")
        projected = signal("projected")
        prep_done = signal("prep_done")
        prep_read = signal("prep_read")
        prepared = signal("prepared")
        act_read = signal("act_read")
        act_prepared = signal("act_prepared")
        conv_out = signal("conv_out")
        scored = signal("scored")
        bounded = signal("bounded")
        exped = signal("exped")
        normalised = signal("normalised")
        turned = signal("turned")
        turned_copied = signal("turned_copied")
        mixed = signal("mixed")
        y_stored = signal("y_stored")
        cb_done = signal("cb_done")
        cum_spread = signal("cum_spread")
        spread = signal("spread")
        decay_arg = signal("decay_arg")
        decayed = signal("decayed")
        weighed = signal("weighed")
        ssm_done = signal("ssm_done")
        ssm_read = signal("ssm_read")
        y_hi_made = signal("y_hi_made")
        y_made = signal("y_made")
        cleared = signal("cleared")
        soft = signal("soft")
        convolved = signal("convolved")
        pads_cleared = signal("pads_cleared")
        sunk = signal("sunk")
        skipped = signal("skipped")
        ssm_out = signal("ssm_out")
        bias_ready = signal("bias_ready")

        scores_flat = scores[:, :, :].rearrange("p a b -> p (a b)")
        probs_flat = probs[:, :, :].rearrange("p a b -> p (a b)")
        turned_probs = (probs_t, scores_flat.rearrange("p (k q) -> p k q", k=4))
        decay_f = (chunk(BV), chunk(BV + 1))
        decay_b = (chunk(AV), chunk(CV))
        weighed_by = (mod_row[:, :], rstd[:, :])
        padded = [f[:, 0:2 * (LAT + CONV - 1)].rearrange("p (s t) -> p s t", s=2) for f in (scores_flat, probs_flat)]

        def attention_tasks(last_layer):
            return [(br, h, st, qt) for br in range(3) for h in range(4) for st in range(1 if last_layer else 2) for qt in range(2)]

        SOURCES = (2, 3, 0, 1)

        def first_part(last_layer, t):
            per = 1 if last_layer else 2
            return t // per if t % per == 0 else None

        def second_part(last_layer, t):
            per = 1 if last_layer else 2
            return t // per if t % per == per - 1 else None

        def spread_head(slot):
            return slot // 5 if slot is not None and slot % 5 == 0 and slot < 20 else None

        def source_step(slot):
            if slot is None or slot < 0 or slot >= 20 or slot % 5 == 0:
                return None
            h, i = slot // 5, slot % 5 - 1
            return 4 * h + i, h, SOURCES[i]

        def behind(slot, lag):
            return None if slot is None else slot - lag

        def value_column(br, h):
            return (h // 2 * HD, P + h * HD, 3 * P + h // 2 * HD)[br]

        def dve_link(dve, ins):
            dve_chain.done(ins, dve_chain.count)
            dve.wait_ge(dve_chain.sem, dve_chain.count)

        def act_link(act, ins):
            act_chain.done(ins, act_chain.count)
            act.wait_ge(act_chain.sem, act_chain.count)

        block = ctx.enter_context(nc.Block())

        def tokens(l, name):
            return LAT if l == LAYERS - 1 and name in ("q", "merge", "ffn2") else TOK

        def in_tokens(l, c):
            return tokens(l, "q") if c in QCHUNKS or c >= SC_ else TOK

        def streams(n):
            return range(n // LAT)

        inner_first = {}
        n_inner = 0
        for l in range(LAYERS):
            for ffn in (1, 2):
                for part, (_, n) in enumerate(PARTS):
                    inner_first[l, ffn, part] = n_inner
                    n_inner += n
        add_first = {}
        n_add = 0
        for l in range(LAYERS):
            for step in [(1, 0), (1, 1), (1, 2), "out", (2, 0), (2, 1), (2, 2)]:
                add_first[l, step] = n_add
                n_add += DC

        COND_AT = 256 + 2 * PACK2

        def start_chunks(i):
            return range(2 * i, 2 * i + 2)

        TURN_AT = 5

        def next_norm(l, name):
            if name == (1, 2):
                return (l, "mix"), TOK
            if name == "out":
                return (l, 2), tokens(l, "ffn2")
            if name == (2, 2):
                return ((l + 1, 1), TOK) if l + 1 < LAYERS else (("final", 0), LAT)
            return None, 0

        n_roots = {next_norm(l, name)[0]: 3 * l + i for l in range(LAYERS) for i, name in enumerate([(1, 2), "out", (2, 2)])}

        def next_modulation(l, name, d):
            if (l, name, d) == (0, (1, 0), 0):
                return [(0, "gate")]
            if name == (1, 2) and d == TURN_AT:
                return [(l, "rest")]
            return [(l + 1, "in")] if name == (2, 2) and d == TURN_AT and l + 1 < LAYERS else []

        @block.sync
        def _(sp):
            def columns(w, l, col, rows=None, row0=0):
                v = w[l].rearrange("(c p) n -> p c n", p=P)
                if rows is not None:
                    v = v[:, row0:row0 + rows, :]
                return v[:, :, bass.ds(col, P)]

            def load(u, i, per, *sources):
                unit = units[u]
                if u >= SLOTS or not isinstance(i, int):
                    old = units[u - SLOTS + per[0]]
                    if old.kind == "mod":
                        sp.wait_ge(unit_done, u - SLOTS + 1 + i * per[0])
                    else:
                        sp.wait_ge(lo_made, old.product - per[1] + 1 + i * per[1])
                for rows, src in sources:
                    sp.dma_start(raw[unit.slot][:, rows[0]:rows[1], :], src).then_inc(loaded[unit.slot], 16)

            def stage(u0, n, source):
                for j in range(SLOTS):
                    load(u0 + j, 0, (0, 0), *source(j))
                turns = (n - SLOTS) // SLOTS
                if turns > 0:
                    with sp.Fori(1, turns + 1) as i:
                        for j in range(SLOTS):
                            load(u0 + j, i, (SLOTS, SLOTS), *source(i * SLOTS + j))
                for j in range(SLOTS * (turns + 1), n):
                    load(u0 + j, 0, (0, 0), *source(j))

            cond_loads.done(sp.dma_start(cond_in[0:DC, :], c.rearrange("a (r c) -> (a r) c", c=P)))
            cond_loads.done(sp.dma_start(cond_in[DC:2 * DC, :], c_ctx.rearrange("(r c) -> r c", c=P)), "all")

            for l in range(LAYERS):
                if l == 0:
                    stage(first["mod"], MOD_FIRST, lambda j: [((0, DC), columns(w_mod, 0, j * P))])
                for ffn in (1, 2):
                    wg, wu, wd = ffn_weights[ffn]
                    if ffn == 2:
                        for pos, col in enumerate(IN_ORDER):
                            load(first["in", l] + pos, 0, (0, 0), ((0, DC), columns(w_in, l, col * P)))

                        u0 = first["merge", l]

                        def merge_unit(k, d, i):
                            load(u0 + k, i, (SLOTS, SLOTS) if not isinstance(i, int) else (0, 0),
                                 ((0, DC), columns(w_in, l, GATE_COL + k * D + d * P)),
                                 ((DC, DC + 2), w_branch[l, k].rearrange("(c p) n -> p c n", p=P)[:, :, bass.ds(d * P, P)]))
                        for k in range(4):
                            merge_unit(k, 0, 0)
                        with sp.Fori(1, DC) as d:
                            for k in range(4):
                                merge_unit(k, d, d)
                        stage(first["out", l], DC, lambda j: [((0, DC), columns(w_out, l, j * P))])
                    for part, (c0, n) in enumerate(PARTS):
                        u0 = first["up", l, ffn, part]

                        extra = MOD_AT.get((l, ffn, part))
                        ahead = extra[2] if extra else 0
                        step = 1 + ahead

                        def turn_loads(i, per):
                            for j in range(4):
                                for q in range(ahead):
                                    load(u0 + step * j + q, i, per, ((0, DC), columns(
                                        w_mod, extra[0], i * (4 * ahead * P) + (extra[1] + ahead * j + q) * P)))
                                load(u0 + step * j + step - 1, i, per,
                                     ((0, DC), columns((wg, wu)[j % 2], l, i * (2 * P) + (c0 + j // 2) * P)))
                        turn_loads(0, (0, 0))
                        with sp.Fori(1, n // 2) as i:
                            turn_loads(i, (4 * step, 4))
                        stage(first["down", l, ffn, part], DC, lambda j: [((0, n), columns(wd, l, j * P, n, c0))])
            for t in range(2):
                start_copied.wait(sp, ("out", t))
                out_stored.done(sp.dma_start(out[0, t * P:(t + 1) * P, :], out_rows[:, t, :]), t)
            out_stored.wait(sp, 1)

        def split_hi(act, n, i=0, per=(0, 0)):
            if n >= len(product_units):
                return
            unit = units[product_units[n]]
            act.wait_ge(loaded[unit.slot], unit.loaded + i * (16 * unit.dmas * per[0] // SLOTS))
            if n >= 2:
                act.wait_ge(hi_used, n - 1 + i * per[1])
                act.wait_ge(lo_made, n - 1 + i * per[1])
            act.activation(w_hi[n % 2][:, 0:unit.rows, :], raw[unit.slot][:, 0:unit.rows, :], ACT.Copy).then_inc(hi_made, 1)

        def split_lo(dve, n, i=0, per=(0, 0)):
            if n >= len(product_units):
                return
            unit = units[product_units[n]]
            dve.wait_ge(hi_made, n + 1 + i * per[1])
            if n >= 2:
                dve.wait_ge(unit_done, product_units[n - 2] + 1 + i * per[0])
            dve.tensor_tensor(w_lo[n % 2][:, 0:unit.rows, :], raw[unit.slot][:, 0:unit.rows, :],
                              w_hi[n % 2][:, 0:unit.rows, :].bitcast(F32), ALU.subtract).then_inc(lo_made, 1)

        def turns(eng, n_turns, body):
            body(0)
            if n_turns > 2:
                with eng.Fori(1, n_turns - 1) as i:
                    body(i)
            if n_turns > 1:
                body(n_turns - 1)

        def at(u0, j, i, step=1):
            j = step * j + step - 1
            return (u0 + 4 * step * i + j, 0, (0, 0)) if isinstance(i, int) else (u0 + j, i, (4 * step, 4))

        def step_of(l, ffn, part):
            return 1 + MOD_AT[l, ffn, part][2] if (l, ffn, part) in MOD_AT else 1

        mod_first = {"start": 0}
        n_mod = MOD_FIRST // 4
        for key in sorted(MOD_AT):
            mod_first[key] = n_mod
            n_mod += PARTS[key[2]][1] // 2 * MOD_AT[key][2]
        mod_first["end"] = n_mod
        portion_fours = {(0, "in"): MOD_FIRST // 4, (0, "gate"): mod_first[0, 1, 1], (0, "rest"): mod_first[0, 2, 0],
                         (1, "in"): mod_first[1, 1, 0], (1, "rest"): mod_first["end"]}

        @block.tensor
        def _(pe):
            def product(u, i, per, *terms):
                unit = units[u]
                s = unit.product % 2
                pe.wait_ge(hi_made, unit.product + 1 + i * per[1])
                for psum, row0, rows, rhs, before in terms:
                    for k in range(rows):
                        if before:
                            before(k)
                        hi, lo = rhs(k)
                        pe.matmul(psum, w_hi[s][:, row0 + k, :], hi, start=(k == 0), stop=False)
                        mm = pe.matmul(psum, w_hi[s][:, row0 + k, :], lo, start=False, stop=False)
                mm.then_inc(hi_used, 1)
                pe.wait_ge(lo_made, unit.product + 1 + i * per[1])
                for psum, row0, rows, rhs, _ in terms:
                    for k in range(rows):
                        mm = pe.matmul(psum, w_lo[s][:, row0 + k, :], rhs(k)[0], start=False, stop=(k == rows - 1))
                mm.then_inc(unit_done, 1)

            def first_pair(a, b, n, key, between=None):
                for u, i, per in (a, b):
                    pe.wait_ge(lo_made, units[u].product + 1 + i * per[1])
                for step in range(DC + 2):
                    for which, ((u, _, _), k) in enumerate(((a, step), (b, step - 2))):
                        if not 0 <= k < DC:
                            continue
                        if which == 0:
                            h_made.wait(pe, (*key, k))
                        s = units[u].product % 2
                        psum, hi, lo = bank[which][:, 0:n], h_hi[:, k, 0:n], h_lo[:, k, 0:n]
                        pe.matmul(psum, w_hi[s][:, k, :], hi, start=(k == 0), stop=False)
                        mm = pe.matmul(psum, w_hi[s][:, k, :], lo, start=False, stop=False)
                        if k == DC - 1:
                            mm.then_inc(hi_used, 1)
                        mm = pe.matmul(psum, w_lo[s][:, k, :], hi, start=False, stop=(k == DC - 1))
                        if k == DC - 1:
                            mm.then_inc(unit_done, 1)
                            if which == 0 and between:
                                between()

            def h_rhs(n):
                return lambda k: (h_hi[:, k, 0:n], h_lo[:, k, 0:n])

            def sum_squares(key, n):
                summed.wait(pe, (key, DC - 2))
                pe.matmul(bank[6][:, 0:n], const("ones"), wb[:, 1, 0:n], start=True, stop=False)
                squares.wait(pe, (key, DC - 1))
                mm = pe.matmul(bank[6][:, 0:n], const("ones"), wa[:, (DC - 1) % 2, 0:n], start=False, stop=True)
                sums.done(mm, key)

            def modulation(u, i, per, j, m):
                unit = units[u]
                pe.wait_ge(loaded[unit.slot], unit.loaded + i * (16 * per[0] // SLOTS))
                if j == 0 and m is not None:
                    pe.wait_ge(mod_copied, m)
                for k in range(DC):
                    rows = slice(32 * (k % 4), 32 * (k % 4) + 32)
                    mm = pe.matmul(bank[7][rows, j * P:(j + 1) * P], cact[:, k, :], raw[unit.slot][:, k, :],
                                   start=(k < 4), stop=(k >= 4))
                mm.then_inc(unit_done, 1)

            def turn_modulation(l, portion):
                mod_loads.wait(pe, (l, portion))
                r0, r1, _, _ = PORTIONS[l, portion]
                n = r1 - r0
                pe.wait_ge(mod_copied, portion_fours[l, portion])
                for s in range(2):
                    for j in range(4):
                        mm = pe.matmul(bank[7][:, s * MOD_CHUNKS + r0:s * MOD_CHUNKS + r1], scores_flat[0:n, (4 * s + j) * P:(4 * s + j + 1) * P],
                                       const("ident")[0:n, 0:n], start=(j == 0), stop=(j == 3))
                mod_turned.done(mm, (l, portion))

            def up(l, ffn, part, n):
                u0, c0 = first["up", l, ffn, part], inner_first[l, ffn, part]
                step = step_of(l, ffn, part)

                if (ffn, part) == (1, 0):
                    vectors.wait(pe, (l, "in"))
                if (l, ffn, part) == (0, 1, 1):
                    vectors.wait(pe, (0, "gate"))

                def body(i):
                    start = 0
                    if part == 0 and isinstance(i, int) and i == 0:
                        m0 = mod_first.get((l, ffn, part))
                        if step == 2:
                            modulation(u0, 0, (0, 0), 0, m0)
                        for j in range(2):
                            pe.wait_ge(silu_done if j == 0 else inner_made, c0)
                        first_pair(at(u0, 0, 0, step), at(u0, 1, 0, step), n, (l, ffn),
                                   (lambda: modulation(u0 + 2, 0, (0, 0), 1, m0)) if step == 2 else None)
                        start = 2
                    for j in range(start, 4):
                        u, ii, per = at(u0, j, i, step)
                        for q in range(step - 1):
                            index = (step - 1) * j + q
                            modulation(u - (step - 1) + q, ii, per, index % 4, i * (step - 1) + (mod_first[l, ffn, part] + index // 4))
                        if not (isinstance(i, int) and i == 0):
                            read = silu_done if j % 2 == 0 else inner_made
                            pe.wait_ge(read, i * 2 + (c0 + j // 2 - 1))
                        product(*at(u0, j, i, step), (bank[j][:, 0:n], 0, DC, h_rhs(n), None))
                turns(pe, PARTS[part][1] // 2, body)

            def between(l, name, d):
                key, n = next_norm(l, name)
                for args in next_modulation(l, name, d):
                    turn_modulation(*args)
                if key and d == DC - 1:
                    sum_squares(key, n)

            def down(l, ffn, part, n):
                u0, a0 = first["down", l, ffn, part], add_first[l, (ffn, part)]
                rows = PARTS[part][1]
                last = inner_first[l, ffn, part] + rows
                for d in range(DC):
                    if a0 + d >= 2:
                        pe.wait_ge(added, a0 + d - 1)
                    product(u0 + d, 0, (0, 0), (bank[4 + d % 2][:, 0:n], 0, rows, lambda k: (inner_hi[:, k, 0:n], inner_lo[:, k, 0:n]),
                                                (lambda k: pe.wait_ge(inner_lo_made, last - rows + k + 1)) if d == 0 else None))
                    between(l, (ffn, part), d)

            def prepare(l, step, i):
                if step == "qk":
                    n = in_tokens(l, NORMED[i])
                    if i > 0:
                        act_read.wait(pe, (l, "qk", i - 1))
                    squares.wait(pe, (l, "qk", i))
                    mm = pe.matmul(bank[5][:, 0:n], const("blockones"), wa[:, i % 2, 0:n], start=True, stop=True)
                elif step == "rope":
                    c = ROTATED[i]
                    if i >= 2:
                        prep_read.wait(pe, (l, "rope", i - 2))
                    if c in NORMED:
                        prepared.wait(pe, (l, "qk", NORMED.index(c)))
                    else:
                        projected.wait(pe, (l, c))
                    mm = pe.matmul(bank[6 + i % 2][:, 0:LAT], const("rot"), chunk(c)[:, 0:LAT], start=True, stop=True)
                elif step == "swap":
                    c = SWAPPED[i]
                    prepared.wait(pe, (l, "rope", ROTATED.index(c)))
                    if c == CK:
                        act_read.wait(pe, (l, "qk", 2))
                    else:
                        prep_read.wait(pe, (l, "v", 3))
                    mm = pe.matmul(bank[5][:, :], const("swap"), chunk(c), start=True, stop=True)
                elif step == "v":
                    if i == 0:
                        act_prepared.wait(pe, (l, "swap", 1))
                    else:
                        prep_read.wait(pe, (l, "v", i - 1))
                    projected.wait(pe, (l, VCHUNKS[i]))
                    for t in range(4):
                        mm = pe.transpose(bank[5][:, t * P:(t + 1) * P], chunk(VCHUNKS[i])[:, t * P:(t + 1) * P], const("ident"))
                elif step == "dt":
                    prepared.wait(pe, (l, "wdt"))
                    for k in range(DC):
                        pe.matmul(bank[4][0:8, :], wdt_hi[:, k, :], h_hi[:, k, :], start=(k == 0), stop=False)
                        pe.matmul(bank[4][0:8, :], wdt_hi[:, k, :], h_lo[:, k, :], start=False, stop=False)
                        mm = pe.matmul(bank[4][0:8, :], wdt_lo[:, k, :], h_hi[:, k, :], start=False, stop=(k == DC - 1))
                elif step == "x":
                    conv_out.wait(pe, (l, i))
                    prep_read.wait(pe, (l, "rope", 4 + i))
                    for t in range(4):
                        mm = pe.transpose(bank[6 + i][:, t * P:(t + 1) * P], chunk(XS + i)[:, t * P:(t + 1) * P], const("ident"))
                elif step == "tok":
                    prepared.wait(pe, (l, "dt", 0))
                    for t in range(4):
                        pe.transpose(bank[4][:, t * 16:t * 16 + 8], dt_t[:, t * P:(t + 1) * P], const("ident")[0:8, 0:8])
                        mm = pe.transpose(bank[4][:, t * 16 + 8:t * 16 + 16], da_t[:, t * P:(t + 1) * P], const("ident")[0:8, 0:8])
                elif step == "cum":
                    prepared.wait(pe, (l, "tok", 0))
                    act_prepared.wait(pe, (l, "swap", 0))
                    for st in range(2):
                        n_mm = 0
                        for j in range(2):
                            for src, tri in ((tokf, "trif"), (tokb, "trib")):
                                strip = const(tri)[:, P - j * P:P - j * P + LAT]
                                mm = pe.matmul(bank[5][0:8, st * LAT:(st + 1) * LAT], src[:, 2 * st + j, :], strip,
                                               start=(n_mm == 0), stop=(n_mm == 3))
                                n_mm += 1
                elif step == "tot":
                    prepared.wait(pe, (l, "x", 0))
                    for j in range(2):
                        mm = pe.matmul(bank[6][:, 0:8], const("ones"), tok[:, 2 + j, 8:16], start=(j == 0), stop=(j == 1))
                elif step == "cumtok":
                    prepared.wait(pe, (l, "cum", 0))
                    for t in range(4):
                        mm = pe.transpose(bank[4][:, t * 8:t * 8 + 8], dt_t[:, t * P:(t + 1) * P], const("ident")[0:8, 0:8])
                else:
                    return
                prep_done.done(mm, (l, step, i))

            cond_loads.wait(pe, "all")
            const_loads.wait(pe, "first")
            pe_start.done(pe.transpose(bank[0][:, COND_AT:COND_AT + 2 * DC], cond_in[:, :], const("ident")[0:2 * DC, 0:2 * DC]), "cond")

            def turn_packs():
                start_loads.wait(pe, "all")
                for l in range(LAYERS):
                    pe.transpose(bank[0][:, l * P:(l + 1) * P], pack1[:, l, :], const("ident"))
                for l in range(LAYERS):
                    mm = pe.transpose(bank[0][:, 256 + l * PACK2:256 + (l + 1) * PACK2], pack2[:, l, :], const("ident")[0:PACK2, 0:PACK2])
                pe_start.done(mm, "packs")

            for l in range(LAYERS):
                last_layer = l == LAYERS - 1
                if l == 0:
                    cond_ready.wait(pe, "c")
                    cleared.wait(pe, "all")
                    for i in range(MOD_FIRST // 4):
                        for j in range(4):
                            modulation(*at(first["mod"], j, i), j, i or None)
                        if i == 1:
                            turn_packs()
                        for k in start_chunks(i):
                            if k == 0:
                                pack_loads.wait(pe, "all")
                            if k >= 3:
                                start_copied.wait(pe, ("x", k - 3))
                            for t in range(4):
                                mm = pe.transpose(bank[1 + k % 3][:, t * P:(t + 1) * P], x_in[:, t, k * P:(k + 1) * P], const("ident"))
                            pe_start.done(mm, ("x", k))
                    sum_squares((0, 1), TOK)
                    turn_modulation(0, "in")

                for part in range(len(PARTS)):
                    up(l, 1, part, TOK)
                    down(l, 1, part, TOK)

                u0 = first["in", l]
                for pos, c in enumerate(IN_ORDER):
                    if pos >= 4:
                        projected.wait(pe, (l, IN_ORDER[pos - 4]))
                    if pos == 0:
                        const_loads.wait(pe, "all")
                        pe.wait_ge(inner_made, inner_first[l, 1, 2] + PARTS[2][1])
                        first_pair((u0, 0, (0, 0)), (u0 + 1, 0, (0, 0)), TOK, (l, "mix"))
                    if pos >= 2:
                        product(u0 + pos, 0, (0, 0), (bank[pos % 4][:, 0:in_tokens(l, c)], 0, DC, h_rhs(in_tokens(l, c)), None))
                    for step, i in PREP.get(pos, ()):
                        prepare(l, step, i)

                tasks = attention_tasks(last_layer)
                n_tasks = len(tasks)

                n = tokens(l, "q")

                def mix(job):
                    br, h, st, _ = tasks[2 * job]
                    if job >= 1:
                        y_stored.wait(pe, (l, job - 1))
                    turned_copied.wait(pe, (l, 2 * job + 1))
                    row = HD * (h % 2)
                    v0 = value_column(br, h)
                    tiles = range(4) if st == 0 else range(2, 4)
                    for t in tiles:
                        mm = pe.matmul(bank[4][row:row + HD, 0:LAT], v_tok[:, t, v0:v0 + HD], turned_probs[job % 2][:, t, :],
                                       start=(t == tiles[0]), stop=(t == tiles[-1]))
                    mixed.done(mm, (l, job))

                def spread_sums(h, r):
                    if h > 0 or r > 0:
                        spread.wait(pe, (l, h - 1 + r, 1 - r))
                    mm = pe.matmul(bank[6][:, :], const("sel")[0:8, (4 * r + h) * P:(4 * r + h + 1) * P], dt_t[:, :],
                                   start=True, stop=True)
                    cum_spread.done(mm, (l, h, r))

                for t in range(n_tasks + 7):
                    head = spread_head(first_part(last_layer, t))
                    if t == 0:
                        projected.wait(pe, (l, IN_ORDER[-1]))
                        act_prepared.wait(pe, (l, "swap", 0))
                        prepared.wait(pe, (l, "cumtok", 0))
                    if head is not None:
                        spread_sums(head, 0)
                    if t < n_tasks:
                        br, h, st, qt = tasks[t]
                        if t >= 2:
                            exped.wait(pe, (l, t - 2))
                        row = HD * (h % 2)
                        q = chunk((AQ, BQ, CQ)[br] + h // 2)[row:row + HD, st * LAT + qt * P:st * LAT + (qt + 1) * P]
                        if br == 1:
                            k = chunk(BK + h // 2)
                        elif h // 2 == h % 2:
                            k = chunk((AK, None, CK)[br])
                        else:
                            k = k_swap[:, br // 2]
                        keys = slice(0, TOK) if st == 0 else slice(LAT, TOK)
                        mm = pe.matmul(bank[t % 2][:, 0:TOK - keys.start], q, k[row:row + HD, keys], start=True, stop=True)
                        scored.done(mm, (l, t))
                    if 3 <= t < n_tasks + 3:
                        s = t - 3
                        if s >= 2:
                            turned_copied.wait(pe, (l, s - 2))
                        normalised.wait(pe, (l, s))
                        for kt in range(4 if tasks[s][2] == 0 else 2):
                            mm = pe.transpose(bank[2 + s % 2][:, kt * P:(kt + 1) * P], probs[:, s % 3, kt * P:(kt + 1) * P], const("ident"))
                        turned.done(mm, (l, s))
                    if t % 2 == 0 and 0 <= (t - 6) // 2 < n_tasks // 2:
                        mix((t - 6) // 2)
                    slot = second_part(last_layer, t)
                    head = spread_head(slot)
                    if head is not None:
                        spread_sums(head, 1)
                    found = source_step(behind(slot, 1))
                    if found:
                        step, h, s = found
                        nn = n if s >= 2 else LAT
                        if step > 0:
                            weighed.wait(pe, (l, step - 1))
                        g = h // 2
                        mm = pe.matmul(bank[5][:, 0:nn], chunk(SB_ + g)[:, s * P:(s + 1) * P], chunk(SC_ + g)[:, 0:nn], start=True, stop=True)
                        cb_done.done(mm, (l, step))
                    found = source_step(behind(slot, 2))
                    if found:
                        step, h, s = found
                        nn = n if s >= 2 else LAT
                        if step == 8:
                            ssm_read.wait(pe, (l, "y", 0))
                        weighed.wait(pe, (l, step))
                        row = HD * (h % 2)
                        mm = pe.matmul(bank[7][row:row + HD, 0:nn], x_tok[:, s, h * HD:(h + 1) * HD], weighed_by[step % 2][:, 0:nn],
                                       start=(step % 4 == 0), stop=(step % 4 == 3))
                        ssm_done.done(mm, (l, step))
                for g in range(2):
                    squares.wait(pe, (l, "ssm", g))
                    mm = pe.matmul(bank[6][:, 0:n], const("ones"), wa[:, g, 0:n], start=(g == 0), stop=(g == 1))
                prep_done.done(mm, (l, "ssm"))

                u0 = first["merge", l]
                g0 = l * 4 * DC
                turned_copied.wait(pe, (l, n_tasks - 1))

                def merge_turn(d):
                    straight = isinstance(d, int)
                    for k in range(4):
                        if not (straight and d == 0):
                            pe.wait_ge(gated, d * 4 + (g0 + k - 3))
                        u, ii, per = at(u0, k, d)

                        def before(c):
                            if straight and d == 0:
                                y_made.wait(pe, (l, 2 * k + c))
                                if c == 0 and k == 0:
                                    y_stored.wait(pe, (l, n_tasks // 2 - 1))
                                if c == 0 and k == 2:
                                    roots.wait(pe, (l, "ssm"))
                        product(u, ii, per, (bank[k][:, 0:n], 0, DC, h_rhs(n), None),
                                (bank[4 + k][:, 0:n], DC, 2, lambda c: (y_hi[:, 2 * k + c, 0:n], y_lo[:, 2 * k + c, 0:n]), before))
                turns(pe, DC, merge_turn)

                u0, a0 = first["out", l], add_first[l, "out"]
                for d in range(DC):
                    pe.wait_ge(added, a0 + d - 1)
                    if d == 0:
                        pe.wait_ge(gated, g0 + 4 * DC)
                    product(u0 + d, 0, (0, 0), (bank[4 + d % 2][:, 0:n], 0, DC, h_rhs(n),
                                                (lambda k: h_made.wait(pe, (l, "merged", k))) if d == 0 else None))
                    between(l, "out", d)

                n = tokens(l, "ffn2")
                for part in range(len(PARTS)):
                    up(l, 2, part, n)
                    down(l, 2, part, n)

            for t in range(2):
                for half in range(2):
                    for k in range(4 * half, 4 * half + 4):
                        if t == 0:
                            normed.wait(pe, ("final", k))
                        mm = pe.transpose(bank[2 * t + half][:, (k % 4) * P:(k % 4 + 1) * P], X[:, k, t * P:(t + 1) * P], const("ident"))
                    pe_start.done(mm, ("out", t, half))

        @block.scalar
        def _(act):
            def square(key, n, k):
                if k >= 2:
                    summed.wait(act, (key, max(k - 2, 1)))
                squares.done(act.activation(wa[:, k % 2, 0:n], X[:, k, 0:n], ACT.Square), (key, k))

            def root(key, psum_signal, step, psum, dst, scale):
                psum_signal.wait(act, step)
                roots.done(act.activation(dst, psum, ACT.Sqrt, bias=eps_col[0:psum.shape[0], 0:1], scale=scale), key)

            def norm_block(l, which, n, mod_i):
                root((l, which), sums, (l, which), bank[6][:, 0:n], rstd[:, 0:n], 1.0 / D)
                vectors.wait(act, (l, "in" if mod_i == 0 else "rest"))
                for k in range(DC):
                    normed.wait(act, (l, which, k))
                    for st in streams(n):
                        cols = slice(st * LAT, (st + 1) * LAT)
                        ins = act.activation(h_hi[:, k, cols], wa[:, k % 2, cols], ACT.Identity,
                                             bias=mod[:, 3 * mod_i * DC + k, st:st + 1])
                    h_hi_made.done(ins, (l, which, k))

            def up(l, ffn, part, n):
                u0, c0 = first["up", l, ffn, part], inner_first[l, ffn, part]
                n0 = units[u0].product

                step = step_of(l, ffn, part)

                def body(i):
                    straight = isinstance(i, int)
                    for j in range(4):
                        _, ii, per = at(u0, j, i, step)
                        c = c0 + j // 2
                        if step > 1 and (step - 1) * (j + 1) % 4 == 0:
                            copy_modulation(u0 + step * (j + 1) - 1 + i * (4 * step),
                                            i * (step - 1) + (mod_first[l, ffn, part] + (step - 1) * (j + 1) // 4 - 1))
                        split_hi(act, n0 + j + 2 + (4 * i if straight else 0), ii, per)
                        if j % 2 == 0:
                            act.wait_ge(unit_done, u0 + step * (j + 1) + i * (4 * step))
                            if not (straight and c + 2 * i < 2):
                                act.wait_ge(inner_made, i * 2 + (c - 1))
                            act.activation(wa[:, (j // 2) % 2, 0:n], bank[j][:, 0:n], ACT.Silu).then_inc(silu_done, 1)
                        if j % 2 == 1:
                            act.wait_ge(inner_made, i * 2 + (c + 1))
                            act.activation(inner_hi[:, bass.ds(i * 2 + j // 2, 1), 0:n], wb[:, (j // 2) % 2:(j // 2) % 2 + 1, 0:n],
                                           ACT.Copy).then_inc(inner_hi_made, 1)
                turns(act, PARTS[part][1] // 2, body)

            def copy_modulation(done, m):
                act.wait_ge(unit_done, done)
                if not (isinstance(m, int) and m == 0):
                    act.wait_ge(mod_stored, m * 32)
                act.activation(mod_row[:, :], bank[7][:, :], ACT.Copy).then_inc(mod_copied, 1)

            def block_splits(l, name, u0):
                key, n = next_norm(l, name)
                for d in range(DC):
                    if key and d == 0:
                        act.activation(early_root[:, n_roots[key]:n_roots[key] + 1], eps_col[:, 0:1], ACT.Sqrt)
                    split_hi(act, units[u0].product + d + 2)
                    if key:
                        act.wait_ge(added, add_first[l, name] + d + 1)
                        square(key, n, d)

            def prepare(l, step, i):
                if step == "square":
                    c = NORMED[i]
                    n = in_tokens(l, c)
                    projected.wait(act, (l, c))
                    if i >= 2:
                        prep_done.wait(act, (l, "qk", i - 2))
                    squares.done(act.activation(wa[:, i % 2, 0:n], chunk(c)[:, 0:n], ACT.Square), (l, "qk", i))
                elif step == "qk":
                    n = in_tokens(l, NORMED[i])
                    prep_done.wait(act, (l, "qk", i))
                    if i >= 1:
                        prepared.wait(act, (l, "qk", i - 1))
                    act_read.done(act.activation(rstd[:, 0:n], bank[5][:, 0:n], ACT.Sqrt, bias=eps_col[:, 0:1], scale=1.0 / HD), (l, "qk", i))
                elif step == "swap":
                    prep_done.wait(act, (l, "swap", i))
                    act_prepared.done(act.activation(k_swap[:, i, :], bank[5][:, :], ACT.Copy), (l, "swap", i))
                elif step == "conv" and i > 0 or step == "convend":
                    j = i if step == "convend" else i - 1
                    m = in_tokens(l, XS + j)
                    convolved.wait(act, (l, j))
                    conv_out.done(act.activation(chunk(XS + j)[:, 0:m], wb[:, j % 2, 0:m], ACT.Silu,
                                                 bias=vec2[:, l, V_CONVB + j:V_CONVB + j + 1]), (l, j))
                elif step == "dt":
                    prep_done.wait(act, (l, "dt", 0))
                    prep_done.wait(act, (l, "qk", 2))
                    act_link(act, act.activation(wa[0:8, 0, :], bank[4][0:8, :], ACT.Identity, bias=dtv[:, 0:1]))
                    act_link(act, act.activation(dt_t[:, :], wa[0:8, 0, :], ACT.Abs))
                    act_link(act, act.activation(dt_t[:, :], dt_t[:, :], ACT.Exp, scale=-1.0))
                    act_link(act, act.activation(dtv[:, 2:3], dtv[:, 1:2], ACT.Exp))
                    soft.done(act.activation(da_t[:, :], dt_t[:, :], ACT.Ln, bias=const("ones")[0:8, 0:1]), (l, "dt"))

            const_loads.done(act.dma_start(cst[:, 0:FIRST_CONSTS], consts[:, 0:FIRST_CONSTS]), "first")
            pack_loads.done(act.dma_start(x_in[:, 0:2, :], x[0].rearrange("(t p) d -> p t d", p=P)))
            pack_loads.done(act.dma_start(x_in[:, 2:4, :], ctx_tokens[0].rearrange("(t p) d -> p t d", p=P)), "all")
            cleared.wait(act, "all")
            pe_start.wait(act, "cond")
            for st in range(2):
                cond_ready.done(act.activation(cact[:, :, st], bank[0][:, COND_AT + st * DC:COND_AT + (st + 1) * DC], ACT.Silu), "c")

            start_loads.done(act.dma_start(pack1[0:MOD_CHUNKS, :, :], b_mod.rearrange("l (r c) -> r l c", c=P)))
            for n, w in enumerate((norm_ffn1, norm_mix, norm_ffn2)):
                r = V_NORM + n * DC
                start_loads.done(act.dma_start(pack1[r:r + DC, :, :], w.rearrange("l (r c) -> r l c", c=P)))
            start_loads.done(act.dma_start(pack1[V_BGATE:V_BGATE + 4 * DC, :, :], b_gate.rearrange("l (r c) -> r l c", c=P)))
            for l in range(LAYERS):
                start_loads.done(act.dma_start(pack2[V_CONVW:V_CONVW + 6 * CONV, l, :], ssm_conv_w[l].rearrange("j (r c) -> (j r) c", c=P)))
            start_loads.done(act.dma_start(pack2[V_CONVB:V_CONVB + 6, :, :], ssm_conv_b.rearrange("l (r c) -> r l c", c=P)))
            start_loads.done(act.dma_start(pack2[V_SNORM:V_SNORM + 2, :, :], ssm_norm.rearrange("l (r c) -> r l c", c=P)))
            for v, w in ((V_QG, qk_norm_q), (V_KG, qk_norm_k)):
                for half in range(2):
                    start_loads.done(act.dma_start(pack2[v:v + 1, :, half * HD:(half + 1) * HD],
                                                  w.rearrange("(a l) c -> a l c", a=1)))
            start_loads.done(act.dma_start(skip_all[:, :], ssm_d.rearrange("(a l) h -> a (l h)", a=1).to_broadcast([P, LAYERS * 4])))
            for l in range(LAYERS):
                start_loads.done(act.dma_start(pack2[V_FIN:V_FIN + DC, l, :], final_norm.rearrange("(r c) -> r c", c=P)))
            start_loads.mark("all")

            for l in range(LAYERS):
                last_layer = l == LAYERS - 1
                if l == 0:
                    for i in range(MOD_FIRST // 4):
                        copy_modulation(first["mod"] + 4 + i * 4, i)
                        if i == 1:
                            pe_start.wait(act, "packs")
                            start_copied.done(act.activation(vec1[:, :, :], bank[0][:, 0:2 * P].rearrange("p (l r) -> p l r", l=LAYERS), ACT.Copy))
                            start_copied.done(act.activation(vec2[:, :, :], bank[0][:, 256:COND_AT].rearrange("p (l r) -> p l r", l=LAYERS),
                                                             ACT.Copy), "packs")
                        for k in start_chunks(i):
                            pe_start.wait(act, ("x", k))
                            start_copied.done(act.activation(X[:, k, :], bank[1 + k % 3][:, :], ACT.Copy), ("x", k))
                            start_copied.wait(act, ("x", k))
                            square((0, 1), TOK, k)
                    const_loads.done(act.dma_start(cst[:, FIRST_CONSTS:CONSTS], consts[:, FIRST_CONSTS:CONSTS]), "all")
                    for s in range(2):
                        split_hi(act, s)
                norm_block(l, 1, TOK, 0)
                for part in range(len(PARTS)):
                    up(l, 1, part, TOK)
                    block_splits(l, (1, part), first["down", l, 1, part])

                norm_block(l, "mix", TOK, 1)
                layer_loads.wait(act, l)
                act_prepared.done(act.activation(wdt_hi[:, :, :], wdt_raw[:, :, :], ACT.Copy), (l, "wdt_hi"))
                u0 = first["in", l]
                for pos, c in enumerate(IN_ORDER):
                    n = in_tokens(l, c)
                    split_hi(act, units[u0 + pos].product + 2)
                    act.wait_ge(unit_done, u0 + pos + 1)
                    src = bank[pos % 4][:, 0:n]
                    if XS <= c < XS + 6:
                        i = c - XS
                        if i >= 2:
                            convolved.wait(act, (l, i - 2))
                        else:
                            pads_cleared.wait(act, l)
                        ins = act.activation(padded[i % 2][:, 0:n // LAT, 2:2 + LAT], src.rearrange("p (s t) -> p s t", t=LAT), ACT.Copy)
                    else:
                        ins = act.activation(chunk(c)[:, 0:n], src, ACT.Silu if c in (Z, Z + 1) else ACT.Copy)
                    projected.done(ins, (l, c))
                    for step, i in PREP.get(pos, ()):
                        prepare(l, step, i)
                n = tokens(l, "q")

                tasks = attention_tasks(last_layer)
                n_tasks = len(tasks)

                def store_y(job):
                    br, h, st, _ = tasks[2 * job]
                    row = HD * (h % 2)
                    mixed.wait(act, (l, job))
                    y_stored.done(act.activation(chunk((AQ, BQ, CQ)[br] + h // 2)[row:row + HD, st * LAT:(st + 1) * LAT],
                                                 bank[4][row:row + HD, 0:LAT], ACT.Copy), (l, job))

                def copy_spread(h, r):
                    cum_spread.wait(act, (l, h, r))
                    if h > 0:
                        decay_arg.wait(act, (l, 4 * h - 1, r))
                    spread.done(act.activation(wa[:, r, :], bank[6][:, :], ACT.Copy), (l, h, r))

                for t in range(n_tasks + 7):
                    slot = first_part(last_layer, t)
                    head = spread_head(slot)
                    if head is not None:
                        copy_spread(head, 0)
                    found = source_step(slot)
                    if found:
                        step, h, s = found
                        if step >= 2:
                            weighed.wait(act, (l, step - 2))
                        if s >= 2:
                            spread.wait(act, (l, h, 1))
                            for r, dst in enumerate((decay_f, decay_b)):
                                decayed.done(act.activation(dst[step % 2][:, 0:LAT], wa[:, r, 0:LAT], ACT.Exp,
                                                            bias=tct[:, s % 2, 4 * r + h:4 * r + h + 1]), (l, step))
                    if 3 <= t < n_tasks + 3:
                        s = t - 3
                        _, _, st, qt = tasks[s]
                        turned.wait(act, (l, s))
                        if s // 2 >= 2:
                            mixed.wait(act, (l, s // 2 - 2))
                        k0 = 0 if st == 0 else 2
                        turned_copied.done(act.activation(turned_probs[s // 2 % 2][:, k0:4, qt * P:(qt + 1) * P],
                                                          bank[2 + s % 2][:, 0:(4 - k0) * P].rearrange("p (k q) -> p k q", q=P), ACT.Copy), (l, s))
                    if t < n_tasks:
                        br, h, st, qt = tasks[t]
                        s = t % 2
                        nk = TOK if st == 0 else CTX
                        bounded.wait(act, (l, t))
                        if t >= 3:
                            turned.wait(act, (l, t - 3))
                        ins = act.activation(probs[:, t % 3, 0:nk], bank[s][:, 0:nk], ACT.Exp, bias=smax[:, s, 1:2], scale=SCALE, accum_out=smax[:, s, 2:3])
                        if br == 0:
                            sunk.done(act.activation(smax[:, s, 3:4], sink8[:, h:h + 1], ACT.Exp, bias=smax[:, s, 1:2], scale=SCALE), (l, t))
                        exped.done(ins, (l, t))
                    if t % 2 == 1 and 0 <= (t - 7) // 2 < n_tasks // 2:
                        store_y((t - 7) // 2)
                    slot = second_part(last_layer, t)
                    head = spread_head(slot)
                    if head is not None:
                        copy_spread(head, 1)
                    found = source_step(slot)
                    if found:
                        step, h, s = found
                        st = s // 2
                        if not (last_layer and st == 1):
                            for r, dst in enumerate((decay_f, decay_b)):
                                decay_arg.wait(act, (l, step, r))
                                decayed.done(act.activation(dst[step % 2][:, st * LAT:(st + 1) * LAT],
                                                            wb[:, r, (step % 2) * LAT:(step % 2 + 1) * LAT], ACT.Exp), (l, step))
                        decayed.mark((l, step))

                for g in range(2):
                    skipped.wait(act, (l, g))
                    squares.done(act.activation(wa[:, g, 0:n], chunk(Z + g)[:, 0:n], ACT.Square), (l, "ssm", g))

                weighed.wait(act, (l, 15))
                y_stored.wait(act, (l, n_tasks // 2 - 1))
                for b, c in enumerate(QCHUNKS):
                    if b == 2:
                        root((l, "ssm"), prep_done, (l, "ssm"), bank[6][:, 0:n], rstd[:, 0:n], 1.0 / 256)
                    if c == Z:
                        ssm_out.wait(act, (l, 1))
                    y_hi_made.done(act.activation(y_hi[:, b, 0:n], chunk(c)[:, 0:n], ACT.Copy), (l, b))

                u0 = first["merge", l]
                n0, g0 = units[u0].product, l * 4 * DC

                def merge_turn(d):
                    straight = isinstance(d, int)
                    for k in range(4):
                        _, ii, per = at(u0, k, d)
                        split_hi(act, n0 + k + 2 + (4 * d if straight else 0), ii, per)
                        act.wait_ge(unit_done, u0 + k + 1 + d * 4)
                        if not (straight and d == 0 and k < 2):
                            act.wait_ge(gated, d * 4 + (g0 + k - 1))
                        act.activation(wa[:, k % 2, 0:n], bank[k][:, 0:n], ACT.Sigmoid,
                                       bias=vec1[:, l, bass.ds(d + (V_BGATE + k * DC), 1)]).then_inc(gate_done, 1)
                turns(act, DC, merge_turn)

                for k in range(DC):
                    act.wait_ge(branch_added, 3 * (l * DC + k + 1))
                    if k == 0:
                        act.wait_ge(unit_done, first["out", l])
                    h_hi_made.done(act.activation(h_hi[:, k, 0:n], Q[:, k, 0:n], ACT.Copy), (l, "merged", k))
                block_splits(l, "out", first["out", l])

                n = tokens(l, "ffn2")
                norm_block(l, 2, n, 2)
                for part in range(len(PARTS)):
                    up(l, 2, part, n)
                    block_splits(l, (2, part), first["down", l, 2, part])

            root("final", sums, ("final", 0), bank[6][:, 0:LAT], rstd[:, 0:LAT], 1.0 / D)
            for t in range(2):
                for half in range(2):
                    pe_start.wait(act, ("out", t, half))
                    ins = act.activation(out_rows[:, t, half * 512:(half + 1) * 512], bank[2 * t + half][:, :], ACT.Copy)
                    start_copied.done(ins, ("out", t))

        @block.vector
        def _(dve):
            def link(ins):
                dve_link(dve, ins)

            def split_h(key, n, source, k):
                h_hi_made.wait(dve, (*key, k))
                h_made.done(dve.tensor_tensor(h_lo[:, k, 0:n], source, h_hi[:, k, 0:n].bitcast(F32), ALU.subtract), (*key, k))

            def add_square(key, n, k):
                squares.wait(dve, (key, k))
                if k == 1:
                    summed.done(dve.tensor_tensor(wb[:, 1, 0:n], wa[:, 0, 0:n], wa[:, 1, 0:n], ALU.add), (key, k))
                elif k > 1:
                    summed.wait(dve, (key, k - 1))
                    summed.done(dve.tensor_tensor(wb[:, 1, 0:n], wb[:, 1, 0:n], wa[:, k % 2, 0:n], ALU.add), (key, k))

            def invert_root(key, n):
                roots.wait(dve, key)
                link(dve.reciprocal(rstd[:, 0:n], rstd[:, 0:n]))

            def norm_block(l, which, n, mod_i):
                key = (l, which)
                if key != (0, 1):
                    invert_root(key, n)
                for k in range(DC + 1):
                    if k < DC:
                        if k >= 2:
                            h_hi_made.wait(dve, (l, which, k - 2))
                            h_made.wait(dve, (l, which, k - 2))
                        for st in streams(n):
                            cols = slice(st * LAT, (st + 1) * LAT)
                            ins = dve.scalar_tensor_tensor(out=wa[:, k % 2, cols], in0=X[:, k, cols], scalar=gain[:, mod_i, k, st:st + 1],
                                                           in1=rstd[:, cols], op0=ALU.mult, op1=ALU.mult)
                        normed.done(ins, (l, which, k))
                    if k >= 1:
                        j = k - 1
                        normed.wait(dve, (l, which, j))
                        h_hi_made.wait(dve, (l, which, j))
                        for st in streams(n):
                            cols = slice(st * LAT, (st + 1) * LAT)
                            ins = dve.scalar_tensor_tensor(out=h_lo[:, j, cols], in0=wa[:, j % 2, cols],
                                                           scalar=mod[:, 3 * mod_i * DC + j, st:st + 1],
                                                           in1=h_hi[:, j, cols].bitcast(F32), op0=ALU.add, op1=ALU.subtract)
                        h_made.done(ins, (l, which, j))

            def up(l, ffn, part, n):
                u0, c0 = first["up", l, ffn, part], inner_first[l, ffn, part]
                n0 = units[u0].product

                step = step_of(l, ffn, part)

                def body(i):
                    straight = isinstance(i, int)
                    for j in range(4):
                        _, ii, per = at(u0, j, i, step)
                        c = c0 + j // 2
                        b = (j // 2) % 2
                        split_lo(dve, n0 + j + 2 + (4 * i if straight else 0), ii, per)
                        if j % 2 == 1:
                            dve.wait_ge(unit_done, u0 + step * (j + 1) + i * (4 * step))
                            dve.wait_ge(silu_done, i * 2 + (c + 1))
                            if not (straight and c + 2 * i < 2):
                                dve.wait_ge(inner_lo_made, i * 2 + (c - 1))
                            dve.tensor_tensor(wb[:, b, 0:n], bank[j][:, 0:n], wa[:, b, 0:n], ALU.mult).then_inc(inner_made, 1)
                        if j % 2 == 1:
                            dve.wait_ge(inner_hi_made, i * 2 + (c + 1))
                            at_chunk = bass.ds(i * 2 + j // 2, 1)
                            dve.tensor_tensor(inner_lo[:, at_chunk, 0:n], wb[:, b:b + 1, 0:n],
                                              inner_hi[:, at_chunk, 0:n].bitcast(F32), ALU.subtract).then_inc(inner_lo_made, 1)
                turns(dve, PARTS[part][1] // 2, body)

            def add_block(l, name, u0, n, gate_i):
                norm_key, norm_n = next_norm(l, name)
                for d in range(DC):
                    split_lo(dve, units[u0 + d].product + 2)
                    if norm_key and d > 0:
                        add_square(norm_key, norm_n, d - 1)
                    for args in next_modulation(l, name, d):
                        modulation_vectors(*args)
                    dve.wait_ge(unit_done, u0 + d + 1)
                    for st in streams(n):
                        cols = slice(st * LAT, (st + 1) * LAT)
                        ins = dve.scalar_tensor_tensor(out=X[:, d, cols], in0=bank[4 + d % 2][:, cols], scalar=gatev[:, gate_i, d, st:st + 1],
                                                       in1=X[:, d, cols], op0=ALU.mult, op1=ALU.add)
                    ins.then_inc(added, 1)

            def modulation_vectors(l, portion):
                mod_turned.wait(dve, (l, portion))
                start_copied.wait(dve, "packs")
                if (l, portion) == (1, "in"):
                    dve.wait_ge(added, add_first[l - 1, (1, 2)] + DC)
                r0, r1, norms, gates = PORTIONS[l, portion]
                for s in range(2):
                    link(dve.tensor_tensor(mod[:, r0:r1, s], bank[7][:, s * MOD_CHUNKS + r0:s * MOD_CHUNKS + r1],
                                           vec1[:, l, V_BMOD + r0:V_BMOD + r1], ALU.add))
                for i in norms:
                    for s in range(2):
                        vectors.done(dve.scalar_tensor_tensor(out=gain[:, i, :, s], in0=mod[:, (3 * i + 1) * DC:(3 * i + 2) * DC, s], scalar=1.0,
                                                              in1=vec1[:, l, V_NORM + i * DC:V_NORM + (i + 1) * DC], op0=ALU.add, op1=ALU.mult), (l, portion))
                for i in gates:
                    vectors.done(dve.tensor_scalar(gatev[:, i, :, :], mod[:, (3 * i + 2) * DC:(3 * i + 3) * DC, :],
                                                   1.0 if i == 1 else 0.5, None, ALU.mult), (l, portion))
                vectors.wait(dve, (l, portion))

            def prepare(l, step, i):
                if step in ("v", "rope", "x", "tok", "cum", "tot", "cumtok"):
                    prep_done.wait(dve, (l, step, i))
                if step == "conv":
                    nn = in_tokens(l, XS + i)
                    projected.wait(dve, (l, XS + i))
                    if i >= 2:
                        conv_out.wait(dve, (l, i - 2))
                    acc = wb[:, i % 2, 0:nn].rearrange("p (s t) -> p s t", t=LAT)
                    for j in range(CONV):
                        src = padded[i % 2][:, 0:nn // LAT, j:j + LAT]
                        w = vec2[:, l, V_CONVW + 6 * j + i:V_CONVW + 6 * j + i + 1]
                        if j == 0:
                            ins = dve.tensor_scalar(acc, src, w, None, ALU.mult)
                        else:
                            ins = dve.scalar_tensor_tensor(out=acc, in0=src, scalar=w, in1=acc, op0=ALU.mult, op1=ALU.add)
                        if j < CONV - 1:
                            link(ins)
                    convolved.done(ins, (l, i))
                elif step == "qk":
                    c = NORMED[i]
                    n = in_tokens(l, c)
                    act_read.wait(dve, (l, "qk", i))
                    link(dve.reciprocal(rstd[:, 0:n], rstd[:, 0:n]))
                    g = V_KG if c == CK else V_QG
                    prepared.done(dve.scalar_tensor_tensor(out=chunk(c)[:, 0:n], in0=chunk(c)[:, 0:n], scalar=vec2[:, l, g:g + 1],
                                                           in1=rstd[:, 0:n], op0=ALU.mult, op1=ALU.mult), (l, "qk", i))
                elif step == "rope":
                    if i == 0:
                        conv_out.wait(dve, (l, 5))
                    if i >= 2:
                        prepared.wait(dve, (l, "rope", i - 2))
                    lat = chunk(ROTATED[i])[:, 0:LAT]
                    work = wb[:, i % 2, 0:LAT]
                    prep_read.done(dve.tensor_tensor(work, bank[6 + i % 2][:, 0:LAT], const("ropes"), ALU.mult), (l, "rope", i))
                    link(dve.tensor_tensor(lat, lat, const("ropec"), ALU.mult))
                    prep_read.wait(dve, (l, "rope", i))
                    prepared.done(dve.tensor_tensor(lat, lat, work, ALU.add), (l, "rope", i))
                elif step == "v":
                    prep_read.done(dve.tensor_copy(v_tok[:, :, i * P:(i + 1) * P], bank[5][:, :].rearrange("p (t f) -> p t f", t=4)), (l, "v", i))
                elif step == "dt":
                    soft.wait(dve, (l, "dt"))
                    link(dve.scalar_tensor_tensor(out=dt_t[:, :], in0=wa[0:8, 0, :], scalar=0.0, in1=da_t[:, :], op0=ALU.max, op1=ALU.add))
                    prepared.done(dve.tensor_scalar(da_t[:, :], dt_t[:, :], dtv[:, 2:3], -1.0, ALU.mult, ALU.mult), (l, "dt", 0))
                elif step == "x":
                    prepared.done(dve.tensor_copy(x_tok[:, :, i * P:(i + 1) * P], bank[6 + i][:, :].rearrange("p (t f) -> p t f", t=4)), (l, "x", i))
                elif step == "tok":
                    link(dve.tensor_copy(tok[:, :, :], bank[4][:, 0:64].rearrange("p (t r) -> p t r", t=4)))
                    dve.tensor_copy(tokf[:, :, 0:4], tok[:, :, 8:12])
                    prepared.done(dve.tensor_copy(tokb[:, :, 4:8], tok[:, :, 12:16]), (l, "tok", 0))
                elif step == "cum":
                    prepared.done(dve.tensor_copy(dt_t[:, :], bank[5][0:8, :]), (l, "cum", 0))
                elif step == "tot":
                    link(dve.tensor_copy(tot[:, :], bank[6][:, 0:8]))
                elif step == "cumtok":
                    link(dve.tensor_scalar(nct[:, :, :], bank[4][:, 0:32].rearrange("p (t r) -> p t r", t=4), -1.0, None, ALU.mult))
                    for j in range(2):
                        ins = dve.tensor_tensor(tct[:, j, :], tot[:, :], nct[:, 2 + j, :], ALU.add)
                    prepared.done(ins, (l, "cumtok", 0))

            start_loads.wait(dve, "all")
            for l in range(LAYERS):
                for g in range(2):
                    for half in range(2):
                        rows = slice(half * HD, (half + 1) * HD)
                        head = 4 * l + 2 * g + half
                        ins = dve.tensor_copy(skip_w[rows, l, g:g + 1], skip_all[rows, head:head + 1])
            link(ins)
            for l in range(LAYERS):
                last_layer = l == LAYERS - 1
                nq = tokens(l, "q")
                if l == 0:
                    for k in range(DC - 1):
                        add_square((0, 1), TOK, k)
                    for s in range(2):
                        split_lo(dve, s)
                    invert_root((0, 1), TOK)
                    modulation_vectors(0, "in")

                norm_block(l, 1, TOK, 0)
                for part in range(len(PARTS)):
                    up(l, 1, part, TOK)
                    add_block(l, (1, part), first["down", l, 1, part], TOK, 0)

                norm_block(l, "mix", TOK, 1)
                act_prepared.wait(dve, (l, "wdt_hi"))
                prepared.done(dve.tensor_tensor(wdt_lo[:, :, :], wdt_raw[:, :, :], wdt_hi[:, :, :].bitcast(F32), ALU.subtract), (l, "wdt"))
                u0 = first["in", l]
                for i in range(2):
                    ins = dve.memset(padded[i][:, :, 0:2], 0.0)
                    ins = dve.memset(padded[i][:, :, 2 + LAT:4 + LAT], 0.0)
                pads_cleared.done(ins, l)
                for pos in range(IN_CHUNKS):
                    split_lo(dve, units[u0 + pos].product + 2)
                    for step, i in PREP.get(pos, ()):
                        prepare(l, step, i)
                layer_loads.wait(dve, l)
                link(dve.tensor_scalar(sink8[:, :], sink8[:, :], BIG, None, ALU.mult))
                bias_ready.wait(dve, l)

                tasks = attention_tasks(last_layer)
                n_tasks = len(tasks)
                for t in range(n_tasks + 7):
                    found = source_step(first_part(last_layer, t))
                    if found:
                        step, h, s = found
                        st, j = s // 2, s % 2
                        spread.wait(dve, (l, h, 1))
                        if step >= 2:
                            decayed.wait(dve, (l, step - 2))
                        for r, mask in enumerate(("maskf", "maskb")):
                            if not (last_layer and st == 1):
                                strip = const(mask)[:, P - j * P:P - j * P + LAT]
                                decay_arg.done(dve.scalar_tensor_tensor(
                                    out=wb[:, r, (step % 2) * LAT:(step % 2 + 1) * LAT], in0=wa[:, r, st * LAT:(st + 1) * LAT],
                                    scalar=nct[:, s, 4 * r + h:4 * r + h + 1], in1=strip, op0=ALU.add, op1=ALU.add), (l, step, r))
                    if t < n_tasks:
                        br, h, st, qt = tasks[t]
                        s = t % 2
                        scored.wait(dve, (l, t))
                        nk = TOK if st == 0 else CTX
                        if br < 2 and st == 0:
                            mask = const("wmask")[:, qt * LAT:(qt + 1) * LAT] if br == 0 else nbias[:, h, qt, :]
                            link(dve.tensor_tensor(bank[s][:, 0:LAT], bank[s][:, 0:LAT], mask, ALU.add))
                        link(dve.reduce_max(smax[:, s, 0:1], bank[s][:, 0:nk], AX_X))
                        if br == 0:
                            ins = dve.tensor_scalar(smax[:, s, 1:2], smax[:, s, 0:1], sink8[:, h:h + 1], -SCALE, ALU.max, ALU.mult)
                        else:
                            ins = dve.tensor_scalar(smax[:, s, 1:2], smax[:, s, 0:1], -SCALE, None, ALU.mult)
                        bounded.done(ins, (l, t))
                    if 1 <= t <= n_tasks:
                        br, h, st, qt = tasks[t - 1]
                        s = (t - 1) % 2
                        nk = TOK if st == 0 else CTX
                        exped.wait(dve, (l, t - 1))
                        if br == 0:
                            sunk.wait(dve, (l, t - 1))
                            link(dve.tensor_tensor(smax[:, s, 2:3], smax[:, s, 2:3], smax[:, s, 3:4], ALU.add))
                        link(dve.reciprocal(smax[:, s, 2:3], smax[:, s, 2:3]))
                        normalised.done(dve.tensor_scalar(probs[:, (t - 1) % 3, 0:nk], probs[:, (t - 1) % 3, 0:nk], smax[:, s, 2:3], None, ALU.mult), (l, t - 1))
                    slot = second_part(last_layer, t)
                    found = source_step(behind(slot, 1))
                    if found:
                        step, h, s = found
                        nn = nq if s >= 2 else LAT
                        decayed.wait(dve, (l, step))
                        if step >= 2:
                            ssm_done.wait(dve, (l, step - 2))
                        f, b = decay_f[step % 2][:, 0:nn], decay_b[step % 2][:, 0:nn]
                        link(dve.tensor_scalar(b, b, tok[:, s, 4 + h:5 + h], None, ALU.mult))
                        link(dve.scalar_tensor_tensor(out=f, in0=f, scalar=tok[:, s, h:h + 1], in1=b, op0=ALU.mult, op1=ALU.add))
                        cb_done.wait(dve, (l, step))
                        weighed.done(dve.tensor_tensor(weighed_by[step % 2][:, 0:nn], f, bank[5][:, 0:nn], ALU.mult), (l, step))
                    found = source_step(behind(slot, 3))
                    if found and found[0] % 8 == 7:
                        g = found[0] // 8
                        ssm_done.wait(dve, (l, found[0]))
                        x_g, z_g = chunk(XS + g)[:, 0:nq], chunk(Z + g)[:, 0:nq]
                        ssm_read.done(dve.scalar_tensor_tensor(out=x_g, in0=x_g, scalar=skip_w[:, l, g:g + 1], in1=bank[7][:, 0:nq],
                                                               op0=ALU.mult, op1=ALU.add), (l, "y", g))
                        ssm_read.wait(dve, (l, "y", g))
                        skipped.done(dve.tensor_tensor(z_g, x_g, z_g, ALU.mult), (l, g))
                for b, c in enumerate(QCHUNKS):
                    if b == 2:
                        roots.wait(dve, (l, "ssm"))
                        link(dve.reciprocal(rstd[:, 0:nq], rstd[:, 0:nq]))
                        for g in range(2):
                            z_g = chunk(Z + g)[:, 0:nq]
                            ssm_out.done(dve.scalar_tensor_tensor(out=z_g, in0=z_g, scalar=vec2[:, l, V_SNORM + g:V_SNORM + g + 1],
                                                                  in1=rstd[:, 0:nq], op0=ALU.mult, op1=ALU.mult), (l, g))
                    y_hi_made.wait(dve, (l, b))
                    y_made.done(dve.tensor_tensor(y_lo[:, b, 0:nq], chunk(c)[:, 0:nq], y_hi[:, b, 0:nq].bitcast(F32), ALU.subtract), (l, b))
                y_made.wait(dve, (l, 7))

                u0 = first["merge", l]
                n0, g0 = units[u0].product, l * 4 * DC

                def merge_turn(d):
                    straight = isinstance(d, int)
                    for k in range(4):
                        _, ii, per = at(u0, k, d)
                        split_lo(dve, n0 + k + 2 + (4 * d if straight else 0), ii, per)
                        dve.wait_ge(unit_done, u0 + k + 1 + d * 4)
                        dve.wait_ge(gate_done, d * 4 + (g0 + k + 1))
                        merged = Q[:, bass.ds(d, 1), 0:nq]
                        work = wb[:, k % 2:k % 2 + 1, 0:nq]
                        branch = bank[4 + k][:, 0:nq].unsqueeze(1)
                        gate = wa[:, k % 2:k % 2 + 1, 0:nq]
                        if k == 1 and not (straight and d == 0):
                            dve.wait_ge(branch_added, d * 3 + 3 * l * DC)
                        dve.tensor_tensor(merged if k == 0 else work, gate, branch, ALU.mult).then_inc(gated, 1)
                        if k > 0:
                            dve.wait_ge(gated, d * 4 + (g0 + k + 1))
                            if k > 1:
                                dve.wait_ge(branch_added, d * 3 + (3 * l * DC + k - 1))
                            dve.tensor_tensor(merged, merged, work, ALU.add).then_inc(branch_added, 1)
                turns(dve, DC, merge_turn)
                for k in range(DC):
                    split_h((l, "merged"), nq, Q[:, k, 0:nq], k)
                add_block(l, "out", first["out", l], nq, 1)

                n = tokens(l, "ffn2")
                norm_block(l, 2, n, 2)
                for part in range(len(PARTS)):
                    up(l, 2, part, n)
                    add_block(l, (2, part), first["down", l, 2, part], n, 2)

            roots.wait(dve, "final")
            link(dve.reciprocal(rstd[:, 0:LAT], rstd[:, 0:LAT]))
            for k in range(DC):
                normed.done(dve.scalar_tensor_tensor(out=X[:, k, 0:LAT], in0=X[:, k, 0:LAT], scalar=vec2[:, 0, V_FIN + k:V_FIN + k + 1],
                                                     in1=rstd[:, 0:LAT], op0=ALU.mult, op1=ALU.mult), ("final", k))

        @block.gpsimd
        def _(pool):
            pool.memset(eps_col[:, :], EPS)
            pool.memset(tokf[:, :, :], 0.0)
            pool.memset(tokb[:, :, :], 0.0)
            cleared.done(pool.memset(cact[:, :, :], 0.0), "all")

            def store_modulation(l, chunk0, m):
                pool.wait_ge(mod_copied, m + 1)
                for s in range(2):
                    pool.dma_start(mod_rows[l, s, :, bass.ds(chunk0 * P, 4 * P)], mod_row[s::32, :]).then_inc(mod_stored, 16)

            def load_modulation(l, portion):
                pool.wait_ge(mod_stored, 32 * portion_fours[l, portion])
                r0, r1, _, _ = PORTIONS[l, portion]
                if portion != "in":
                    mod_turned.wait(pool, (l, "gate" if (l, portion) == (0, "rest") else "in"))
                elif l > 0:
                    y_made.wait(pool, (l - 1, 7))
                mod_loads.done(pool.dma_start(scores_flat[0:r1 - r0, :].rearrange("r (q c) -> r q c", c=P),
                                              mod_rows[l].rearrange("s j (r c) -> r (s j) c", c=P)[r0:r1]), (l, portion))

            def small_loads(l):
                if l > 0:
                    y_made.wait(pool, (l - 1, 7))
                layer_loads.done(pool.dma_start(sink8[:, :], attn_sink[l:l + 1, :].to_broadcast([P, 4])))
                layer_loads.done(pool.dma_start(dtv[:, 0:1], ssm_dt_bias[l].rearrange("a (b o) -> (a b) o", o=1)))
                layer_loads.done(pool.dma_start(dtv[:, 1:2], ssm_a_log[l].rearrange("a (b o) -> (a b) o", o=1)))
                layer_loads.done(pool.dma_start(wdt_raw[:, :, :], w_in[l].rearrange("(c p) n -> p c n", p=P)[:, :, DT_COL:GATE_COL]), l)

            def neighbourhood_bias(l):
                const_loads.wait(pool, "all")
                if l == 0:
                    rows_written.wait(pool, "all")
                for h in range(4):
                    for qr in range(ROWS):
                        t, a = qr // 2, qr % 2
                        src = bass.AP(bias_rows.tensor, bias_rows[l, h, ROWS - 1 - qr, 0, NA_COLS - 1:NA_COLS].offset,
                                      [[P - 1, GRID_W], [GRID_W * P, ROWS], [1, GRID_W]])
                        bias_loads.done(pool.dma_start(
                            nbias[a * GRID_W:(a + 1) * GRID_W, h, t, :].rearrange("p (r c) -> p r c", r=ROWS), src), l)
                bias_loads.wait(pool, l)
                tiles = [(h, t) for h in range(4) for t in range(2)]
                for h, t in tiles:
                    pool_chain.done(pool.tensor_tensor(nbias[:, h, t, :], nbias[:, h, t, :], const("nvalid"), ALU.mult), (l, h, t))
                for h, t in tiles:
                    pool_chain.wait(pool, (l, h, t))
                    bias_ready.done(pool.tensor_tensor(nbias[:, h, t, :], nbias[:, h, t, :], const("nneg"), ALU.add), l)

            small_loads(0)
            with pool.Fori(0, MOD_FIRST // 4) as i:
                store_modulation(0, i * 4, i)
            load_modulation(0, "in")
            for l in range(LAYERS):
                for h in range(4):
                    row = na_rpb[l, h, NA_ROWS - ROWS, 0:1]
                    src = bass.AP(row.tensor, row.offset, [[2 * NA_COLS - 1, 2 * ROWS - 1], [0, GRID_W], [1, P]])
                    rows_written.done(pool.dma_start(bias_rows[l, h], src), "all")
            for key in sorted(MOD_AT):
                l, chunk0, ahead = MOD_AT[key]
                if key == (0, 1, 1):
                    load_modulation(0, "gate")
                if key == (0, 2, 0):
                    load_modulation(0, "rest")
                    neighbourhood_bias(0)
                if key == (1, 1, 0):
                    load_modulation(1, "in")
                    small_loads(1)
                m0 = mod_first[key]
                with pool.Fori(0, PARTS[key[2]][1] // 2 * ahead) as i:
                    store_modulation(l, i * 4 + chunk0, i + m0)
            load_modulation(1, "rest")
            neighbourhood_bias(1)


_INS = ['x', 'c', 'ctx', 'c_ctx', 'w_mod', 'b_mod', 'norm_ffn1', 'ffn1_w_gate', 'ffn1_w_up', 'ffn1_w_down',
        'norm_mix', 'w_in', 'b_gate', 'attn_sink', 'na_rpb', 'qk_norm_q', 'qk_norm_k', 'ssm_conv_w', 'ssm_conv_b',
        'ssm_dt_bias', 'ssm_a_log', 'ssm_d', 'ssm_norm', 'w_branch', 'w_out', 'norm_ffn2', 'ffn2_w_gate',
        'ffn2_w_up', 'ffn2_w_down', 'final_norm']
_OUTS = [((1, LAT, D), 'float32')]


def kernel(**inputs):
    import numpy as _np
    import concourse.bacc as _bacc
    from concourse import mybir as _mybir
    from concourse.bass_utils import run_bass_kernel_spmd as _run

    arrays = {f"in_{name}_dram": _np.ascontiguousarray(inputs[name]) for name in _INS}
    arrays["in_consts_dram"] = constants()
    values = {}
    for _ in range(2):
        nc = _bacc.Bacc("TRN2", target_bir_lowering=False, num_devices=1)
        args = [nc.dram_tensor(n, a.shape, _mybir.dt.from_np(a.dtype), kind="ExternalInput").ap() for n, a in arrays.items()]
        for i, (shape, dtype) in enumerate(_OUTS):
            args.append(nc.dram_tensor(f"out_{i}_dram", shape, _mybir.dt.from_np(_np.dtype(dtype)), kind="ExternalOutput").ap())
        build(nc, values, *args)
    r = _run(nc, [arrays], core_ids=[0])
    return r.results[0]["out_0_dram"]
```
